# Optimizing a Trainium2 kernel written in Bass

```python
import jax, jax.numpy as jnp
from jax import lax
import numpy as np
import math

D_MODEL = 1024
BATCH = 1
SEQ = 256
DEPTH = 1

HEAD_DIM = 64
N_Q_HEADS = 8
N_KV_HEADS = 2
Q_PER_KV = N_Q_HEADS // N_KV_HEADS
ATTN_WIDTH = N_Q_HEADS * HEAD_DIM
KV_WIDTH = N_KV_HEADS * HEAD_DIM
WINDOW = 128
ATTN_BLOCK = WINDOW
ROPE_THETA = 10000.0
CONV_WIDTH = D_MODEL - ATTN_WIDTH
CONV_K = 3
IN_PROJ_WIDTH = ATTN_WIDTH + 2 * KV_WIDTH + 3 * CONV_WIDTH
SPLITS = (ATTN_WIDTH, ATTN_WIDTH + KV_WIDTH, ATTN_WIDTH + 2 * KV_WIDTH,
          ATTN_WIDTH + 2 * KV_WIDTH + CONV_WIDTH, ATTN_WIDTH + 2 * KV_WIDTH + 2 * CONV_WIDTH)
PEER_HEADS = 8
PEER_KEYS = 128
PEER_EXPERTS = PEER_KEYS * PEER_KEYS
PEER_TOPK = 16
PEER_QDIM = 256
PEER_HALF = PEER_QDIM // 2
PEER_CHUNK = 128
N_MOD = 6
EPS = 1e-6
NEG = -1e30


def rmsnorm(x, g):
    x32 = x.astype(jnp.float32)
    y = x32 * lax.rsqrt(jnp.mean(x32 * x32, axis=-1, keepdims=True) + EPS)
    return (y * g.astype(jnp.float32)).astype(x.dtype)

def modulate(h, shift, scale):
    return h * (1.0 + scale[:, None, :]) + shift[:, None, :]

def rope(t, cos, sin):
    t1, t2 = jnp.split(t.astype(jnp.float32), 2, axis=-1)
    out = jnp.concatenate([t1 * cos - t2 * sin, t2 * cos + t1 * sin], axis=-1)
    return out.astype(t.dtype)

def sliding_window_attention(q, k, v, sinks):
    B, S = q.shape[0], q.shape[1]
    nb = S // ATTN_BLOCK
    qb = q.reshape(B, nb, ATTN_BLOCK, N_KV_HEADS, Q_PER_KV, HEAD_DIM)

    def band(t):
        tb = t.reshape(B, nb, ATTN_BLOCK, N_KV_HEADS, HEAD_DIM)
        prev = jnp.pad(tb, ((0, 0), (1, 0), (0, 0), (0, 0), (0, 0)))[:, :-1]
        return jnp.concatenate([prev, tb], axis=2)

    kb, vb = band(k), band(v)
    s = jnp.einsum('bnqhgd,bnkhd->bnhgqk', qb, kb).astype(jnp.float32) * (HEAD_DIM ** -0.5)
    qi = jnp.arange(ATTN_BLOCK)[:, None]
    kj = jnp.arange(2 * ATTN_BLOCK)[None, :]
    dist = qi + ATTN_BLOCK - kj
    blk = jnp.arange(nb)[:, None, None]
    valid = (dist >= 0) & (dist < WINDOW) & (blk * ATTN_BLOCK - ATTN_BLOCK + kj >= 0)
    s = jnp.where(valid[None, :, None, None], s, NEG)
    sink = sinks.astype(jnp.float32).reshape(1, 1, N_KV_HEADS, Q_PER_KV, 1, 1)
    m = jnp.maximum(jnp.max(s, axis=-1, keepdims=True), sink)
    e = jnp.exp(s - m)
    p = e / (jnp.sum(e, axis=-1, keepdims=True) + jnp.exp(sink - m))
    o = jnp.einsum('bnhgqk,bnkhd->bnqhgd', p.astype(v.dtype), vb)
    return o.reshape(B, S, ATTN_WIDTH)

def short_conv(h, w):
    S = h.shape[1]
    hp = jnp.pad(h, ((0, 0), (CONV_K - 1, 0), (0, 0)))
    y = w[0] * hp[:, 0:S]
    for k in range(1, CONV_K):
        y = y + w[k] * hp[:, k:k + S]
    return y

def peer(h, wq, subkeys, u_tab, v_tab):
    B, S, D = h.shape
    T = B * S
    xt = h.reshape(T, D)
    q = (xt @ wq).reshape(T, PEER_HEADS, 2, PEER_HALF)
    sc = jnp.einsum('thpd,hpkd->thpk', q, subkeys).astype(jnp.float32)
    vals, ids = lax.top_k(sc, PEER_TOPK)
    cand = (vals[:, :, 0, :, None] + vals[:, :, 1, None, :]).reshape(T, PEER_HEADS, PEER_TOPK * PEER_TOPK)
    cid = (ids[:, :, 0, :, None] * PEER_KEYS + ids[:, :, 1, None, :]).reshape(T, PEER_HEADS, PEER_TOPK * PEER_TOPK)
    top, pos = lax.top_k(cand, PEER_TOPK)
    idx = jnp.take_along_axis(cid, pos, axis=-1)
    g = jax.nn.softmax(top, axis=-1).astype(h.dtype)
    nc = T // PEER_CHUNK

    def expert_chunk(args):
        xc, ic, gc = args
        u = jnp.take(u_tab, ic, axis=0)
        a = jnp.einsum('chkd,cd->chk', u, xc)
        wgt = gc * jax.nn.gelu(a)
        vv = jnp.take(v_tab, ic, axis=0)
        return jnp.einsum('chk,chkd->cd', wgt, vv)

    out = lax.map(expert_chunk, (xt.reshape(nc, PEER_CHUNK, D),
                                 idx.reshape(nc, PEER_CHUNK, PEER_HEADS, PEER_TOPK),
                                 g.reshape(nc, PEER_CHUNK, PEER_HEADS, PEER_TOPK)))
    return out.reshape(B, S, D)

def first_inputs(seed: int = 0) -> dict:
    key = jax.random.key(seed)
    ks = jax.random.split(key, 20)
    f32 = jnp.float32
    D = D_MODEL

    def nrm(k, shape, scale):
        return jax.random.normal(k, shape, f32) * scale

    return {
        "x": nrm(ks[0], (BATCH, SEQ, D), 1.0),
        "c": nrm(ks[1], (BATCH, D), 1.0),
        "positions": jnp.broadcast_to(jnp.arange(SEQ, dtype=jnp.int32)[None, :], (BATCH, SEQ)),
        "ada_w": nrm(ks[2], (DEPTH, D, N_MOD * D), 0.5 * D ** -0.5),
        "ada_b": nrm(ks[3], (DEPTH, N_MOD * D), 0.02),
        "norm1_g": 1.0 + nrm(ks[4], (DEPTH, D), 0.02),
        "w_in": nrm(ks[5], (DEPTH, D, IN_PROJ_WIDTH), D ** -0.5),
        "q_norm_g": 1.0 + nrm(ks[6], (DEPTH, HEAD_DIM), 0.02),
        "k_norm_g": 1.0 + nrm(ks[7], (DEPTH, HEAD_DIM), 0.02),
        "sinks": nrm(ks[8], (DEPTH, N_Q_HEADS), 0.5),
        "conv_w": nrm(ks[9], (DEPTH, CONV_K, CONV_WIDTH), CONV_K ** -0.5),
        "attn_out_g": 1.0 + nrm(ks[10], (DEPTH, ATTN_WIDTH), 0.02),
        "conv_out_g": 1.0 + nrm(ks[11], (DEPTH, CONV_WIDTH), 0.02),
        "w_out": nrm(ks[12], (DEPTH, D, D), D ** -0.5),
        "norm2_g": 1.0 + nrm(ks[13], (DEPTH, D), 0.02),
        "peer_wq": nrm(ks[14], (DEPTH, D, PEER_HEADS * PEER_QDIM), D ** -0.5),
        "peer_subkeys": nrm(ks[15], (DEPTH, PEER_HEADS, 2, PEER_KEYS, PEER_HALF), PEER_HALF ** -0.5),
        "peer_u": nrm(ks[16], (DEPTH, PEER_EXPERTS, D), D ** -0.5),
        "peer_v": nrm(ks[17], (DEPTH, PEER_EXPERTS, D), (PEER_HEADS * PEER_TOPK) ** -0.5),
    }

def first_block(x, c, positions, ada_w, ada_b, norm1_g, w_in, q_norm_g, k_norm_g, sinks, conv_w,
              attn_out_g, conv_out_g, w_out, norm2_g, peer_wq, peer_subkeys, peer_u, peer_v):
    B, S, _ = x.shape
    inv_freq = ROPE_THETA ** (-jnp.arange(0, HEAD_DIM, 2, dtype=jnp.float32) / HEAD_DIM)
    ang = positions.astype(jnp.float32)[..., None] * inv_freq
    cos = jnp.cos(ang)[:, :, None, :]
    sin = jnp.sin(ang)[:, :, None, :]
    c_act = jax.nn.silu(c)

    for l in range(DEPTH):
        mod = c_act @ ada_w[l] + ada_b[l]
        shift1, scale1, gate1, shift2, scale2, gate2 = jnp.split(mod, N_MOD, axis=-1)

        h = modulate(rmsnorm(x, norm1_g[l]), shift1, scale1)
        proj = h @ w_in[l]
        q, k, v, cb, cc, cu = jnp.split(proj, SPLITS, axis=-1)

        q = rope(rmsnorm(q.reshape(B, S, N_Q_HEADS, HEAD_DIM), q_norm_g[l]), cos, sin)
        k = rope(rmsnorm(k.reshape(B, S, N_KV_HEADS, HEAD_DIM), k_norm_g[l]), cos, sin)
        v = v.reshape(B, S, N_KV_HEADS, HEAD_DIM)
        attn = sliding_window_attention(q, k, v, sinks[l])

        conv = cb * short_conv(cc * cu, conv_w[l])

        merged = jnp.concatenate([rmsnorm(attn, attn_out_g[l]), rmsnorm(conv, conv_out_g[l])], axis=-1)
        x = x + gate1[:, None, :] * (merged @ w_out[l])

        h2 = modulate(rmsnorm(x, norm2_g[l]), shift2, scale2)
        x = x + gate2[:, None, :] * peer(h2, peer_wq[l], peer_subkeys[l], peer_u[l], peer_v[l])
    return x


N_META = 16
S5_WIDTH = D_MODEL // 2
S5_GROUP = 16
S5_GROUPS = S5_WIDTH // S5_GROUP
S5_STATE = 64
DT_MIN = 1e-3
DT_MAX = 1e-1
M_HEADS = 4
M_DK = D_MODEL // 8
M_DV = D_MODEL // 4
M_QK_WIDTH = M_HEADS * M_DK
M_V_WIDTH = M_HEADS * M_DV
M_CHUNK = 64
CONV_WIDTH_2 = 4
D_FF = 4 * D_MODEL
ALPHA = (2.0 * DEPTH) ** 0.25
BETA = (8.0 * DEPTH) ** -0.25
LN_EPS = 1e-5
IN_SIZES = (S5_WIDTH, M_QK_WIDTH, M_QK_WIDTH, M_V_WIDTH, M_V_WIDTH, M_HEADS, M_HEADS, D_MODEL, D_MODEL)
IN_WIDTH = sum(IN_SIZES)
F_GATE_OFFSET = S5_WIDTH + 2 * M_QK_WIDTH + 2 * M_V_WIDTH + M_HEADS


def _layer_norm(x, g, b):
    xf = x.astype(jnp.float32)
    mu = jnp.mean(xf, axis=-1, keepdims=True)
    var = jnp.mean(jnp.square(xf - mu), axis=-1, keepdims=True)
    y = (xf - mu) * lax.rsqrt(var + LN_EPS)
    return (y * g.astype(jnp.float32) + b.astype(jnp.float32)).astype(x.dtype)

def _head_norm(h, g):
    hf = h.astype(jnp.float32)
    mu = jnp.mean(hf, axis=-1, keepdims=True)
    var = jnp.mean(jnp.square(hf - mu), axis=-1, keepdims=True)
    return (hf - mu) * lax.rsqrt(var + LN_EPS) * g.astype(jnp.float32).reshape(M_HEADS, M_DV)

def _split_columns(p):
    parts, start = [], 0
    for size in IN_SIZES:
        parts.append(p[..., start:start + size])
        start += size
    return parts

def _causal_depthwise_conv(x, w, b):
    c = x.shape[-1]
    y = lax.conv_general_dilated(
        x, w[:, None, :].astype(x.dtype), window_strides=(1,),
        padding=((CONV_WIDTH_2 - 1, 0),), dimension_numbers=("NWC", "WIO", "NWC"),
        feature_group_count=c)
    return y + b

def _linear_recurrence_combine(left, right):
    a_l, b_l = left
    a_r, b_r = right
    return a_l * a_r, a_r * b_l + b_r

def _s5_mixer(u, lam_re, lam_im, log_dt, b_re, b_im, c_re, c_im, d_skip):
    f32 = jnp.float32
    bsz, length, _ = u.shape
    uf = u.astype(f32).reshape(bsz, length, S5_GROUPS, S5_GROUP)
    lam = lax.complex(lam_re.astype(f32), lam_im.astype(f32))
    dt = jnp.exp(log_dt.astype(f32))[:, None]
    lam_bar = jnp.exp(lam * dt)
    b_mat = lax.complex(b_re.astype(f32), b_im.astype(f32))
    b_bar = ((lam_bar - 1.0) / lam)[..., None] * b_mat
    bu = jnp.einsum("gph,blgh->blgp", b_bar, uf.astype(jnp.complex64))
    a = jnp.broadcast_to(lam_bar, (1, length, S5_GROUPS, S5_STATE))
    _, state = lax.associative_scan(_linear_recurrence_combine, (a, bu), axis=1)
    c_mat = lax.complex(c_re.astype(f32), c_im.astype(f32))
    y = jnp.real(jnp.einsum("ghp,blgp->blgh", c_mat, state))
    y = y + d_skip.astype(f32).reshape(S5_GROUPS, S5_GROUP) * uf
    return y.reshape(bsz, length, S5_WIDTH)

def _mlstm_mixer(q, k, v, i_pre, f_pre):
    f32 = jnp.float32
    bsz, length = q.shape[:2]
    n_pad = M_CHUNK - N_META
    n_chunks = (length + n_pad) // M_CHUNK

    def to_chunks(t, fill):
        t = t.astype(f32)
        t = jnp.pad(t, ((0, 0), (n_pad, 0)) + ((0, 0),) * (t.ndim - 2), constant_values=fill)
        t = t.reshape((bsz, n_chunks, M_CHUNK) + t.shape[2:])
        return jnp.moveaxis(t, (1, 3), (0, 2))

    qc = to_chunks(q, 0.0)
    kc = to_chunks(k * (M_DK ** -0.5), 0.0)
    vc = to_chunks(v, 0.0)
    log_i = to_chunks(i_pre, -jnp.inf)
    log_f = to_chunks(jax.nn.log_sigmoid(f_pre.astype(f32)), 0.0)
    causal = jnp.tril(jnp.ones((M_CHUNK, M_CHUNK), dtype=bool))

    def chunk_step(carry, inp):
        c_st, n_st, m_st = carry
        q_c, k_c, v_c, li_c, lf_c = inp
        b = jnp.cumsum(lf_c, axis=-1)
        d_mat = jnp.where(causal, b[..., :, None] - b[..., None, :] + li_c[..., None, :], -jnp.inf)
        m_inter = b + m_st[..., None]
        m_row = jnp.maximum(m_inter, jnp.max(d_mat, axis=-1))
        w_intra = jnp.exp(d_mat - m_row[..., None])
        w_inter = jnp.exp(m_inter - m_row)
        s = jnp.einsum("bhsd,bhjd->bhsj", q_c, k_c) * w_intra
        num = (jnp.einsum("bhsj,bhje->bhse", s, v_c)
               + w_inter[..., None] * jnp.einsum("bhsd,bhde->bhse", q_c, c_st))
        den = jnp.sum(s, axis=-1) + w_inter * jnp.einsum("bhsd,bhd->bhs", q_c, n_st)
        h_c = num / jnp.maximum(jnp.abs(den), jnp.exp(-m_row))[..., None]
        b_last = b[..., -1]
        g_log = b_last[..., None] - b + li_c
        m_new = jnp.maximum(b_last + m_st, jnp.max(g_log, axis=-1))
        w_k = jnp.exp(g_log - m_new[..., None])
        decay = jnp.exp(b_last + m_st - m_new)
        c_new = decay[..., None, None] * c_st + jnp.einsum("bhj,bhjd,bhje->bhde", w_k, k_c, v_c)
        n_new = decay[..., None] * n_st + jnp.einsum("bhj,bhjd->bhd", w_k, k_c)
        return (c_new, n_new, m_new), h_c

    init = (jnp.zeros((bsz, M_HEADS, M_DK, M_DV), f32),
            jnp.zeros((bsz, M_HEADS, M_DK), f32),
            jnp.zeros((bsz, M_HEADS), f32))
    _, h = lax.scan(chunk_step, init, (qc, kc, vc, log_i, log_f))
    h = jnp.moveaxis(h, (0, 2), (1, 3)).reshape(bsz, n_chunks * M_CHUNK, M_HEADS, M_DV)
    return h[:, n_pad:]

def second_inputs(seed: int = 0) -> dict:
    key = jax.random.key(seed)
    ks = jax.random.split(key, 27)
    f32 = jnp.float32

    def nrm(k, shape, scale):
        return scale * jax.random.normal(k, shape, f32)

    b_in = nrm(ks[5], (DEPTH, IN_WIDTH), 0.02)
    b_in = b_in.at[:, F_GATE_OFFSET:F_GATE_OFFSET + M_HEADS].add(jnp.linspace(3.0, 6.0, M_HEADS))
    s5_lambda_re = -0.5 + nrm(ks[8], (DEPTH, S5_GROUPS, S5_STATE), 0.01)
    s5_lambda_im = jnp.pi * jnp.arange(S5_STATE, dtype=f32) + nrm(ks[9], (DEPTH, S5_GROUPS, S5_STATE), 0.01)
    s5_log_dt = jax.random.uniform(ks[10], (DEPTH, S5_GROUPS), f32, math.log(DT_MIN), math.log(DT_MAX))
    return {
        "x": nrm(ks[0], (BATCH, SEQ, D_MODEL), 1.0),
        "meta_tokens": nrm(ks[1], (N_META, D_MODEL), 1.0),
        "ln0_g": 1.0 + nrm(ks[2], (D_MODEL,), 0.05),
        "ln0_b": nrm(ks[3], (D_MODEL,), 0.02),
        "w_in": nrm(ks[4], (DEPTH, D_MODEL, IN_WIDTH), D_MODEL ** -0.5),
        "b_in": b_in,
        "qk_conv_w": nrm(ks[6], (DEPTH, CONV_WIDTH_2, 2 * M_QK_WIDTH), CONV_WIDTH_2 ** -0.5),
        "qk_conv_b": nrm(ks[7], (DEPTH, 2 * M_QK_WIDTH), 0.02),
        "s5_lambda_re": s5_lambda_re,
        "s5_lambda_im": s5_lambda_im,
        "s5_log_dt": s5_log_dt,
        "s5_b_re": nrm(ks[11], (DEPTH, S5_GROUPS, S5_STATE, S5_GROUP), (2.0 * S5_GROUP) ** -0.5),
        "s5_b_im": nrm(ks[12], (DEPTH, S5_GROUPS, S5_STATE, S5_GROUP), (2.0 * S5_GROUP) ** -0.5),
        "s5_c_re": nrm(ks[13], (DEPTH, S5_GROUPS, S5_GROUP, S5_STATE), S5_STATE ** -0.5),
        "s5_c_im": nrm(ks[14], (DEPTH, S5_GROUPS, S5_GROUP, S5_STATE), S5_STATE ** -0.5),
        "s5_d": nrm(ks[15], (DEPTH, S5_WIDTH), 1.0),
        "s5_w_glu": nrm(ks[16], (DEPTH, S5_WIDTH, 2 * D_MODEL), S5_WIDTH ** -0.5),
        "m_norm_g": 1.0 + nrm(ks[17], (DEPTH, M_V_WIDTH), 0.05),
        "m_w_out": nrm(ks[18], (DEPTH, M_V_WIDTH, D_MODEL), M_V_WIDTH ** -0.5),
        "w_o": nrm(ks[19], (DEPTH, D_MODEL, D_MODEL), BETA * D_MODEL ** -0.5),
        "ln1_g": 1.0 + nrm(ks[20], (DEPTH, D_MODEL), 0.05),
        "ln1_b": nrm(ks[21], (DEPTH, D_MODEL), 0.02),
        "w_up": nrm(ks[22], (DEPTH, D_MODEL, D_FF), D_MODEL ** -0.5),
        "b_up": nrm(ks[23], (DEPTH, D_FF), 0.02),
        "w_down": nrm(ks[24], (DEPTH, D_FF, D_MODEL), BETA * D_FF ** -0.5),
        "ln2_g": 1.0 + nrm(ks[25], (DEPTH, D_MODEL), 0.05),
        "ln2_b": nrm(ks[26], (DEPTH, D_MODEL), 0.02),
    }

def second_block(x, meta_tokens, ln0_g, ln0_b, w_in, b_in, qk_conv_w, qk_conv_b,
              s5_lambda_re, s5_lambda_im, s5_log_dt, s5_b_re, s5_b_im, s5_c_re, s5_c_im,
              s5_d, s5_w_glu, m_norm_g, m_w_out, w_o, ln1_g, ln1_b, w_up, b_up, w_down,
              ln2_g, ln2_b):
    bsz = x.shape[0]
    meta = jnp.broadcast_to(meta_tokens[None].astype(x.dtype), (bsz, N_META, D_MODEL))
    h = _layer_norm(jnp.concatenate([meta, x], axis=1), ln0_g, ln0_b)
    length = h.shape[1]
    for layer in range(DEPTH):
        p = h @ w_in[layer] + b_in[layer]
        u_s5, q, k, v, o_pre, i_pre, f_pre, g_s5, g_m = _split_columns(p)
        y_s5 = _s5_mixer(u_s5, s5_lambda_re[layer], s5_lambda_im[layer], s5_log_dt[layer],
                         s5_b_re[layer], s5_b_im[layer], s5_c_re[layer], s5_c_im[layer], s5_d[layer])
        z = jax.nn.gelu(y_s5).astype(h.dtype) @ s5_w_glu[layer]
        y_s5 = z[..., :D_MODEL] * jax.nn.sigmoid(z[..., D_MODEL:])
        qk = jax.nn.silu(_causal_depthwise_conv(jnp.concatenate([q, k], axis=-1),
                                                qk_conv_w[layer], qk_conv_b[layer]))
        q_h = qk[..., :M_QK_WIDTH].reshape(bsz, length, M_HEADS, M_DK)
        k_h = qk[..., M_QK_WIDTH:].reshape(bsz, length, M_HEADS, M_DK)
        v_h = v.reshape(bsz, length, M_HEADS, M_DV)
        hm = _mlstm_mixer(q_h, k_h, v_h, i_pre, f_pre)
        hm = _head_norm(hm, m_norm_g[layer]).reshape(bsz, length, M_V_WIDTH).astype(h.dtype)
        y_m = (jax.nn.sigmoid(o_pre) * hm) @ m_w_out[layer]
        mix = jax.nn.sigmoid(g_s5) * y_s5 + jax.nn.sigmoid(g_m) * y_m
        h = _layer_norm(ALPHA * h + mix @ w_o[layer], ln1_g[layer], ln1_b[layer])
        ff = jnp.square(jax.nn.relu(h @ w_up[layer] + b_up[layer])) @ w_down[layer]
        h = _layer_norm(ALPHA * h + ff, ln2_g[layer], ln2_b[layer])
    return h[:, N_META:]


def setup_inputs(seed=0):
    out = dict(first_inputs(seed))
    for name, value in second_inputs(seed + 1).items():
        if name != "x":
            out[name + "_2"] = value
    return out


def reference(
    x, c, positions, ada_w, ada_b, norm1_g, w_in, q_norm_g, k_norm_g, sinks, conv_w, attn_out_g,
    conv_out_g, w_out, norm2_g, peer_wq, peer_subkeys, peer_u, peer_v, meta_tokens_2, ln0_g_2,
    ln0_b_2, w_in_2, b_in_2, qk_conv_w_2, qk_conv_b_2, s5_lambda_re_2, s5_lambda_im_2,
    s5_log_dt_2, s5_b_re_2, s5_b_im_2, s5_c_re_2, s5_c_im_2, s5_d_2, s5_w_glu_2, m_norm_g_2,
    m_w_out_2, w_o_2, ln1_g_2, ln1_b_2, w_up_2, b_up_2, w_down_2, ln2_g_2, ln2_b_2,
):
    x = first_block(
        x, c, positions, ada_w, ada_b, norm1_g, w_in, q_norm_g, k_norm_g, sinks, conv_w,
        attn_out_g, conv_out_g, w_out, norm2_g, peer_wq, peer_subkeys, peer_u, peer_v,
    )
    return second_block(
        x, meta_tokens_2, ln0_g_2, ln0_b_2, w_in_2, b_in_2, qk_conv_w_2, qk_conv_b_2,
        s5_lambda_re_2, s5_lambda_im_2, s5_log_dt_2, s5_b_re_2, s5_b_im_2, s5_c_re_2, s5_c_im_2,
        s5_d_2, s5_w_glu_2, m_norm_g_2, m_w_out_2, w_o_2, ln1_g_2, ln1_b_2, w_up_2, b_up_2,
        w_down_2, ln2_g_2, ln2_b_2,
    )


_drawn_inputs = setup_inputs


def setup_inputs(seed=0):
    import zlib

    import numpy as np

    out = dict(_drawn_inputs(seed))
    spreads = {}
    factors = {'norm1_g': 6.857,
     'q_norm_g': 8.0,
     'k_norm_g': 8.0,
     'sinks': 64.0,
     'attn_out_g': 8.0,
     'conv_out_g': 8.0,
     'norm2_g': 8.0,
     'peer_wq': 3.906,
     'peer_subkeys': 3.933,
     'peer_u': 4.337,
     'peer_v': 3.873,
     'qk_conv_b_2': 8.0,
     's5_lambda_re_2': 64.0,
     's5_lambda_im_2': 58.248,
     's5_log_dt_2': 60.952,
     's5_b_re_2': 64.0,
     's5_b_im_2': 64.0,
     's5_c_re_2': 64.0,
     's5_c_im_2': 64.0,
     'm_norm_g_2': 7.803,
     'ln1_b_2': 2.681,
     'b_up_2': 4.607,
     'ln2_b_2': 2.759}
    for name, (base, spread) in spreads.items():
        noise = np.random.default_rng([zlib.crc32(name.encode()), seed]).standard_normal(out[name].shape)
        drawn = base * np.exp(spread * noise) if base else spread * noise
        out[name] = __import__('jax').numpy.asarray(drawn.astype(out[name].dtype))
    for name, factor in factors.items():
        out[name] = (out[name] * factor).astype(out[name].dtype)
    return out
```

```python
from contextlib import ExitStack
import math

import numpy as np

import concourse.bass as bass
from concourse import mybir

ALU = mybir.AluOpType
ACT = mybir.ActivationFunctionType
F32 = mybir.dt.float32
U32 = mybir.dt.uint32
I32 = mybir.dt.int32
X = mybir.AxisListType.X

P = 128
D = 1024
KD = D // P
SEQ = 256
TT = SEQ // P
META = 16
LEN = META + SEQ
HD = 64
NQ, NKV = 8, 2
QPK = NQ // NKV
AW = NQ * HD
QKW = (NQ + NKV) * HD
CW = D - AW
CT = CW // P
THETA = 10000.0
EPS = 1e-6
LN_EPS = 1e-5
NEG = -1e30
HEADS, KEYS, TOPK = 8, 128, 16
EXPERTS = KEYS * KEYS
HP = 2 * HEADS
S5W, S5G, S5H, S5P = 512, 32, 16, 64
SI = S5G * S5P // P
MH, DK, DV = 4, 128, 256
FF = 4 * D
ALPHA = 2.0 ** 0.25
LOWEST = -3.0e38

TWO_PI = 2.0 * math.pi
C1 = 6.28125
C2 = float(np.float32(np.round((TWO_PI - C1) * 2.0 ** 22) / 2.0 ** 22))
C3 = TWO_PI - C1 - C2
PI_IN = 3.1415925

RING = 3
CHUNK = 4096
GW = 12
NR = 8
ACC = 4

PACK = [("c", KD), ("conv_w", 3 * CT), ("conv_g", CT), ("b_uqk", 12), ("qk_w", 32), ("qk_b", 8),
        ("lam_re", SI), ("lam_im", SI), ("s5_d", 4), ("b_up", FF // P)]
PACK_AT, PACK_W = {}, 0
for _name, _w in PACK:
    PACK_AT[_name] = (PACK_W, PACK_W + _w)
    PACK_W += _w

U0, Q0, K0, V0, O0, IF0, GS0, GM0 = 0, 512, 1024, 1536, 2560, 3584, 3592, 4616


def plan():
    chunks, groups = [], []

    def add(name, w, c, n, k0=0, kt=KD, gs=()):
        chunks.append((name, w, k0, kt, c, n))
        groups.append(list(gs))

    def ada(lo, hi):
        for i in range(lo, hi):
            add("ada", "ada_w", 512 * i, 512, gs=[("ada", i)])

    ada(0, 4)
    add("in1", "w_in", 0, 512, gs=[("q1", t) for t in range(TT)])
    add("in1", "w_in", 512, 256, gs=[("kv1", t) for t in range(TT)])
    for j, nm in enumerate(("cb", "cc", "cu")):
        add("in1", "w_in", 768 + 512 * j, 512, gs=[(nm, m) for m in range(4)])
    ada(4, 12)
    for n in range(2):
        add("out1", "w_out", 512 * n, 512, gs=[("out1", TT * n + t) for t in range(TT)])
    for n in range(4):
        add("wq", "peer_wq", 512 * n, 512, gs=[("wq", 4 * n + m) for m in range(4)])
    for nm, c in (("u", U0), ("q2", Q0), ("k2", K0)):
        add("in2", "w_in_2", c, 512, gs=[(nm, m) for m in range(4)])
    for n in range(2):
        add("in2", "w_in_2", V0 + 512 * n, 512, gs=[("v2", 3 * n + t) for t in range(3)])
    for nm, c in (("o2", O0), ("gs", GS0), ("gm", GM0)):
        for n in range(2):
            add("in2", "w_in_2", c + 512 * n, 512, gs=[(nm, TT * n + t) for t in range(TT)])
    for n in range(2):
        add("glu", "s5_w_glu_2", D * n, D, kt=4, gs=[("glu", 4 * n + i) for i in range(4)])
    for n in range(2):
        add("mo", "m_w_out_2", 512 * n, 512, gs=[("mo", TT * n + t) for t in range(TT)])
    for n in range(2):
        add("wo", "w_o_2", 512 * n, 512, gs=[("wo", TT * n + t) for t in range(TT)])
    for n in range(8):
        add("up", "w_up_2", 512 * n, 512, gs=[("up", 4 * n + m) for m in range(4)])
    for n in range(8):
        add("down", "w_down_2", 0, D, k0=4 * n, kt=4, gs=[])
    return chunks, groups


CHUNKS, GROUPS = plan()
GROUP_NO = {}
for _gs in GROUPS:
    for _g in _gs:
        GROUP_NO[_g] = len(GROUP_NO)


def build(nc, T, out):
    with ExitStack() as ctx:
        def sb(name, shape, dt=F32):
            return ctx.enter_context(nc.sbuf_tensor(name, shape, dt))

        def sem(name):
            return ctx.enter_context(nc.semaphore(name))

        def over(ap, axis, n):
            ap = ap.unsqueeze(axis)
            shape = list(ap.shape)
            shape[axis] = n
            return ap.broadcast_to(shape)

        ring = sb("weight_ring", [P, RING, CHUNK])
        xres = sb("xres", [P, TT, D])
        featT = sb("featT", [P, KD, LEN])
        hbuf = sb("hbuf", [P, TT, D])
        modr = sb("modr", [P, 6 * D])
        wk = sb("work", [P, 8704])
        G = sb("gathered", [P, GW * D])
        vec = sb("vectors", [P, 4 * D])
        pack = sb("pack", [P, PACK_W])
        ident = sb("ident", [P, P])
        ones = sb("ones", [P, P])
        mask = sb("mask", [P, 2, P])
        causal = sb("causal", [P, P])
        iota_t = sb("iota_t", [P, LEN])
        iota16 = sb("iota16", [P, TOPK])
        rope_t = sb("rope_t", [P, 4, TT, HD // 2])
        inv_freq = sb("inv_freq", [P, HD // 2])
        uT = sb("uT", [P, 4, LEN])
        idx = sb("idx", [P, TT, HEADS * TOPK], U32)
        gates = sb("gates", [P, TT, HEADS * TOPK])
        stage = sb("stage", [P, 2, TOPK], U32)
        dots = sb("dots", [P, TOPK])
        gel = sb("gel", [P, TOPK])
        wgt = sb("wgt", [P, TOPK])
        st = sb("stats", [P, 96])
        pos_i = sb("pos_i", [P, TT], I32)
        w_if = sb("w_if", [P, KD, 2 * MH])
        b_if = sb("b_if", [MH, 2])
        s5_dt = sb("s5_log_dt", [P, SI])
        s5_mag = sb("s5_mag", [P, SI])
        s5_th = sb("s5_theta", [P, SI])
        col2 = sb("mlstm_cols", [P, 68])
        psum = ctx.enter_context(nc.psum_tensor("psum", [P, 8, 512], F32))

        def pk(name):
            a, b = PACK_AT[name]
            return pack[:, a:b]

        crep = G[:, 0:1024].rearrange("p (k m) -> p k m", k=KD)
        qkv = G[:, 1024:2560].rearrange("p (t n) -> p t n", t=TT)
        qkr = G[:, 2560:3840].rearrange("p (t n) -> p t n", t=TT)
        S = G[:, 3840:4864].rearrange("p (j k) -> p j k", j=QPK)
        pT = G[:, 4864:5888].rearrange("p (b j q) -> p b j q", b=2, j=QPK)
        qT = G[:, 5888:6912].rearrange("p (t j q) -> p t j q", t=TT, j=QPK)
        kT = G[:, 6912:7168]
        attn = G[:, 7168:8192].rearrange("p (t n) -> p t n", t=TT)
        cbT = G[:, 8192:9216].rearrange("p (m n) -> p m n", m=CT)
        hp = G[:, 9216:10248].rearrange("p (m n) -> p m n", m=CT)
        cy = G[:, 10248:11272].rearrange("p (m n) -> p m n", m=CT)
        junk = wk[:, 0:1280]
        junk_a = wk[:, 1280:2304]
        rp = wk[:, 2304:3584].rearrange("p (n a b) -> p n a b", n=2, b=HD // 2)
        A1, A2, attn_g = vec[:, 0:D], vec[:, D:2 * D], vec[:, 2 * D:2 * D + AW]
        qg, kg = vec[:, 2560:2624], vec[:, 2624:2688]
        sinks = vec[:, 2688:2696]
        shift1, scale1, gate1, shift2, scale2, gate2 = (modr[:, D * i:D * (i + 1)] for i in range(6))
        qpT = wk[:, 0:4096].rearrange("p (a t) -> p a t", a=HP)
        skT = wk[:, 4096:6144].rearrange("p (a k) -> p a k", a=HP)
        rt = wk[:, 6144:8704]
        vals = rt[:, 0:256].rearrange("p (a k) -> p a k", a=HP)
        ids_u = rt[:, 256:512].bitcast(U32).rearrange("p (a k) -> p a k", a=HP)
        ids_f = rt[:, 512:768].rearrange("p (h s k) -> p h s k", s=2, k=TOPK)
        top = rt[:, 768:896].rearrange("p (h k) -> p h k", h=HEADS)
        pos_u = rt[:, 896:1024].bitcast(U32).rearrange("p (h k) -> p h k", h=HEADS)
        ab_u = rt[:, 1024:1280].bitcast(U32).rearrange("p (s n) -> p s n", s=2)
        ab_f = rt[:, 1280:1536].rearrange("p (s n) -> p s n", s=2)
        pick = rt[:, 1536:1792].rearrange("p (s n) -> p s n", s=2)
        rsm = rt[:, 1792:1824]
        cand = G[:, 0:2048].rearrange("p (h n) -> p h n", h=HEADS)
        cand2 = G[:, 2048:4096].rearrange("p (h n) -> p h n", h=HEADS)
        sc = G[:, 4096:8192].rearrange("p (t a k) -> p t a k", t=TT, a=HP)
        sc2 = G[:, 8192:10240].rearrange("p (a k) -> p a k", a=HP)
        onehot = G[:, 10240:12288]
        rows = G[:, 0:NR * D].rearrange("p (s n) -> p s n", s=NR)
        acc = wk[:, 0:2048].rearrange("p (s n) -> p s n", s=2)
        ln0_g, ln0_b = wk[:, 2048:3072], wk[:, 3072:4096]
        xmeta = wk[0:META, 4096:5120]
        bc_raw = wk[:, 5120:6144].rearrange("p (s i h) -> p s i h", s=4, i=SI)
        bb = wk[:, 6144:7168].rearrange("p (s i h) -> p s i h", s=4, i=SI)
        bd = wk[:, 7168:8192].rearrange("p (s n) -> p s n", s=2)
        s5c = wk[:, 8192:8448].rearrange("p (s i) -> p s i", s=16)
        s5k = wk[:, 8448:8464].bitcast(I32)
        bdT = modr[:, 3072:4096].rearrange("p (s q n) -> p s q n", s=2, q=4)
        cd = modr[:, 4096:5120].rearrange("p (s i n) -> p s i n", s=2, i=SI)
        qk_in = modr[:, 0:2200].rearrange("p (m n) -> p m n", m=8)
        gyT = modr[:, 0:1024].rearrange("p (m n) -> p m n", m=4)
        row_a = modr[0:MH, 2200:3016].rearrange("p (s n) -> p s n", s=3)
        vtok = G[:, 0:3072].rearrange("p (t n) -> p t n", t=3)
        otok = G[:, 3072:5120].rearrange("p (t n) -> p t n", t=TT)
        gs = G[:, 5120:7168].rearrange("p (t n) -> p t n", t=TT)
        gm = G[:, 7168:9216].rearrange("p (t n) -> p t n", t=TT)
        qkT = G[:, 9216:11392].rearrange("p (m n) -> p m n", m=8)
        row_b = G[0:MH, 11392:12208].rearrange("p (s n) -> p s n", s=3)
        QW = 4 * LEN
        s5t = [wk[:, QW * i:QW * (i + 1)].rearrange("p (i n) -> p i n", i=4) for i in range(8)]
        s5t_i = wk[:, QW * 3:QW * 4].bitcast(I32).rearrange("p (i n) -> p i n", i=4)
        PT = wk[:, 0:3072].rearrange("p (b h n) -> p b h n", b=3, h=MH)
        hm = wk[:, 3072:5120].rearrange("p (t n) -> p t n", t=TT)
        tmp2 = wk[:, 5120:7168].rearrange("p (t n) -> p t n", t=TT)
        ffT = wk[:, 0:8192].rearrange("p (k n) -> p k n", k=FF // P)
        m_norm, ln1_g, ln1_b = vec[:, 0:D], vec[:, D:2 * D], vec[:, 2 * D:3 * D]
        ln2_g, ln2_b = modr[:, 0:D], modr[:, D:2 * D]
        fin = G[:, 0:2048].rearrange("p (t n) -> p t n", t=TT)

        ring_full = [sem(f"ring_full{i}") for i in range(RING)]
        chunk_used = sem("chunk_used")
        bank_full = [sem(f"bank_full{i}") for i in range(ACC)]
        bank_free = [sem(f"bank_free{i}") for i in range(ACC)]
        turned = sem("turned")
        turn_read = sem("turn_read")
        row_full = [sem(f"row_full{i}") for i in range(NR)]
        row_free = sem("row_free")
        S_ = {}

        def flag(name):
            if name not in S_:
                S_[name] = sem(name)
            return S_[name]

        def group_wait(eng, name, i):
            g = GROUP_NO[(name, i)]
            eng.wait_ge(bank_full[g % ACC], g // ACC + 1)

        def bank_of(name, i):
            return psum[:, GROUP_NO[(name, i)] % ACC, :]

        def read_out(ins, name, i):
            ins.then_inc(bank_free[GROUP_NO[(name, i)] % ACC], 1)

        block = ctx.enter_context(nc.Block())
        turns = []
        turns += [("h1", t, q) for t in range(TT) for q in range(2)]
        turns += [("qT", t, 0) for t in range(TT)] + [("kT", 0, 0), ("css", 0, 0)]
        for t in range(TT):
            for s in range(NKV):
                turns += [("P", t, 2 * s + b) for b in range(t + 1)]
        turns += [("m", t, 0) for t in range(TT)]
        turns += [("h2", t, q) for t in range(TT) for q in range(2)]
        turns += [("sc", t, b) for t in range(TT) for b in range(4)]
        turns += [("bd", c, 0) for c in range(2)] + [("meta", 0, q) for q in range(2)]
        turns += [("h0", t, q) for t in range(TT) for q in range(2)]
        turns += [("if", c, 0) for c in range(2)] + [("ga", 0, 0), ("den", 0, 0)]
        for nm in ("hm", "mix", "hb"):
            turns += [(nm, t, q) for t in range(TT) for q in range(2)]
        turn_no = {u: n for n, u in enumerate(turns)}

        def turn_bank(*u):
            return psum[:, 4 + turn_no[u] % 2, :]

        def turn_wait(eng, *u):
            eng.wait_ge(turned, turn_no[u] + 1)

        def turn_read_wait(eng, *u):
            eng.wait_ge(turn_read, turn_no[u] + 1)

        def read_wait(eng, name, i):
            g = GROUP_NO[(name, i)]
            eng.wait_ge(bank_free[g % ACC], g // ACC + 1)

        @block.sync
        def _(sp):
            for c, (_, w, k0, kt, col, n) in enumerate(CHUNKS):
                if c >= RING:
                    if GROUPS[c - RING]:
                        group_wait(sp, *GROUPS[c - RING][-1])
                    else:
                        sp.wait_ge(flag("down_used"), c - RING - (len(CHUNKS) - 8) + 1)
                dst = ring[:, c % RING, 0:kt * n].rearrange("p (k n) -> p k n", k=kt)
                src = T[w].rearrange("(k p) n -> p k n", p=P)[:, k0:k0 + kt, col:col + n]
                sp.dma_start(dst, src).then_inc(ring_full[c % RING], 16)
            for t in range(TT):
                sp.wait_ge(flag("fin_ready"), t + 1)
                sp.dma_start(out[t * P:(t + 1) * P, :], fin[:, t, :]).then_inc(flag("stored"), 16)
            sp.wait_ge(flag("stored"), 16 * TT)

        def rowvec(name, lo, hi):
            return T[name][lo:hi].partition_broadcast(P)

        @block.gpsimd
        def _(pool):
            pool.memset(ident[:, :], 0.0)
            pool.memset(ones[:, :], 1.0)
            pool.memset(mask[:, :, :], 0.0)
            pool.memset(causal[:, :], 1.0)
            pool.iota(iota_t[:, :], [[1, LEN]], base=0, channel_multiplier=0,
                      allow_small_or_imprecise_dtypes=True)
            pool.iota(iota16[:, :], [[1, TOPK]], base=0, channel_multiplier=0,
                      allow_small_or_imprecise_dtypes=True)
            for j in range(HD // 2):
                pool.memset(inv_freq[:, j:j + 1], float(np.float32(THETA) ** np.float32(-2.0 * j / HD)))
            pool.drain()
            pool.affine_select(out=ident[:, :], in_=ident[:, :], compare_op=ALU.not_equal, fill=1.0,
                               base=0, pattern=[[-1, P]], channel_multiplier=1)
            pool.affine_select(out=mask[:, 0, :], in_=mask[:, 0, :], compare_op=ALU.is_gt, fill=NEG,
                               base=0, pattern=[[1, P]], channel_multiplier=-1)
            pool.affine_select(out=mask[:, 1, :], in_=mask[:, 1, :], compare_op=ALU.is_ge, fill=NEG,
                               base=0, pattern=[[-1, P]], channel_multiplier=1)
            pool.affine_select(out=causal[:, :], in_=causal[:, :], compare_op=ALU.is_ge, fill=0.0,
                               base=0, pattern=[[1, P]], channel_multiplier=-1)
            pool.drain().then_inc(flag("consts"), 1)

            pool.wait_ge(flag("h2_ready"), 1)
            for i, c in enumerate((V0, O0, GS0, GM0)):
                pool.dma_start(vec[:, D * i:D * (i + 1)], rowvec("b_in_2", c, c + D)).then_inc(
                    flag("in_bias2"), 16)
            pool.wait_ge(flag("routed"), 1)
            pool.dma_start(bc_raw, T["s5_bc"]).then_inc(flag("in_bc"), 16)
            pool.dma_start(ln0_g, rowvec("ln0_g_2", 0, D)).then_inc(flag("in_ln0"), 16)
            pool.dma_start(ln0_b, rowvec("ln0_b_2", 0, D)).then_inc(flag("in_ln0"), 16)
            pool.dma_start(xmeta, T["meta_tokens_2"]).then_inc(flag("in_ln0"), 16)

            for t in range(TT):
                with pool.Fori(0, HEADS // 2) as pair:
                    for par in range(2):
                        for part, tab in enumerate(("peer_u", "peer_v")):
                            for k in range(TOPK):
                                at = 32 * par + TOPK * part + k
                                s = at % NR
                                pool.wait_ge(row_free, pair * 64 + (t * 256 + at + 1))
                                if part == 0 and k == 0:
                                    pool.wait_ge(flag("staged"), pair * 2 + (t * HEADS + par + 1))
                                pool.sem_inc(flag("gather_cleared"), 1)
                                pool.indirect_dma_start(
                                    rows[:, s, :], None, T[tab],
                                    bass.IndirectOffsetOnAxis(ap=stage[:, par, k:k + 1], axis=0),
                                ).then_inc(row_full[s], 16)

            for t in range(3):
                for n in range(2):
                    read_wait(pool, "v2", 3 * n + t)
            pool.wait_ge(flag("in_bias2"), 64)
            pool.tensor_tensor(vtok[0:META, 0, :], vtok[0:META, 0, :], vec[0:META, 0:D], ALU.add)
            pool.tensor_tensor(vtok[:, 1:3, :], vtok[:, 1:3, :], over(vec[:, 0:D], 1, TT),
                               ALU.add).then_inc(flag("v_ready"), 1)
            for i, (nm, dst) in enumerate((("o2", otok), ("gs", gs), ("gm", gm))):
                for j in range(2 * TT):
                    read_wait(pool, nm, j)
                pool.tensor_tensor(dst, dst, over(vec[:, D * (i + 1):D * (i + 2)], 1, TT),
                                   ALU.add).then_inc(flag("gate_biased"), 1)
            pool.drain()
            pool.dma_start(m_norm, rowvec("m_norm_g_2", 0, D)).then_inc(flag("in_ln1"), 16)
            pool.dma_start(ln1_g, rowvec("ln1_g_2", 0, D)).then_inc(flag("in_ln1"), 16)
            pool.dma_start(ln1_b, rowvec("ln1_b_2", 0, D)).then_inc(flag("in_ln1"), 16)
            pool.wait_ge(flag("glu_read"), 1)
            pool.dma_start(ln2_g, rowvec("ln2_g_2", 0, D)).then_inc(flag("in_ln2"), 16)
            pool.dma_start(ln2_b, rowvec("ln2_b_2", 0, D)).then_inc(flag("in_ln2"), 16)

        @block.tensor
        def _(pe):
            used = [0]

            def begin_turn(*u):
                if turn_no[u] >= 2:
                    pe.wait_ge(turn_read, turn_no[u] - 1)
                return turn_bank(*u)

            def transpose_tile(name, t, src, rows_=P, ready=None):
                for q in range(2):
                    bank = begin_turn(name, t, q)
                    if ready and q == 0:
                        pe.wait_ge(*ready)
                    for j in range(4):
                        k = 4 * q + j
                        last = pe.transpose(bank[:, j * rows_:(j + 1) * rows_],
                                            src[:, k * P:(k + 1) * P], ident[0:rows_, 0:rows_])
                    last.then_inc(turned, 1)

            def next_chunk():
                c = used[0]
                used[0] += 1
                pe.wait_ge(ring_full[c % RING], 16 * (c // RING + 1))
                kt, n = CHUNKS[c][3], CHUNKS[c][5]
                return ring[:, c % RING, 0:kt * n].rearrange("p (k n) -> p k n", k=kt)

            def group(name, i, lhs, rhs, kt, m, n):
                g = GROUP_NO[(name, i)]
                if g >= ACC:
                    pe.wait_ge(bank_free[g % ACC], g // ACC)
                for k in range(kt):
                    last = pe.matmul(psum[0:m, g % ACC, 0:n], lhs(k), rhs(k),
                                     start=(k == 0), stop=(k == kt - 1))
                last.then_inc(bank_full[g % ACC], 1)

            def by_token(name, i, t, w, src, n=512, col=0, kt=KD, base=0, m=P):
                group(name, i, lambda k: src[:, k, base + t * P:base + t * P + m],
                      lambda k: w[:, k, col:col + n], kt, m, n)

            def by_feature(name, i, w, m, lo, hi):
                group(name, i, lambda k: w[:, k, m * P:(m + 1) * P], lambda k: featT[:, k, lo:hi],
                      KD, P, hi - lo)

            def ada(i):
                w = next_chunk()
                group("ada", i, lambda k: crep[:, k, :], lambda k: w[:, k, :], KD, P, 512)

            pe.wait_ge(flag("crep_ready"), 1)
            pe.wait_ge(flag("consts"), 1)
            for i in range(4):
                ada(i)
            for t in range(TT):
                transpose_tile("h1", t, hbuf[:, t, :], ready=(flag("h1_ready"), 1))
            turn_read_wait(pe, "h1", TT - 1, 1)
            w = next_chunk()
            for t in range(TT):
                by_token("q1", t, t, w, featT)
            w = next_chunk()
            for t in range(TT):
                by_token("kv1", t, t, w, featT, n=256)
            for nm in ("cb", "cc", "cu"):
                w = next_chunk()
                for m in range(4):
                    by_feature(nm, m, w, m, 0, SEQ)
            ada(4)
            ada(5)
            pe.wait_ge(flag("rope_done"), 1)
            for t in range(TT):
                bank = begin_turn("qT", t, 0)
                for j in range(QPK):
                    last = pe.transpose(bank[:, j * P:(j + 1) * P],
                                        qkr[:, t, j * P:(j + 1) * P], ident[:, :])
                last.then_inc(turned, 1)
            bank = begin_turn("kT", 0, 0)
            for t in range(TT):
                last = pe.transpose(bank[:, t * P:(t + 1) * P], qkr[:, t, AW:QKW], ident[:, :])
            last.then_inc(turned, 1)
            bank = begin_turn("css", 0, 0)
            pe.wait_ge(flag("conv_sq"), 1)
            for m in range(CT):
                last = pe.matmul(bank[:, 0:SEQ], ones[:, :], hp[:, m, 0:SEQ],
                                 start=(m == 0), stop=(m == CT - 1))
            last.then_inc(turned, 1)
            turn_read_wait(pe, "kT", 0, 0)
            unit = 0
            extra = [6, 7, 8, 9, 10, 11]
            for t in range(TT):
                nk = P * (t + 1)
                for s in range(NKV):
                    if unit:
                        pe.wait_ge(flag("O_read"), unit)
                    for j in range(QPK):
                        last = pe.matmul(psum[:, 6 + j // 2, (j % 2) * 256:(j % 2) * 256 + nk],
                                         qT[64 * s:64 * s + 64, t, j, :], kT[64 * s:64 * s + 64, 0:nk],
                                         start=True, stop=True)
                    last.then_inc(flag("S_full"), 1)
                    for _ in range(2 if unit < 2 else 1):
                        ada(extra.pop(0))
                    pe.wait_ge(flag("exp_done"), unit + 1)
                    for b in range(t + 1):
                        bank = begin_turn("P", t, 2 * s + b)
                        for j in range(QPK):
                            last = pe.transpose(bank[:, j * P:(j + 1) * P],
                                                S[:, j, b * P:(b + 1) * P], ident[:, :])
                        last.then_inc(turned, 1)
                    turn_read_wait(pe, "P", t, 2 * s + t)
                    for j in range(QPK):
                        for b in range(t + 1):
                            last = pe.matmul(psum[:, 6, j * HD:(j + 1) * HD], pT[:, b, j, :],
                                             qkv[:, b, QKW + s * HD:QKW + (s + 1) * HD],
                                             start=(b == 0), stop=(b == t))
                    last.then_inc(flag("O_full"), 1)
                    unit += 1
            pe.wait_ge(flag("attn_normed"), 1)
            for t in range(TT):
                bank = begin_turn("m", t, 0)
                for j in range(4):
                    last = pe.transpose(bank[:, j * P:(j + 1) * P], attn[:, t, j * P:(j + 1) * P],
                                        ident[:, :])
                last.then_inc(turned, 1)
            turn_read_wait(pe, "m", TT - 1, 0)
            pe.wait_ge(flag("conv_merged"), 1)
            for n in range(2):
                w = next_chunk()
                for t in range(TT):
                    by_token("out1", TT * n + t, t, w, featT)
            for t in range(TT):
                transpose_tile("h2", t, hbuf[:, t, :], ready=(flag("h2_ready"), 1))
            turn_read_wait(pe, "h2", TT - 1, 1)
            for n in range(4):
                w = next_chunk()
                for m in range(4):
                    by_feature("wq", 4 * n + m, w, m, 0, SEQ)
            pe.wait_ge(flag("in_sk"), 16)
            for a in range(HP - 4, HP):
                read_wait(pe, "wq", a)
            for t in range(TT):
                for b in range(4):
                    bank = begin_turn("sc", t, b)
                    for j in range(4):
                        last = pe.matmul(bank[:, j * KEYS:(j + 1) * KEYS],
                                         qpT[:, 4 * b + j, t * P:(t + 1) * P], skT[:, 4 * b + j, :],
                                         start=True, stop=True)
                    last.then_inc(turned, 1)
            pe.wait_ge(flag("bd_ready"), 1)
            for c in range(2):
                bank = begin_turn("bd", c, 0)
                for q in range(4):
                    last = pe.transpose(bank[:, q * P:(q + 1) * P], bd[:, c, q * P:(q + 1) * P],
                                        ident[:, :])
                last.then_inc(turned, 1)
            transpose_tile("meta", 0, xmeta, rows_=META, ready=(flag("meta_ready"), 1))
            for t in range(TT):
                transpose_tile("h0", t, hbuf[:, t, :], ready=(flag("h0_ready"), 1))
            turn_read_wait(pe, "h0", TT - 1, 1)
            for nm in ("u", "q2", "k2"):
                w = next_chunk()
                for m in range(4):
                    by_feature(nm, m, w, m, 0, LEN)
            pe.wait_ge(flag("in_if"), 32)
            for c in range(2):
                bank = begin_turn("if", c, 0)
                for k in range(KD):
                    last = pe.matmul(bank[0:MH, 0:LEN], w_if[:, k, MH * c:MH * (c + 1)], featT[:, k, :],
                                     start=(k == 0), stop=(k == KD - 1))
                last.then_inc(turned, 1)

            def s5_in(q):
                read_wait(pe, "u", q)
                turn_read_wait(pe, "bd", 1, 0)
                if q:
                    pe.wait_ge(flag("y_read"), q)
                for i in range(4):
                    for c in range(2):
                        n = 8 * q + 2 * i + c
                        if n >= 2:
                            pe.wait_ge(flag("bu_read"), n - 1)
                        pe.matmul(psum[:, 6 + c, 0:LEN], bdT[32 * i:32 * i + 32, c, q, :],
                                  uT[32 * i:32 * i + 32, q, :], start=True,
                                  stop=True).then_inc(flag("bu_full"), 1)

            def s5_out(q):
                pe.wait_ge(flag("state_ready"), q + 1)
                for i in range(4):
                    for c in range(2):
                        last = pe.matmul(psum[32 * i:32 * i + 32, 6, 0:SEQ], cd[:, c, 4 * q + i, :],
                                         s5t[4 + c][:, i, META:LEN], start=(c == 0), stop=(c == 1))
                last.then_inc(flag("y_full"), 1)

            s5_in(0)
            for n in range(2):
                w = next_chunk()
                by_token("v2", 3 * n, 0, w, featT, m=META)
                for t in range(TT):
                    by_token("v2", 3 * n + 1 + t, t, w, featT, base=META)
            for q, nm in enumerate(("o2", "gs", "gm")):
                s5_out(q)
                s5_in(q + 1)
                for n in range(2):
                    w = next_chunk()
                    for t in range(TT):
                        by_token(nm, TT * n + t, t, w, featT, base=META)
            pe.wait_ge(flag("rows_ready"), 1)
            bank = begin_turn("ga", 0, 0)
            pe.transpose(bank[0:META, 0:MH], row_b[:, 0, 0:META], ident[0:MH, 0:MH])
            for t in range(TT):
                lo = META + t * P
                pe.transpose(bank[:, MH * (1 + t):MH * (2 + t)], row_b[:, 0, lo:lo + P],
                             ident[0:MH, 0:MH])
                last = pe.transpose(bank[:, MH * (3 + t):MH * (4 + t)], row_b[:, 2, lo:lo + P],
                                    ident[0:MH, 0:MH])
            last.then_inc(turned, 1)
            s5_out(3)
            pe.wait_ge(flag("y_read"), 4)
            for h in range(MH):
                last = pe.matmul(psum[:, 6 + h // 2, (h % 2) * SEQ:(h % 2 + 1) * SEQ],
                                 ident[0:MH, h:h + 1].broadcast_to([MH, P]), row_b[:, 1, META:LEN],
                                 start=True, stop=True)
            last.then_inc(flag("mbc_full"), 1)
            pe.wait_ge(flag("conv2_done"), 1)
            n = 0
            for b in range(3):
                nr = META if b == 0 else P
                lo = 0 if b == 0 else META + (b - 1) * P
                for hh in range(2):
                    if n < 2:
                        pe.wait_ge(flag("mbc_read"), 1)
                    else:
                        pe.wait_ge(flag("st_read"), n - 1)
                    for h in (2 * hh, 2 * hh + 1):
                        last = pe.matmul(psum[0:nr, 6 + n % 2, (h % 2) * SEQ:(h % 2 + 1) * SEQ],
                                         qkT[:, MH + h, lo:lo + nr], qkT[:, h, META:LEN],
                                         start=True, stop=True)
                    last.then_inc(flag("st_full"), 1)
                    n += 1
            pe.wait_ge(flag("PT_ready"), 1)
            pe.wait_ge(flag("v_ready"), 1)

            def key_tiles(t):
                return [(b, META if b == 0 else P) for b in range(t + 2)]

            bank = begin_turn("den", 0, 0)
            for t in range(TT):
                for h in range(MH):
                    for b, nr in key_tiles(t):
                        last = pe.matmul(bank[:, MH * t + h:MH * t + h + 1],
                                         PT[0:nr, b, h, t * P:(t + 1) * P], ones[0:nr, 0:1],
                                         start=(b == 0), stop=(b == t + 1))
            last.then_inc(turned, 1)
            n = 0
            for t in range(TT):
                for hh in range(2):
                    if n < 2:
                        pe.wait_ge(flag("st_read"), 6)
                    else:
                        pe.wait_ge(flag("num_read"), n - 1)
                    for h in (2 * hh, 2 * hh + 1):
                        for b, nr in key_tiles(t):
                            last = pe.matmul(psum[:, 6 + n % 2, (h % 2) * DV:(h % 2 + 1) * DV],
                                             PT[0:nr, b, h, t * P:(t + 1) * P],
                                             vtok[0:nr, b, h * DV:(h + 1) * DV],
                                             start=(b == 0), stop=(b == t + 1))
                    last.then_inc(flag("num_full"), 1)
                    n += 1
            pe.wait_ge(flag("gy_ready"), 4)
            for z in range(2):
                w = next_chunk()
                for n in range(2):
                    for t in range(TT):
                        by_token("glu", 4 * z + 2 * n + t, t, w, gyT, col=512 * n, kt=4)
            for nm, ready, prod in (("hm", "hm_ready", "mo"), ("mix", "mix_ready", "wo")):
                src = hm if nm == "hm" else gs
                for t in range(TT):
                    transpose_tile(nm, t, src[:, t, :], ready=(flag(ready), 1))
                turn_read_wait(pe, nm, TT - 1, 1)
                for n in range(2):
                    w = next_chunk()
                    for t in range(TT):
                        by_token(prod, TT * n + t, t, w, featT)
            for t in range(TT):
                transpose_tile("hb", t, hbuf[:, t, :], ready=(flag("hb_ready"), 1))
            turn_read_wait(pe, "hb", TT - 1, 1)
            for n in range(8):
                w = next_chunk()
                for m in range(4):
                    by_feature("up", 4 * n + m, w, m, 0, SEQ)
            for n in range(8):
                w = next_chunk()
                pe.wait_ge(flag("ff_ready"), n + 1)
                for t in range(TT):
                    for half in range(2):
                        for k in range(4):
                            last = pe.matmul(psum[:, 4 + 2 * t + half, :],
                                             ffT[:, 4 * n + k, t * P:(t + 1) * P],
                                             w[:, k, 512 * half:512 * (half + 1)],
                                             start=(n == 0 and k == 0), stop=(n == 7 and k == 3))
                last.then_inc(flag("down_used"), 1)
        ss, ms, sd, rs = (st[:, 2 * i:2 * i + 2] for i in range(4))
        mss, mms, msd, mrs = (st[0:META, 8 + i:9 + i] for i in range(4))
        qss, qrs = st[:, 12:32], st[:, 32:52]
        rmax, esink, den4 = st[:, 52:56], st[:, 56:60], st[:, 60:64]
        c_act = st[:, 64:72]
        eps_c, ln_eps_c = st[:, 72:73], st[:, 73:74]
        gcol = col2[:, 0:20]
        enm, dens, rden = col2[:, 20:28], col2[:, 28:36], col2[:, 36:44]
        hsum, hvar, hrs = col2[:, 44:52], col2[:, 52:60], col2[:, 60:68]
        css = wk[:, 3584:3840]
        dt_, lr, th, thk, thc, mag, cosv, sinv, lbr, lbi, fr, fi, n2, ta, tb, ts_ = (
            s5c[:, i, :] for i in range(16))

        @block.scalar
        def _(act):
            def load(dst, src, name):
                act.dma_start(dst, src).then_inc(flag(name), 16)

            load(pack[:, :], T["pack"], "in_pack")
            load(pos_i[:, :], T["positions"], "in_pos")
            load(xres[:, :, :], T["x"].rearrange("(t p) n -> p t n", p=P), "in_x")
            load(modr[:, :], rowvec("ada_b", 0, 6 * D), "in_mod")
            load(A1, rowvec("norm1_g", 0, D), "in_n1")
            load(A2, rowvec("norm2_g", 0, D), "in_vec")
            load(attn_g, rowvec("attn_out_g", 0, AW), "in_vec")
            load(qg, rowvec("q_norm_g", 0, HD), "in_vec")
            load(kg, rowvec("k_norm_g", 0, HD), "in_vec")
            load(sinks, rowvec("sinks", 0, NQ), "in_vec")
            load(skT, T["subkeys"], "in_sk")
            load(w_if[:, :, :], T["w_if"], "in_if")
            load(b_if[:, :], T["b_if"], "in_if")
            load(s5_dt[:, :], T["log_dt"], "in_dt")

            act.wait_ge(flag("in_pack"), 16)
            act.activation(c_act, pk("c"), ACT.Silu).then_inc(flag("c_act"), 1)

            def square_sums(src, dst, scratch, name, tiles=TT):
                for t in range(tiles):
                    act.activation(scratch, src(t), ACT.Square, accum_out=dst(t)).then_inc(flag(name), 1)
                    act.drain()

            def roots(n, a, b, name):
                act.wait_ge(flag(n), 1)
                act.activation(b, a, ACT.Sqrt).then_inc(flag(name), 1)

            act.wait_ge(flag("in_x"), 16)
            square_sums(lambda t: xres[:, t, :], lambda t: ss[:, t:t + 1], junk_a, "n1_ss")
            roots("n1_ms", ms, sd, "n1_sd")
            act.wait_ge(flag("rope_reduced"), 1)
            act.activation(rope_t[:, 0:2, :, :], rope_t[:, 0:2, :, :], ACT.Sin).then_inc(
                flag("rope_tab"), 1)

            def read_turn(dst, src, *u, func=None, **kw):
                turn_wait(act, *u)
                ins = act.activation(dst, src, func, **kw) if func else act.copy(dst, src)
                ins.then_inc(turn_read, 1)

            def to_features(name, t, lo, width=P):
                for q in range(2):
                    src = turn_bank(name, t, q)[:, 0:4 * width].rearrange("p (j n) -> p j n", j=4)
                    read_turn(featT[:, 4 * q:4 * q + 4, lo:lo + width], src, name, t, q)

            def read_group(dst, name, i, n=512, m=P, func=None, **kw):
                group_wait(act, name, i)
                src = bank_of(name, i)[0:m, 0:n]
                ins = act.activation(dst, src, func, **kw) if func else act.copy(dst, src)
                read_out(ins, name, i)

            for t in range(TT):
                to_features("h1", t, t * P)
            for t in range(TT):
                read_group(qkv[:, t, 0:AW], "q1", t)
            for t in range(TT):
                read_group(qkv[:, t, AW:768], "kv1", t, n=256)
            for m in range(CT):
                read_group(cbT[:, m, :], "cb", m, n=SEQ)
            for m in range(CT):
                read_group(hp[:, m, 2:2 + SEQ], "cc", m, n=SEQ)
            roots("qk_ms", qss, qrs, "qk_sd")
            for t in range(TT):
                src = turn_bank("qT", t, 0).rearrange("p (j n) -> p j n", j=QPK)
                read_turn(qT[:, t, :, :], src, "qT", t, 0)
            read_turn(kT, turn_bank("kT", 0, 0)[:, 0:SEQ], "kT", 0, 0)
            read_turn(css, turn_bank("css", 0, 0)[:, 0:SEQ], "css", 0, 0, func=ACT.Sqrt,
                      scale=1.0 / CW, bias=eps_c)
            unit = 0
            for t in range(TT):
                nk = P * (t + 1)
                for s in range(NKV):
                    act.wait_ge(flag("S_shifted"), unit + 1)
                    act.activation(S[:, :, 0:nk], S[:, :, 0:nk], ACT.Exp)
                    act.activation(esink, esink, ACT.Exp).then_inc(flag("exp_done"), 1)
                    for b in range(t + 1):
                        src = turn_bank("P", t, 2 * s + b).rearrange("p (j n) -> p j n", j=QPK)
                        read_turn(pT[:, b, :, :], src, "P", t, 2 * s + b)
                    unit += 1
            act.wait_ge(flag("attn_done"), 1)
            square_sums(lambda t: attn[:, t, :], lambda t: ss[:, t:t + 1], junk_a[:, 0:AW], "at_ss")
            roots("at_ms", ms, sd, "at_sd")
            for t in range(TT):
                src = turn_bank("m", t, 0).rearrange("p (j n) -> p j n", j=4)
                read_turn(featT[:, 0:4, t * P:(t + 1) * P], src, "m", t, 0)
            act.wait_ge(flag("x1_ready"), 1)
            square_sums(lambda t: xres[:, t, :], lambda t: ss[:, t:t + 1], junk_a, "n2_ss")
            roots("n2_ms", ms, sd, "n2_sd")
            for t in range(TT):
                to_features("h2", t, t * P)
            for a in range(HP):
                read_group(qpT[:, a, :], "wq", a, n=SEQ)
            for t in range(TT):
                for b in range(4):
                    src = turn_bank("sc", t, b).rearrange("p (a k) -> p a k", a=4)
                    read_turn(sc[:, t, 4 * b:4 * b + 4, :], src, "sc", t, b)
            for t in range(TT):
                act.wait_ge(flag("top_shifted"), t + 1)
                act.activation(top, top, ACT.Exp).then_inc(flag("top_exp"), 1)
            act.wait_ge(flag("routed"), 1)
            act.wait_ge(flag("in_dt"), 16)
            act.activation(dt_, s5_dt[:, :], ACT.Exp).then_inc(flag("s5_dt_exp"), 1)
            act.wait_ge(flag("s5_args"), 1)
            act.activation(mag, lr, ACT.Exp)
            act.activation(cosv, thc, ACT.Sin)
            act.activation(sinv, thk, ACT.Sin).then_inc(flag("s5_tab"), 1)
            for c in range(2):
                read_turn(bdT[:, c, :, :], turn_bank("bd", c, 0).rearrange("p (q n) -> p q n", q=4),
                          "bd", c, 0)
            act.wait_ge(flag("meta_centered"), 1)
            act.activation(wk[0:META, 0:D], xmeta, ACT.Square, accum_out=mss).then_inc(flag("me_ss"), 1)
            roots("me_ms", mms, msd, "me_sd")
            to_features("meta", 0, 0, META)
            for t in range(TT):
                with act.Fori(0, HEADS // 2) as pair:
                    for par in range(2):
                        act.wait_ge(flag("head_done"), pair * 2 + (t * HEADS + par + 1))
                        act.copy(stage[:, par, :],
                                 idx[:, t, bass.ds(pair * 32 + par * TOPK, TOPK)]).then_inc(
                                     flag("staged"), 1)
                        act.wait_ge(flag("dots_ready"), pair * 2 + (t * HEADS + par + 1))
                        act.activation(gel[:, :], dots[:, :], ACT.Gelu_apprx_tanh).then_inc(
                            flag("gel_ready"), 1)
            act.wait_ge(flag("l0_centered"), 1)
            square_sums(lambda t: hbuf[:, t, :], lambda t: ss[:, t:t + 1], wk[:, 0:D], "l0_ss")
            roots("l0_ms", ms, sd, "l0_sd")
            for t in range(TT):
                to_features("h0", t, META + t * P)
            for m in range(4):
                read_group(uT[:, m, :], "u", m, n=LEN, func=ACT.Identity, bias=pk("b_uqk")[:, m:m + 1])
            for j, nm in enumerate(("q2", "k2")):
                for m in range(4):
                    read_group(qk_in[:, 4 * j + m, 3:3 + LEN], nm, m, n=LEN, func=ACT.Identity,
                               bias=pk("b_uqk")[:, 4 * (j + 1) + m:4 * (j + 1) + m + 1])
            act.wait_ge(flag("in_if"), 32)
            for c in range(2):
                read_turn(row_a[:, c, :], turn_bank("if", c, 0)[0:MH, 0:LEN], "if", c, 0,
                          func=ACT.Identity, bias=b_if[:, c:c + 1])

            def s5_tables(q):
                act.wait_ge(flag("ph_ready"), q + 1)
                act.activation(s5t[0], s5t[5], ACT.Sin)
                act.activation(s5t[1], s5t[4], ACT.Sin).then_inc(flag("s5_sin"), 1)

            def s5_read(q):
                if q:
                    act.wait_ge(flag("state_ready"), q)
                for i in range(4):
                    for c in range(2):
                        act.wait_ge(flag("bu_full"), 8 * q + 2 * i + c + 1)
                        act.copy(s5t[6 + c][:, i, :], psum[:, 6 + c, 0:LEN]).then_inc(flag("bu_read"), 1)

            def gelu_y(q):
                act.wait_ge(flag("y_read"), q + 1)
                act.activation(gyT[:, q, :], gyT[:, q, :], ACT.Gelu_apprx_tanh).then_inc(
                    flag("gy_ready"), 1)

            def read_tokens(name, dst):
                for n in range(2):
                    for t in range(TT):
                        read_group(dst[:, t, 512 * n:512 * (n + 1)], name, TT * n + t)

            s5_tables(0)
            s5_read(0)
            for n in range(2):
                for t in range(3):
                    m = META if t == 0 else P
                    read_group(vtok[0:m, t, 512 * n:512 * (n + 1)], "v2", 3 * n + t, m=m)
            s5_tables(1)
            s5_read(1)
            read_tokens("o2", otok)
            act.wait_ge(flag("conv2_y"), 1)
            for m in range(8):
                last = act.activation(qkT[:, m, :], qkT[:, m, :], ACT.Silu, bias=pk("qk_b")[:, m:m + 1])
            last.then_inc(flag("conv2_done"), 1)
            turn_read_wait(act, "if", 1, 0)
            act.activation(row_a[:, 2, :], row_a[:, 1, :], ACT.Abs)
            act.drain()
            act.activation(row_a[:, 2, :], row_a[:, 2, :], ACT.Exp, scale=-1.0)
            act.drain()
            act.activation(row_a[:, 2, :], row_a[:, 2, :], ACT.Ln, bias=1.0).then_inc(flag("ln_done"), 1)
            s5_tables(2)
            s5_read(2)
            gelu_y(0)
            gelu_y(1)
            read_tokens("gs", gs)
            s5_tables(3)
            s5_read(3)
            gelu_y(2)
            read_tokens("gm", gm)
            turn_wait(act, "ga", 0, 0)
            act.copy(gcol[0:META, 0:MH], turn_bank("ga", 0, 0)[0:META, 0:MH])
            act.copy(gcol[:, MH:5 * MH], turn_bank("ga", 0, 0)[:, MH:5 * MH]).then_inc(turn_read, 1)
            act.drain()
            act.activation(enm, gcol[:, 3 * MH:5 * MH], ACT.Exp, scale=-1.0).then_inc(flag("enm"), 1)
            gelu_y(3)
            act.wait_ge(flag("E_args"), 1)
            act.activation(PT[0:META, 0, :, :], PT[0:META, 0, :, :], ACT.Exp)
            act.activation(PT[:, 1, :, :], PT[:, 1, :, :], ACT.Exp)
            act.activation(PT[:, 2, :, P:SEQ], PT[:, 2, :, P:SEQ], ACT.Exp).then_inc(flag("E_exp"), 1)
            for i, dst in enumerate((otok, gs, gm)):
                act.wait_ge(flag("gate_biased"), i + 1)
                act.activation(dst, dst, ACT.Sigmoid).then_inc(flag("gate_sig"), 1)
            read_turn(dens, turn_bank("den", 0, 0)[:, 0:2 * MH], "den", 0, 0)
            for z in range(2):
                for n in range(2):
                    for t in range(TT):
                        dst = (xres, tmp2)[z][:, t, 512 * n:512 * (n + 1)]
                        read_group(dst, "glu", 4 * z + 2 * n + t, func=(None, ACT.Sigmoid)[z])
            act.drain().then_inc(flag("glu_read"), 1)
            roots("hv_ms", hvar, hrs, "hv_sd")
            for t in range(TT):
                to_features("hm", t, t * P)
            for t in range(TT):
                to_features("mix", t, t * P)
            act.wait_ge(flag("l1_centered"), 1)
            square_sums(lambda t: hbuf[:, t, :], lambda t: ss[:, t:t + 1], wk[:, 0:D], "l1_ss")
            roots("l1_ms", ms, sd, "l1_sd")
            for t in range(TT):
                to_features("hb", t, t * P)
            for k in range(FF // P):
                read_group(ffT[:, k, :], "up", k, n=SEQ, func=ACT.Relu, bias=pk("b_up")[:, k:k + 1])
            act.wait_ge(flag("l2_centered"), 1)
            square_sums(lambda t: fin[:, t, :], lambda t: ss[:, t:t + 1], ring[:, 0, 0:D], "l2_ss")
            roots("l2_ms", ms, sd, "l2_sd")

        @block.vector
        def _(dve):
            def tt(o, a, b, op):
                return dve.tensor_tensor(o, a, b, op)

            def ts(o, a, s1, s2=None, op0=ALU.mult, op1=None):
                if op1 is None:
                    return dve.tensor_scalar(o, a, s1, None, op0)
                return dve.tensor_scalar(o, a, s1, s2, op0, op1)

            def stt(o, a, s, b, op0=ALU.mult, op1=ALU.add):
                return dve.scalar_tensor_tensor(out=o, in0=a, scalar=s, in1=b, op0=op0, op1=op1)

            def reduced_rest(dst, k_f, quarter=0):
                stt(dst, k_f, -C2, dst)
                dve.drain()
                stt(dst, k_f, -C3, dst)
                dve.drain()
                ts(dst, dst, 0.5 * math.pi * quarter, PI_IN, ALU.add, ALU.min)
                dve.drain()
                return ts(dst, dst, -PI_IN, None, ALU.max)

            def reduce_angle(dst, ang, k_i, k_f, quarter=0):
                ts(k_i, ang, 1.0 / TWO_PI, 0.25 * quarter, ALU.mult, ALU.add)
                dve.drain()
                dve.tensor_copy(k_f, k_i)
                dve.drain()
                stt(dst, k_f, -C1, ang)
                dve.drain()
                return reduced_rest(dst, k_f, quarter)

            def mean_squares(name, n, eps, a=ss, b=ms, count=TT):
                dve.wait_ge(flag(name + "_ss"), count)
                ts(b, a, 1.0 / n, eps, ALU.mult, ALU.add).then_inc(flag(name + "_ms"), 1)

            def inverse_roots(name, a=sd, b=rs):
                dve.wait_ge(flag(name + "_sd"), 1)
                dve.reciprocal(b, a)
                dve.drain()

            dve.wait_ge(flag("c_act"), 1)
            dve.tensor_copy(crep, over(c_act, 2, P)).then_inc(flag("crep_ready"), 1)
            dve.wait_ge(flag("in_pos"), 16)
            dve.wait_ge(flag("consts"), 1)
            dve.tensor_copy(st[:, 74:76], pos_i[:, :])
            dve.memset(eps_c, EPS)
            dve.memset(ln_eps_c, LN_EPS)
            dve.memset(hp[:, :, 0:2], 0.0)
            dve.drain()
            for t in range(TT):
                ts(rope_t[:, 2, t, :], inv_freq[:, :], st[:, 74 + t:75 + t])
            dve.drain()
            k_i = junk[:, 0:64].bitcast(I32).rearrange("p (t n) -> p t n", t=TT)
            reduce_angle(rope_t[:, 1, :, :], rope_t[:, 2, :, :], k_i, rope_t[:, 3, :, :])
            dve.drain()
            reduce_angle(rope_t[:, 0, :, :], rope_t[:, 2, :, :], k_i, rope_t[:, 3, :, :],
                         quarter=1).then_inc(flag("rope_reduced"), 1)

            def add_mod(i):
                group_wait(dve, "ada", i)
                if i == 0:
                    dve.wait_ge(flag("in_mod"), 16)
                sl = modr[:, 512 * i:512 * (i + 1)]
                read_out(tt(sl, sl, bank_of("ada", i), ALU.add), "ada", i)

            mean_squares("n1", D, EPS)
            inverse_roots("n1")
            for i in range(4):
                add_mod(i)
            dve.drain()
            dve.wait_ge(flag("in_n1"), 16)
            dve.wait_ge(flag("in_vec"), 16 * 5)

            def modulated(gain, scale, shift, name):
                stt(gain, scale, 1.0, gain, ALU.add, ALU.mult)
                dve.drain()
                for t in range(TT):
                    stt(hbuf[:, t, :], xres[:, t, :], rs[:, t:t + 1], gain, ALU.mult, ALU.mult)
                dve.drain()
                tt(hbuf[:, :, :], hbuf[:, :, :], over(shift, 1, TT), ALU.add).then_inc(flag(name), 1)

            modulated(A1, scale1, shift1, "h1_ready")

            for t in range(TT):
                read_wait(dve, "q1", t)
                read_wait(dve, "kv1", t)
            for t in range(TT):
                sq = junk[:, 0:QKW]
                tt(sq, qkv[:, t, 0:QKW], qkv[:, t, 0:QKW], ALU.mult)
                dve.drain()
                dve.tensor_reduce(qss[:, 10 * t:10 * t + 10],
                                  sq.rearrange("p (h d) -> p h d", d=HD), X, ALU.add)
                dve.drain()
            ts(qss, qss, 1.0 / HD, EPS, ALU.mult, ALU.add).then_inc(flag("qk_ms"), 1)
            dve.wait_ge(flag("qk_sd"), 1)
            dve.reciprocal(qrs, qrs)
            dve.wait_ge(flag("rope_tab"), 1)
            dve.drain()
            for t in range(TT):
                v = qkv[:, t, 0:QKW].rearrange("p (h d) -> p h d", d=HD)
                o = qkr[:, t, :].rearrange("p (h d) -> p h d", d=HD)
                tt(v, v, over(qrs[:, 10 * t:10 * t + 10], 2, HD), ALU.mult)
                dve.drain()
                tt(v[:, 0:NQ, :], v[:, 0:NQ, :], over(qg, 1, NQ), ALU.mult)
                tt(v[:, NQ:10, :], v[:, NQ:10, :], over(kg, 1, NKV), ALU.mult)
                dve.drain()
                x1, x2 = v[:, :, 0:32], v[:, :, 32:64]
                cos, sin = over(rope_t[:, 0, t, :], 1, 10), over(rope_t[:, 1, t, :], 1, 10)
                tt(rp[:, 0, 0:10, :], x1, cos, ALU.mult)
                tt(rp[:, 1, 0:10, :], x2, sin, ALU.mult)
                tt(rp[:, 0, 10:20, :], x2, cos, ALU.mult)
                tt(rp[:, 1, 10:20, :], x1, sin, ALU.mult)
                dve.drain()
                oq = qkr[:, t, 0:AW].rearrange("p (j s d) -> p s j d", s=NKV, d=HD)
                for lo, at, op in ((0, 0, ALU.subtract), (32, 10, ALU.add)):
                    a, b = (rp[:, i, at:at + NQ, :].rearrange("p (s j) d -> p s j d", s=NKV)
                            for i in range(2))
                    tt(oq[:, :, :, lo:lo + 32], a, b, op)
                    tt(o[:, NQ:10, lo:lo + 32], rp[:, 0, at + NQ:at + 10, :],
                       rp[:, 1, at + NQ:at + 10, :], op)
                dve.drain()
            dve.engine_nop().then_inc(flag("rope_done"), 1)

            for m in range(CT):
                read_wait(dve, "cc", m)
                read_wait(dve, "cb", m)
                group_wait(dve, "cu", m)
                sl = hp[:, m, 2:2 + SEQ]
                read_out(tt(sl, sl, bank_of("cu", m)[:, 0:SEQ], ALU.mult), "cu", m)
            dve.drain()
            w = pk("conv_w").rearrange("p (k m) -> p k m", k=3)
            for m in range(CT):
                ts(cy[:, m, :], hp[:, m, 0:SEQ], w[:, 0, m:m + 1])
            for k in (1, 2):
                dve.drain()
                for m in range(CT):
                    stt(cy[:, m, :], hp[:, m, k:k + SEQ], w[:, k, m:m + 1], cy[:, m, :])
            dve.drain()
            tt(cy, cy, cbT, ALU.mult)
            dve.drain()
            tt(hp[:, :, 0:SEQ], cy, cy, ALU.mult).then_inc(flag("conv_sq"), 1)
            add_mod(4)
            add_mod(5)

            unit = 0
            extra = [6, 7, 8, 9, 10, 11]
            for t in range(TT):
                nk = P * (t + 1)
                mk = mask[:, 1 - t:2, :].rearrange("p b k -> p (b k)")
                for s in range(NKV):
                    dve.wait_ge(flag("S_full"), unit + 1)
                    sp4 = psum[:, 6:8, :].rearrange("p b (j k) -> p (b j) k", j=2)[:, :, 0:nk]
                    Sv = S[:, :, 0:nk]
                    stt(Sv, sp4, HD ** -0.5, over(mk, 1, QPK))
                    dve.drain()
                    dve.tensor_reduce(rmax, Sv, X, ALU.max)
                    dve.drain()
                    tt(rmax, rmax, sinks[:, 4 * s:4 * s + 4], ALU.max)
                    dve.drain()
                    tt(esink, sinks[:, 4 * s:4 * s + 4], rmax, ALU.subtract)
                    tt(Sv, Sv, over(rmax, 2, nk), ALU.subtract).then_inc(flag("S_shifted"), 1)
                    for _ in range(2 if unit < 2 else 1):
                        add_mod(extra.pop(0))
                    dve.wait_ge(flag("exp_done"), unit + 1)
                    dve.tensor_reduce(den4, Sv, X, ALU.add)
                    dve.drain()
                    tt(den4, den4, esink, ALU.add)
                    dve.drain()
                    dve.reciprocal(den4, den4)
                    dve.drain()
                    dve.wait_ge(flag("O_full"), unit + 1)
                    tt(attn[:, t, 256 * s:256 * s + 256].rearrange("p (j d) -> p j d", j=QPK),
                       psum[:, 6, 0:256].rearrange("p (j d) -> p j d", j=QPK),
                       over(den4, 2, HD), ALU.mult).then_inc(flag("O_read"), 1)
                    turn_read_wait(dve, "P", t, 2 * s + t)
                    unit += 1
            dve.drain().then_inc(flag("attn_done"), 1)
            turn_read_wait(dve, "css", 0, 0)
            dve.reciprocal(css, css)
            dve.drain()
            for m in range(CT):
                last = stt(featT[:, CT + m, 0:SEQ], cy[:, m, :], pk("conv_g")[:, m:m + 1], css,
                           ALU.mult, ALU.mult)
            last.then_inc(flag("conv_merged"), 1)
            mean_squares("at", AW, EPS)
            inverse_roots("at")
            for t in range(TT):
                last = stt(attn[:, t, :], attn[:, t, :], rs[:, t:t + 1], attn_g, ALU.mult, ALU.mult)
            last.then_inc(flag("attn_normed"), 1)
            for n in range(2):
                for t in range(TT):
                    i = TT * n + t
                    group_wait(dve, "out1", i)
                    read_out(tt(junk[:, 0:512] if i % 2 else junk[:, 512:1024], bank_of("out1", i),
                                gate1[:, 512 * n:512 * (n + 1)], ALU.mult), "out1", i)
                    dve.drain()
                    sl = xres[:, t, 512 * n:512 * (n + 1)]
                    tt(sl, sl, junk[:, 0:512] if i % 2 else junk[:, 512:1024], ALU.add)
            dve.drain().then_inc(flag("x1_ready"), 1)
            mean_squares("n2", D, EPS)
            inverse_roots("n2")
            modulated(A2, scale2, shift2, "h2_ready")

            def top16(src, alt, v, i_):
                n = range(len(src))
                for a in n:
                    dve.max(v[a][:, 0:8], src[a])
                dve.drain()
                for a in n:
                    dve.match_replace(alt[a], v[a][:, 0:8], src[a], LOWEST)
                    dve.max_index(i_[a][:, 0:8], v[a][:, 0:8], src[a])
                dve.drain()
                for a in n:
                    dve.max(v[a][:, 8:16], alt[a])
                dve.drain()
                for a in n:
                    dve.max_index(i_[a][:, 8:16], v[a][:, 8:16], alt[a])
                dve.drain()

            for t in range(TT):
                turn_read_wait(dve, "sc", t, 3)
                a_ = range(HP)
                top16([sc[:, t, a, :] for a in a_], [sc2[:, a, :] for a in a_],
                      [vals[:, a, :] for a in a_], [ids_u[:, a, :] for a in a_])
                dve.tensor_copy(ids_f.rearrange("p h s k -> p (h s) k"), ids_u)
                v4 = vals.rearrange("p (h s) k -> p h s k", s=2)
                c4 = cand.rearrange("p h (a b) -> p h a b", a=TOPK)
                tt(c4, over(v4[:, :, 0, :], 3, TOPK), over(v4[:, :, 1, :], 2, TOPK), ALU.add)
                dve.drain()
                h_ = range(HEADS)
                top16([cand[:, h, :] for h in h_], [cand2[:, h, :] for h in h_],
                      [top[:, h, :] for h in h_], [pos_u[:, h, :] for h in h_])
                pf = pos_u.rearrange("p h k -> p (h k)")
                ts(ab_u[:, 0, :], pf, 4, None, ALU.logical_shift_right)
                ts(ab_u[:, 1, :], pf, TOPK - 1, None, ALU.bitwise_and)
                dve.tensor_copy(rsm[:, 0:8].unsqueeze(2), top[:, :, 0:1])
                dve.drain()
                tt(top, top, over(rsm[:, 0:8], 2, TOPK), ALU.subtract).then_inc(flag("top_shifted"), 1)
                dve.tensor_copy(ab_f, ab_u)
                dve.drain()
                for s in range(2):
                    oh = onehot.rearrange("p (n a) -> p n a", a=TOPK)
                    tt(oh, over(ab_f[:, s, :], 2, TOPK), over(iota16[:, :], 1, P), ALU.is_equal)
                    dve.drain()
                    oh4 = onehot.rearrange("p (h j a) -> p h j a", h=HEADS, a=TOPK)
                    tt(oh4, oh4, over(ids_f[:, :, s, :], 2, TOPK), ALU.mult)
                    dve.drain()
                    dve.tensor_reduce(pick[:, s, :], oh, X, ALU.add)
                    dve.drain()
                stt(idx[:, t, :], pick[:, 0, :], float(KEYS), pick[:, 1, :])
                dve.wait_ge(flag("top_exp"), t + 1)
                dve.tensor_reduce(rsm[:, 8:16], top, X, ALU.add)
                dve.drain()
                dve.reciprocal(rsm[:, 8:16], rsm[:, 8:16])
                dve.drain()
                tt(gates[:, t, :].rearrange("p (h k) -> p h k", h=HEADS), top,
                   over(rsm[:, 8:16], 2, TOPK), ALU.mult)
                dve.drain()
            dve.engine_nop().then_inc(flag("routed"), 1)
            dve.engine_nop().then_inc(row_free, NR)
            dve.engine_nop().then_inc(flag("head_done"), 2)
            lre, lim = pk("lam_re"), pk("lam_im")
            dve.wait_ge(flag("s5_dt_exp"), 1)
            tt(lr, lre, dt_, ALU.mult)
            tt(th, lim, dt_, ALU.mult)
            dve.drain()
            reduce_angle(thk, th, s5k, ta)
            dve.drain()
            reduce_angle(thc, th, s5k, ta, quarter=1).then_inc(flag("s5_args"), 1)
            tt(n2, lre, lre, ALU.mult)
            tt(tb, lim, lim, ALU.mult)
            dve.drain()
            tt(n2, n2, tb, ALU.add)
            dve.drain()
            dve.reciprocal(n2, n2)
            dve.wait_ge(flag("s5_tab"), 1)
            tt(lbr, mag, cosv, ALU.mult)
            tt(lbi, mag, sinv, ALU.mult)
            dve.tensor_copy(s5_mag[:, :], mag)
            dve.tensor_copy(s5_th[:, :], thk)
            dve.drain()
            ts(lbr, lbr, -1.0, None, ALU.add)
            dve.drain()
            tt(ta, lbr, lre, ALU.mult)
            tt(tb, lbi, lim, ALU.mult)
            tt(ts_, lbi, lre, ALU.mult)
            dve.drain()
            tt(fr, ta, tb, ALU.add)
            dve.drain()
            tt(ta, lbr, lim, ALU.mult)
            dve.drain()
            tt(fi, ts_, ta, ALU.subtract)
            tt(fr, fr, n2, ALU.mult)
            dve.drain()
            tt(fi, fi, n2, ALU.mult)
            dve.memset(bd, 0.0)
            dve.memset(cd, 0.0)
            dve.drain()
            dve.wait_ge(flag("in_bc"), 16)
            bre, bim, cre, cim = (bc_raw[:, s, :, :] for s in range(4))
            frb, fib = over(fr, 2, S5H), over(fi, 2, S5H)
            tt(bb[:, 0, :, :], bre, frb, ALU.mult)
            tt(bb[:, 1, :, :], bim, fib, ALU.mult)
            tt(bb[:, 2, :, :], bim, frb, ALU.mult)
            tt(bb[:, 3, :, :], bre, fib, ALU.mult)
            dve.drain()
            bd4 = bd.rearrange("p s (i g h) -> p s i g h", i=SI, g=2)
            cd4 = cd.rearrange("p s i (g h) -> p s i g h", g=2)
            for g in range(2):
                r = slice(64 * g, 64 * g + 64)
                tt(bd4[r, 0, :, g, :], bb[r, 0, :, :], bb[r, 1, :, :], ALU.subtract)
                tt(bd4[r, 1, :, g, :], bb[r, 2, :, :], bb[r, 3, :, :], ALU.add)
                dve.tensor_copy(cd4[r, 0, :, g, :], cre[r, :, :])
                ts(cd4[r, 1, :, g, :], cim[r, :, :], -1.0)
            dve.drain().then_inc(flag("bd_ready"), 1)

            def centered(dst, src, n, mean, name):
                for d, s_, m_ in zip(dst, src, mean):
                    dve.tensor_reduce(m_, s_, X, ALU.add)
                dve.drain()
                for m_ in mean:
                    ts(m_, m_, -1.0 / n)
                dve.drain()
                for d, s_, m_ in zip(dst, src, mean):
                    ts(d, s_, m_, None, ALU.add)
                dve.drain().then_inc(flag(name), 1)

            def two(t3):
                return [t3[:, t, :] for t in range(TT)]

            dve.wait_ge(flag("in_ln0"), 48)
            centered([xmeta], [xmeta], D, [mrs], "meta_centered")
            mean_squares("me", D, LN_EPS, mss, mms, 1)
            inverse_roots("me", msd, mrs)
            stt(xmeta, xmeta, mrs, ln0_g[0:META, :], ALU.mult, ALU.mult)
            dve.drain()
            tt(xmeta, xmeta, ln0_b[0:META, :], ALU.add).then_inc(flag("meta_ready"), 1)

            for t in range(TT):
                dve.memset(acc[:, 0, :], 0.0)
                dve.drain()
                with dve.Fori(0, HEADS // 2) as pair:
                    for par in range(2):
                        for k in range(TOPK):
                            at = 32 * par + k
                            s = at % NR
                            dve.wait_ge(row_full[s], pair * (64 // NR * 16)
                                        + (t * (256 // NR) + at // NR + 1) * 16)
                            dve.tensor_tensor_reduce(rows[:, s, :], rows[:, s, :], hbuf[:, t, :], 1.0,
                                                     0.0, ALU.mult, ALU.add,
                                                     dots[:, k:k + 1]).then_inc(row_free, 1)
                        dve.drain().then_inc(flag("dots_ready"), 1)
                        dve.wait_ge(flag("gel_ready"), pair * 2 + (t * HEADS + par + 1))
                        tt(wgt[:, :], gates[:, t, bass.ds(pair * 32 + par * TOPK, TOPK)], gel[:, :],
                           ALU.mult)
                        dve.drain()
                        for k in range(TOPK):
                            at = 32 * par + TOPK + k
                            s = at % NR
                            dve.wait_ge(row_full[s], pair * (64 // NR * 16)
                                        + (t * (256 // NR) + at // NR + 1) * 16)
                            stt(acc[:, (k + 1) % 2, :], rows[:, s, :], wgt[:, k:k + 1],
                                acc[:, k % 2, :]).then_inc(row_free, 1)
                            dve.drain()
                        dve.engine_nop().then_inc(flag("head_done"), 1)
                tt(acc[:, 1, :], acc[:, 0, :], gate2, ALU.mult)
                dve.drain()
                tt(xres[:, t, :], xres[:, t, :], acc[:, 1, :], ALU.add)
                dve.drain()

            def layer_norm(src, dst, g, b, name, ready=None):
                centered(two(dst), two(src), D, [rs[:, t:t + 1] for t in range(TT)], name + "_centered")
                mean_squares(name, D, LN_EPS)
                inverse_roots(name)
                for t in range(TT):
                    stt(dst[:, t, :], dst[:, t, :], rs[:, t:t + 1], g, ALU.mult, ALU.mult)
                    dve.drain()
                    last = tt(dst[:, t, :], dst[:, t, :], b, ALU.add)
                    if ready and t == TT - 1:
                        last.then_inc(flag(ready), 1)
                return last

            layer_norm(xres, hbuf, ln0_g, ln0_b, "l0", ready="h0_ready")
            dve.memset(qk_in[:, :, 0:3], 0.0)

            def phases(q):
                if q == 0:
                    turn_read_wait(dve, "h0", TT - 1, 1)
                    dve.drain()
                for i in range(4):
                    ts(s5t[2][:, i, :], iota_t[:, :], s5_th[:, 4 * q + i:4 * q + i + 1])
                dve.drain()
                reduce_angle(s5t[4], s5t[2], s5t_i, s5t[5])
                dve.drain()
                reduce_angle(s5t[5], s5t[2], s5t_i, s5t[0], quarter=1).then_inc(flag("ph_ready"), 1)

            def s5_quad(q):
                dve.wait_ge(flag("s5_sin"), q + 1)
                dve.wait_ge(flag("bu_read"), 8 * q + 8)
                cos, sin = s5t[0], s5t[1]
                a, b = s5t[2], s5t[3]

                def turn(re, im, sign):
                    o1, o2 = (ALU.add, ALU.subtract) if sign < 0 else (ALU.subtract, ALU.add)
                    tt(a, cos, re, ALU.mult)
                    tt(b, sin, im, ALU.mult)
                    dve.drain()
                    tt(s5t[4], a, b, o1)
                    dve.drain()
                    tt(a, cos, im, ALU.mult)
                    tt(b, sin, re, ALU.mult)
                    dve.drain()
                    last = tt(s5t[5], a, b, o2)
                    dve.drain()
                    return last

                turn(s5t[6], s5t[7], -1)
                for i in range(4):
                    r = s5_mag[:, 4 * q + i:4 * q + i + 1].broadcast_to([P, LEN])
                    for c in range(2):
                        dve.tensor_tensor_scan(s5t[6 + c][:, i, :], r, s5t[4 + c][:, i, :], 0.0,
                                               ALU.mult, ALU.add)
                dve.drain()
                turn(s5t[6], s5t[7], 1)
                dve.engine_nop().then_inc(flag("state_ready"), 1)

            def s5_y(q):
                dve.wait_ge(flag("y_full"), q + 1)
                stt(gyT[:, q, :], uT[:, q, META:LEN], pk("s5_d")[:, q:q + 1],
                    psum[:, 6, 0:SEQ]).then_inc(flag("y_read"), 1)

            phases(0)
            s5_quad(0)
            for m in range(4):
                read_wait(dve, "q2", m)
                read_wait(dve, "k2", m)
            w = pk("qk_w").rearrange("p (k m) -> p k m", k=4)
            for m in range(8):
                ts(qkT[:, m, :], qk_in[:, m, 0:LEN], w[:, 0, m:m + 1])
            for k in range(1, 4):
                dve.drain()
                for m in range(8):
                    stt(qkT[:, m, :], qk_in[:, m, k:k + LEN], w[:, k, m:m + 1], qkT[:, m, :])
            dve.drain().then_inc(flag("conv2_y"), 1)
            s5_y(0)
            for q in range(1, 3):
                phases(q)
                s5_quad(q)
                s5_y(q)
            phases(3)
            dve.wait_ge(flag("ln_done"), 1)
            li, f, l1p = (row_a[:, i, :] for i in range(3))
            ra, rM, rN = (row_b[:, i, :] for i in range(3))
            stt(f, f, 0.0, l1p, ALU.min, ALU.subtract)
            dve.drain()
            dve.tensor_tensor_scan(rN, ones[0:MH, 0:1].broadcast_to([MH, LEN]), f, 0.0, ALU.mult, ALU.add)
            dve.drain()
            tt(ra, li, rN, ALU.subtract)
            dve.drain()
            dve.tensor_tensor_scan(rM, ones[0:MH, 0:1].broadcast_to([MH, LEN]), ra, 0.0, ALU.mult, ALU.max)
            dve.drain()
            tt(rN, rN, rM, ALU.add).then_inc(flag("rows_ready"), 1)
            s5_quad(3)
            s5_y(3)

            dve.wait_ge(flag("mbc_full"), 1)
            dve.wait_ge(flag("enm"), 1)
            for b in range(3):
                nr, lo = (META, 0) if b == 0 else (P, (b - 1) * P)
                for h in range(MH):
                    src = psum[0:nr, 6 + h // 2, (h % 2) * SEQ + lo:(h % 2 + 1) * SEQ]
                    last = ts(PT[0:nr, b, h, lo:SEQ], src, -1.0, gcol[0:nr, MH * b + h:MH * b + h + 1],
                              ALU.mult, ALU.add)
            last.then_inc(flag("mbc_read"), 1)
            dve.drain()
            parts = [PT[0:META, 0, :, :], PT[:, 1, :, :], PT[:, 2, :, P:SEQ]]
            for p_ in parts:
                last = ts(p_, p_, 0.0, None, ALU.min)
            last.then_inc(flag("E_args"), 1)
            dve.wait_ge(flag("E_exp"), 1)
            for b in (1, 2):
                sl = PT[:, b, :, (b - 1) * P:b * P]
                tt(sl, sl, over(causal[:, :], 1, MH), ALU.mult)
            dve.drain()
            n = 0
            for b in range(3):
                nr, lo = (META, 0) if b == 0 else (P, (b - 1) * P)
                for hh in range(2):
                    dve.wait_ge(flag("st_full"), n + 1)
                    src = psum[0:nr, 6 + n % 2, :].rearrange("p (h n) -> p h n", h=2)[:, :, lo:SEQ]
                    dst = PT[0:nr, b, 2 * hh:2 * hh + 2, lo:SEQ]
                    stt(dst, src, DK ** -0.5, dst, ALU.mult, ALU.mult).then_inc(flag("st_read"), 1)
                    n += 1
            dve.drain().then_inc(flag("PT_ready"), 1)
            turn_read_wait(dve, "den", 0, 0)
            stt(dens, dens, -1.0, dens, ALU.mult, ALU.max)
            dve.drain()
            tt(dens, dens, enm, ALU.max)
            dve.drain()
            dve.reciprocal(rden, dens)
            dve.drain()
            n = 0
            h4 = hm.rearrange("p t (h e) -> p t h e", h=MH)
            for t in range(TT):
                for hh in range(2):
                    dve.wait_ge(flag("num_full"), n + 1)
                    tt(h4[:, t, 2 * hh:2 * hh + 2, :],
                       psum[:, 6 + n % 2, :].rearrange("p (h e) -> p h e", h=2),
                       over(rden[:, MH * t + 2 * hh:MH * t + 2 * hh + 2], 2, DV),
                       ALU.mult).then_inc(flag("num_read"), 1)
                    n += 1
            dve.drain()
            hf = hm.rearrange("p t (h e) -> p (t h) e", h=MH)
            dve.tensor_reduce(hsum, hf, X, ALU.add)
            dve.drain()
            ts(hsum, hsum, -1.0 / DV)
            dve.drain()
            tt(hf, hf, over(hsum, 2, DV), ALU.add)
            dve.drain()
            sq = PT.rearrange("p b h n -> p (b h n)")[:, 0:2048].rearrange("p (a e) -> p a e", e=DV)
            tt(sq, hf, hf, ALU.mult)
            dve.drain()
            dve.tensor_reduce(hvar, sq, X, ALU.add)
            dve.drain()
            ts(hvar, hvar, 1.0 / DV, LN_EPS, ALU.mult, ALU.add).then_inc(flag("hv_ms"), 1)
            dve.wait_ge(flag("hv_sd"), 1)
            dve.reciprocal(hrs, hrs)
            dve.drain()
            tt(hf, hf, over(hrs, 2, DV), ALU.mult)
            dve.drain()
            dve.wait_ge(flag("in_ln1"), 48)
            dve.wait_ge(flag("gate_sig"), 3)
            tt(hm, hm, over(m_norm, 1, TT), ALU.mult)
            dve.drain()
            tt(hm, hm, otok, ALU.mult).then_inc(flag("hm_ready"), 1)
            dve.wait_ge(flag("glu_read"), 1)
            tt(gs, gs, xres[:, :, :], ALU.mult)
            dve.drain()
            tt(gs, gs, tmp2, ALU.mult)
            dve.drain()
            for n in range(2):
                for t in range(TT):
                    i = TT * n + t
                    sl = slice(512 * n, 512 * (n + 1))
                    group_wait(dve, "mo", i)
                    read_out(tt(gm[:, t, sl], gm[:, t, sl], bank_of("mo", i), ALU.mult), "mo", i)
            dve.drain()
            tt(gs, gs, gm, ALU.add).then_inc(flag("mix_ready"), 1)

            def residual(src, t, sl):
                return stt(xres[:, t, sl], hbuf[:, t, sl], ALPHA, src)

            for n in range(2):
                for t in range(TT):
                    i = TT * n + t
                    group_wait(dve, "wo", i)
                    read_out(residual(bank_of("wo", i), t, slice(512 * n, 512 * (n + 1))), "wo", i)
            dve.drain()
            layer_norm(xres, hbuf, ln1_g, ln1_b, "l1", ready="hb_ready")
            for n in range(8):
                read_wait(dve, "up", 4 * n + 3)
                for m in range(3):
                    read_wait(dve, "up", 4 * n + m)
                sl = ffT[:, 4 * n:4 * n + 4, :]
                tt(sl, sl, sl, ALU.mult).then_inc(flag("ff_ready"), 1)
            dve.wait_ge(flag("down_used"), 8)
            for t in range(TT):
                for half in range(2):
                    residual(psum[:, 4 + 2 * t + half, :], t, slice(512 * half, 512 * (half + 1)))
            dve.wait_ge(flag("in_ln2"), 32)
            dve.drain()
            layer_norm(xres, fin, ln2_g, ln2_b, "l2")
            dve.drain().then_inc(flag("fin_ready"), 2)


def kernel(**inputs):
    import concourse.bacc as _bacc
    from concourse.bass_utils import run_bass_kernel_spmd as _run

    A = {n: np.ascontiguousarray(a) for n, a in inputs.items()}

    def cols(v, n):
        return v.reshape(n, P).T

    def state(a):
        return np.moveaxis(a.reshape((SI, P) + a.shape[2:]), 0, 1)

    b_in, w_in2 = A["b_in_2"].reshape(-1), A["w_in_2"][0]
    given = {
        "c": cols(A["c"].reshape(-1), KD),
        "conv_w": np.moveaxis(A["conv_w"][0].reshape(3, CT, P), 2, 0).reshape(P, -1),
        "conv_g": cols(A["conv_out_g"].reshape(-1), CT),
        "b_uqk": cols(b_in[U0:V0], 12),
        "qk_w": np.moveaxis(A["qk_conv_w_2"][0].reshape(4, 8, P), 2, 0).reshape(P, -1),
        "qk_b": cols(A["qk_conv_b_2"].reshape(-1), 8),
        "lam_re": state(A["s5_lambda_re_2"][0]),
        "lam_im": state(A["s5_lambda_im_2"][0]),
        "s5_d": cols(A["s5_d_2"].reshape(-1), 4),
        "b_up": cols(A["b_up_2"].reshape(-1), FF // P),
    }
    c_re, c_im = (np.swapaxes(A[n][0], 1, 2) for n in ("s5_c_re_2", "s5_c_im_2"))
    host = {
        "pack": np.concatenate([given[n] for n, _ in PACK], axis=1),
        "positions": A["positions"].reshape(TT, P).T,
        "x": A["x"].reshape(SEQ, D),
        "subkeys": np.moveaxis(A["peer_subkeys"][0].reshape(HP, KEYS, P), 2, 0),
        "w_if": np.moveaxis(w_in2[:, IF0:IF0 + 2 * MH].reshape(KD, P, 2 * MH), 1, 0),
        "b_if": b_in[IF0:IF0 + 2 * MH].reshape(2, MH).T,
        "log_dt": np.repeat(A["s5_log_dt_2"].reshape(SI, 2).T, S5P, axis=0),
        "s5_bc": np.stack([state(A["s5_b_re_2"][0]), state(A["s5_b_im_2"][0]), state(c_re),
                           state(c_im)], axis=1),
        "meta_tokens_2": A["meta_tokens_2"],
    }
    for n in ("ada_w", "w_in", "w_out", "peer_wq", "peer_u", "peer_v", "w_in_2", "s5_w_glu_2",
              "m_w_out_2", "w_o_2", "w_up_2", "w_down_2"):
        host[n] = A[n][0]
    for n in ("ada_b", "norm1_g", "norm2_g", "q_norm_g", "k_norm_g", "sinks", "attn_out_g", "b_in_2",
              "m_norm_g_2", "ln0_g_2", "ln0_b_2", "ln1_g_2", "ln1_b_2", "ln2_g_2", "ln2_b_2"):
        host[n] = A[n].reshape(-1)

    nc = _bacc.Bacc("TRN2", target_bir_lowering=False, num_devices=1)
    arrays, T = {}, {}
    for n, a in host.items():
        a = np.ascontiguousarray(a)
        arrays[f"in_{n}_dram"] = a
        T[n] = nc.dram_tensor(f"in_{n}_dram", a.shape, mybir.dt.from_np(a.dtype),
                              kind="ExternalInput").ap()
    out = nc.dram_tensor("out_0_dram", (SEQ, D), F32, kind="ExternalOutput").ap()
    build(nc, T, out)
    r = _run(nc, [arrays], core_ids=[0])
    return r.results[0]["out_0_dram"].reshape(1, SEQ, D)
```

```python
from contextlib import ExitStack
import math

import numpy as np

import concourse.bass as bass
from concourse import mybir

ALU = mybir.AluOpType
ACT = mybir.ActivationFunctionType
F32 = mybir.dt.float32
U32 = mybir.dt.uint32
I32 = mybir.dt.int32
X = mybir.AxisListType.X

P = 128
D = 1024
KD = D // P
SEQ = 256
TT = SEQ // P
META = 16
LEN = META + SEQ
HD = 64
NQ, NKV = 8, 2
QPK = NQ // NKV
AW = NQ * HD
QKW = (NQ + NKV) * HD
CW = D - AW
CT = CW // P
THETA = 10000.0
EPS = 1e-6
LN_EPS = 1e-5
NEG = -1e30
HEADS, KEYS, TOPK = 8, 128, 16
EXPERTS = KEYS * KEYS
HP = 2 * HEADS
S5W, S5G, S5H, S5P = 512, 32, 16, 64
SI = S5G * S5P // P
MH, DK, DV = 4, 128, 256
FF = 4 * D
ALPHA = 2.0 ** 0.25
LOWEST = -3.0e38

TWO_PI = 2.0 * math.pi
C1 = 6.28125
C2 = float(np.float32(np.round((TWO_PI - C1) * 2.0 ** 22) / 2.0 ** 22))
C3 = TWO_PI - C1 - C2
PI_IN = 3.1415925

RING = 3
CHUNK = 4096
USES = 64 // 8
GW = 12
STEPS = 8
NR = 8
ACC = 4

PACK = [("c", KD), ("conv_w", 3 * CT), ("conv_g", CT), ("b_uqk", 12), ("qk_w", 32), ("qk_b", 8),
        ("lam_re", SI), ("lam_im", SI), ("s5_d", 4), ("b_up", FF // P)]
PACK_AT, PACK_W = {}, 0
for _name, _w in PACK:
    PACK_AT[_name] = (PACK_W, PACK_W + _w)
    PACK_W += _w

U0, Q0, K0, V0, O0, IF0, GS0, GM0 = 0, 512, 1024, 1536, 2560, 3584, 3592, 4616


def plan():
    chunks, groups = [], []

    def add(name, w, c, n, k0=0, kt=KD, gs=()):
        chunks.append((name, w, k0, kt, c, n))
        groups.append(list(gs))

    def ada(lo, hi):
        for i in range(lo, hi):
            add("ada", "ada_w", 512 * i, 512, gs=[("ada", i)])

    ada(0, 4)
    add("in1", "w_in", 0, 512, gs=[("q1", t) for t in range(TT)])
    add("in1", "w_in", 512, 256, gs=[("kv1", t) for t in range(TT)])
    for j, nm in enumerate(("cb", "cc", "cu")):
        add("in1", "w_in", 768 + 512 * j, 512, gs=[(nm, m) for m in range(4)])
    ada(4, 12)
    for n in range(2):
        add("out1", "w_out", 512 * n, 512, gs=[("out1", TT * n + t) for t in range(TT)])
    for n in range(4):
        add("wq", "peer_wq", 512 * n, 512, gs=[("wq", 4 * n + m) for m in range(4)])
    for nm, c in (("u", U0), ("q2", Q0), ("k2", K0)):
        add("in2", "w_in_2", c, 512, gs=[(nm, m) for m in range(4)])
    for n in range(2):
        add("in2", "w_in_2", V0 + 512 * n, 512, gs=[("v2", 3 * n + t) for t in range(3)])
    for nm, c in (("o2", O0), ("gs", GS0), ("gm", GM0)):
        for n in range(2):
            add("in2", "w_in_2", c + 512 * n, 512, gs=[(nm, TT * n + t) for t in range(TT)])
    for n in range(2):
        add("glu", "s5_w_glu_2", D * n, D, kt=4, gs=[("glu", 4 * n + i) for i in range(4)])
    for n in range(2):
        add("mo", "m_w_out_2", 512 * n, 512, gs=[("mo", TT * n + t) for t in range(TT)])
    for n in range(2):
        add("wo", "w_o_2", 512 * n, 512, gs=[("wo", TT * n + t) for t in range(TT)])
    for n in range(8):
        add("up", "w_up_2", 512 * n, 512, gs=[("up", 4 * n + m) for m in range(4)])
    for n in range(8):
        add("down", "w_down_2", 0, D, k0=4 * n, kt=4, gs=[])
    return chunks, groups


CHUNKS, GROUPS = plan()
LAST_WQ = max(i for i, c in enumerate(CHUNKS) if c[0] == "wq")
GROUP_NO = {}
for _gs in GROUPS:
    for _g in _gs:
        GROUP_NO[_g] = len(GROUP_NO)


def build(nc, T, out):
    with ExitStack() as ctx:
        def sb(name, shape, dt=F32):
            return ctx.enter_context(nc.sbuf_tensor(name, shape, dt))

        def sem(name):
            return ctx.enter_context(nc.semaphore(name))

        def over(ap, axis, n):
            ap = ap.unsqueeze(axis)
            shape = list(ap.shape)
            shape[axis] = n
            return ap.broadcast_to(shape)

        ring = sb("weight_ring", [P, RING, CHUNK])
        xres = sb("xres", [P, TT, D])
        featT = sb("featT", [P, KD, LEN])
        hbuf = sb("hbuf", [P, TT, D])
        modr = sb("modr", [P, 6 * D])
        wk = sb("work", [P, 8704])
        G = sb("gathered", [P, GW * D])
        vec = sb("vectors", [P, 4 * D])
        pack = sb("pack", [P, PACK_W])
        ident = sb("ident", [P, P])
        ones = sb("ones", [P, P])
        mask = sb("mask", [P, 2, P])
        causal = sb("causal", [P, P])
        iota_t = sb("iota_t", [P, LEN])
        iota16 = sb("iota16", [P, TOPK])
        zeros = sb("zeros", [P, P])
        rope_t = sb("rope_t", [P, 4, TT, HD // 2])
        inv_freq = sb("inv_freq", [P, HD // 2])
        uT = sb("uT", [P, 4, LEN])
        next_idx = sb("next_idx", [P, 2 * TOPK], U32)
        next_gate = sb("next_gate", [P, 2 * TOPK])
        bn = sb("bn", [P, TT, 2, 6])
        mv = sb("mean_var", [P, TT + 1, 2])
        stage = sb("stage", [P, 2, TOPK], U32)
        dots = sb("dots", [P, TOPK])
        gel = sb("gel", [P, TOPK])
        wgt = sb("wgt", [P, TOPK])
        st = sb("stats", [P, 96])
        pos_i = sb("pos_i", [P, TT], I32)
        w_if = sb("w_if", [P, KD, 2 * MH])
        b_if = sb("b_if", [MH, 2])
        s5_dt = sb("s5_log_dt", [P, SI])
        s5_mag = sb("s5_mag", [P, SI])
        s5_th = sb("s5_theta", [P, SI])
        col2 = sb("mlstm_cols", [P, 68])
        psum = ctx.enter_context(nc.psum_tensor("psum", [P, 8, 512], F32))

        def pk(name):
            a, b = PACK_AT[name]
            return pack[:, a:b]

        crep = G[:, 0:1024].rearrange("p (k m) -> p k m", k=KD)
        qkv = G[:, 1024:2560].rearrange("p (t n) -> p t n", t=TT)
        qkr = G[:, 2560:3840].rearrange("p (t n) -> p t n", t=TT)
        S = G[:, 3840:4864].rearrange("p (j k) -> p j k", j=QPK)
        pT = G[:, 4864:5888].rearrange("p (b j q) -> p b j q", b=2, j=QPK)
        qT = G[:, 5888:6912].rearrange("p (t j q) -> p t j q", t=TT, j=QPK)
        kT = G[:, 6912:7168]
        attn = G[:, 7168:8192].rearrange("p (t n) -> p t n", t=TT)
        cbT = G[:, 8192:9216].rearrange("p (m n) -> p m n", m=CT)
        hp = G[:, 9216:10248].rearrange("p (m n) -> p m n", m=CT)
        cy = G[:, 10248:11272].rearrange("p (m n) -> p m n", m=CT)
        junk = wk[:, 0:1280]
        junk_a = wk[:, 1280:2304]
        rp = wk[:, 2304:3584].rearrange("p (n a b) -> p n a b", n=2, b=HD // 2)
        A1, A2, attn_g = vec[:, 0:D], vec[:, D:2 * D], vec[:, 2 * D:2 * D + AW]
        qg, kg = vec[:, 2560:2624], vec[:, 2624:2688]
        sinks = vec[:, 2688:2696]
        shift1, scale1, gate1, shift2, scale2, gate2 = (modr[:, D * i:D * (i + 1)] for i in range(6))
        qpT = wk[:, 0:4096].rearrange("p (a t) -> p a t", a=HP)
        skT = wk[:, 4096:6144].rearrange("p (a k) -> p a k", a=HP)
        rt = wk[:, 6144:8704]
        scs = rt[:, 0:512].rearrange("p (a k) -> p a k", a=4)
        cand = rt[:, 512:1024].rearrange("p (h n) -> p h n", h=2)
        onehot = rt[:, 1024:1536]
        vals = rt[:, 1536:1600].rearrange("p (a k) -> p a k", a=4)
        ids_u = rt[:, 1600:1664].bitcast(U32).rearrange("p (a k) -> p a k", a=4)
        ids_f = rt[:, 1664:1728].rearrange("p (h s k) -> p h s k", s=2, k=TOPK)
        top = rt[:, 1728:1760].rearrange("p (h k) -> p h k", h=2)
        pos_u = rt[:, 1760:1792].bitcast(U32).rearrange("p (h k) -> p h k", h=2)
        ab_u = rt[:, 1792:1856].bitcast(U32).rearrange("p (s n) -> p s n", s=2)
        ab_f = rt[:, 1856:1920].rearrange("p (s n) -> p s n", s=2)
        pick = rt[:, 1920:1984].rearrange("p (s n) -> p s n", s=2)
        rsm = rt[:, 1984:1988]
        sc = G[:, NR * D:NR * D + STEPS * 512]
        rows = G[:, 0:NR * D].rearrange("p (s n) -> p s n", s=NR)
        diag = modr[:, 0:D].rearrange("p (s n) -> p s n", s=8)
        peer_out = modr[:, D:2 * D]
        ln0_g, ln0_b = wk[:, 2048:3072], wk[:, 3072:4096]
        xmeta = wk[0:META, 4096:5120]
        bc_raw = wk[:, 5120:6144].rearrange("p (s i h) -> p s i h", s=4, i=SI)
        bb = wk[:, 6144:7168].rearrange("p (s i h) -> p s i h", s=4, i=SI)
        bd = wk[:, 7168:8192].rearrange("p (s n) -> p s n", s=2)
        s5c = wk[:, 8192:8448].rearrange("p (s i) -> p s i", s=16)
        s5k = wk[:, 8448:8464].bitcast(I32)
        turn_b = [mask[:, :, :].rearrange("p b (i n) -> p (b i) n", n=16),
                  rope_t[:, :, :, :].rearrange("p a t (i n) -> p (a t i) n", n=16)]
        turn_ang_a = wk[:, 2176:2720].rearrange("p (s i n) -> p s i n", s=2, i=SI)
        turn_ang_b = wk[:, 2720:3232].rearrange("p (s i n) -> p s i n", s=2, i=SI)
        turn_k = wk[:, 3232:3504].bitcast(I32).rearrange("p (i n) -> p i n", i=SI)
        turn_kf = wk[:, 3504:3776].rearrange("p (i n) -> p i n", i=SI)
        turn_raw = wk[:, 3776:4048].rearrange("p (i n) -> p i n", i=SI)
        turn_a = modr[:, 5120:5664].rearrange("p (s i n) -> p s i n", s=2, i=SI)
        bdT = modr[:, 3072:4096].rearrange("p (s q n) -> p s q n", s=2, q=4)
        cd = modr[:, 4096:5120].rearrange("p (s i n) -> p s i n", s=2, i=SI)
        qk_in = modr[:, 0:2200].rearrange("p (m n) -> p m n", m=8)
        gyT = modr[:, 0:1024].rearrange("p (m n) -> p m n", m=4)
        row_a = modr[0:MH, 2200:3016].rearrange("p (s n) -> p s n", s=3)
        vtok = G[:, 0:3072].rearrange("p (t n) -> p t n", t=3)
        otok = G[:, 3072:5120].rearrange("p (t n) -> p t n", t=TT)
        gs = G[:, 5120:7168].rearrange("p (t n) -> p t n", t=TT)
        gm = G[:, 7168:9216].rearrange("p (t n) -> p t n", t=TT)
        qkT = G[:, 9216:11392].rearrange("p (m n) -> p m n", m=8)
        row_b = G[0:MH, 11392:12208].rearrange("p (s n) -> p s n", s=3)
        QW = 4 * LEN
        s5t = [wk[:, QW * i:QW * (i + 1)].rearrange("p (i n) -> p i n", i=4) for i in range(8)]
        s5t_i = wk[:, QW * 3:QW * 4].bitcast(I32).rearrange("p (i n) -> p i n", i=4)
        PT = wk[:, 0:3072].rearrange("p (b h n) -> p b h n", b=3, h=MH)
        hm = wk[:, 3072:5120].rearrange("p (t n) -> p t n", t=TT)
        tmp2 = wk[:, 5120:7168].rearrange("p (t n) -> p t n", t=TT)
        ffT = wk[:, 0:8192].rearrange("p (k n) -> p k n", k=FF // P)
        m_norm, ln1_g, ln1_b = vec[:, 0:D], vec[:, D:2 * D], vec[:, 2 * D:3 * D]
        ln2_g, ln2_b = modr[:, 0:D], modr[:, D:2 * D]
        fin = G[:, 0:2048].rearrange("p (t n) -> p t n", t=TT)

        ring_full = [sem(f"ring_full{i}") for i in range(RING)]
        chunk_used = sem("chunk_used")
        bank_full = [sem(f"bank_full{i}") for i in range(ACC)]
        bank_free = [sem(f"bank_free{i}") for i in range(ACC)]
        turned = sem("turned")
        turn_read = sem("turn_read")
        row_full = [sem(f"row_full{i}") for i in range(NR)]
        slot_free = [sem(f"slot_free{i}") for i in range(NR)]
        S_ = {}

        def flag(name):
            if name not in S_:
                S_[name] = sem(name)
            return S_[name]

        def group_wait(eng, name, i):
            g = GROUP_NO[(name, i)]
            eng.wait_ge(bank_full[g % ACC], g // ACC + 1)

        def bank_of(name, i):
            return psum[:, GROUP_NO[(name, i)] % ACC, :]

        def read_out(ins, name, i):
            ins.then_inc(bank_free[GROUP_NO[(name, i)] % ACC], 1)

        block = ctx.enter_context(nc.Block())
        ss, ms, sd, rs = (st[:, 2 * i:2 * i + 2] for i in range(4))
        mss, mms, msd, mrs = (st[0:META, 8 + i:9 + i] for i in range(4))
        qss, qrs = st[:, 12:32], st[:, 32:52]
        rmax, esink, den4 = st[:, 52:56], st[:, 56:60], st[:, 60:64]
        c_act = st[:, 64:72]
        eps_c, ln_eps_c = st[:, 72:73], st[:, 73:74]
        gcol = col2[:, 0:20]
        enm, dens, rden = col2[:, 20:28], col2[:, 28:36], col2[:, 36:44]
        hsum, hvar, hrs = col2[:, 44:52], col2[:, 52:60], col2[:, 60:68]
        css = wk[:, 3584:3840]
        dt_, lr, th, thk, thc, mag, cosv, sinv, lbr, lbi, fr, fi, n2, ta, tb, ts_ = (
            s5c[:, i, :] for i in range(16))

        turns = []
        turns += [("h1", t, q) for t in range(TT) for q in range(2)]
        turns += [("qT", t, 0) for t in range(TT)] + [("kT", 0, 0), ("css", 0, 0)]
        for t in range(TT):
            for s in range(NKV):
                turns += [("P", t, 2 * s + b) for b in range(t + 1)]
        turns += [("m", t, 0) for t in range(TT)]
        turns += [("h2", t, q) for t in range(TT) for q in range(2)]
        turns += [("sc", t, b) for b in range(STEPS // TT) for t in range(TT)]
        turns += [("meta", 0, q) for q in range(2)]
        turns += [("h0", t, q) for t in range(TT) for q in range(2)]
        turns += [("if", c, 0) for c in range(2)] + [("bd", c, 0) for c in range(2)]
        turns += [("ga", 0, 0), ("den", 0, 0)]
        for nm in ("hm", "mix", "hb"):
            turns += [(nm, t, q) for t in range(TT) for q in range(2)]
        turn_no = {u: n for n, u in enumerate(turns)}

        def turn_bank(*u):
            return psum[:, 4 + turn_no[u] % 2, :]

        def turn_wait(eng, *u):
            eng.wait_ge(turned, turn_no[u] + 1)

        def turn_read_wait(eng, *u):
            eng.wait_ge(turn_read, turn_no[u] + 1)

        def read_wait(eng, name, i):
            g = GROUP_NO[(name, i)]
            eng.wait_ge(bank_free[g % ACC], g // ACC + 1)

        def rowvec(name, lo, hi):
            return T[name][lo:hi].partition_broadcast(P)

        @block.sync
        def _(sp):
            for c, (_, w, k0, kt, col, n) in enumerate(CHUNKS):
                if c >= RING:
                    if GROUPS[c - RING]:
                        group_wait(sp, *GROUPS[c - RING][-1])
                    else:
                        sp.wait_ge(flag("down_used"), c - RING - (len(CHUNKS) - 8) + 1)
                dst = ring[:, c % RING, 0:kt * n].rearrange("p (k n) -> p k n", k=kt)
                src = T[w].rearrange("(k p) n -> p k n", p=P)[:, k0:k0 + kt, col:col + n]
                sp.dma_start(dst, src).then_inc(ring_full[c % RING], 16)
                if c == LAST_WQ + RING:
                    turn_read_wait(sp, "sc", TT - 1, 3)
                    for dst, name in ((ln0_g, "ln0_g_2"), (ln0_b, "ln0_b_2")):
                        sp.dma_start(dst, rowvec(name, 0, D)).then_inc(flag("in_ln0"), 16)
                    sp.dma_start(xmeta, T["meta_tokens_2"]).then_inc(flag("in_ln0"), 16)
                    sp.dma_start(bc_raw, T["s5_bc"]).then_inc(flag("in_bc"), 16)
                    for i, lo in enumerate((V0, O0, GS0, GM0)):
                        sp.dma_start(vec[:, D * i:D * (i + 1)], rowvec("b_in_2", lo, lo + D)).then_inc(
                            flag("in_bias2"), 16)
            for t in range(TT):
                sp.wait_ge(flag("fin_ready"), t + 1)
                sp.dma_start(out[t * P:(t + 1) * P, :], fin[:, t, :]).then_inc(flag("stored"), 16)
            sp.wait_ge(flag("stored"), 16 * TT)

        @block.gpsimd
        def _(pool):
            pool.memset(ident[:, :], 0.0)
            pool.memset(ones[:, :], 1.0)
            pool.memset(zeros[:, :], 0.0)
            pool.memset(mask[:, :, :], 0.0)
            pool.memset(causal[:, :], 1.0)
            pool.iota(iota_t[:, :], [[1, LEN]], base=0, channel_multiplier=0,
                      allow_small_or_imprecise_dtypes=True)
            pool.iota(iota16[:, :], [[1, TOPK]], base=0, channel_multiplier=0,
                      allow_small_or_imprecise_dtypes=True)
            for j in range(HD // 2):
                pool.memset(inv_freq[:, j:j + 1], float(np.float32(THETA) ** np.float32(-2.0 * j / HD)))
            pool.drain()
            pool.affine_select(out=ident[:, :], in_=ident[:, :], compare_op=ALU.not_equal, fill=1.0,
                               base=0, pattern=[[-1, P]], channel_multiplier=1)
            pool.affine_select(out=mask[:, 0, :], in_=mask[:, 0, :], compare_op=ALU.is_gt, fill=NEG,
                               base=0, pattern=[[1, P]], channel_multiplier=-1)
            pool.affine_select(out=mask[:, 1, :], in_=mask[:, 1, :], compare_op=ALU.is_ge, fill=NEG,
                               base=0, pattern=[[-1, P]], channel_multiplier=1)
            pool.affine_select(out=causal[:, :], in_=causal[:, :], compare_op=ALU.is_ge, fill=0.0,
                               base=0, pattern=[[1, P]], channel_multiplier=-1)
            pool.memset(eps_c, EPS)
            pool.memset(ln_eps_c, LN_EPS)
            pool.drain().then_inc(flag("consts"), 1)

            def gather_step(t, pair):
                for par in range(2):
                    for part, tab in enumerate(("peer_u", "peer_v")):
                        for k in range(TOPK):
                            at = 32 * par + TOPK * part + k
                            s = at % NR
                            if part == 0 and k == 0:
                                pool.wait_ge(flag("staged"), pair * 2 + (t * HEADS + par + 1))
                            pool.wait_ge(slot_free[s], pair * USES + (t * 4 * USES + at // NR + 1))
                            pool.sem_inc(flag("gather_cleared"), 1)
                            pool.indirect_dma_start(
                                rows[:, s, :], None, T[tab],
                                bass.IndirectOffsetOnAxis(ap=stage[:, par, k:k + 1], axis=0),
                            ).then_inc(row_full[s], 16)

            for t in range(TT):
                with pool.Fori(0, 4) as pair:
                    gather_step(t, pair)

            for t in range(3):
                for n in range(2):
                    read_wait(pool, "v2", 3 * n + t)
            pool.wait_ge(flag("in_bias2"), 64)
            pool.tensor_tensor(vtok[0:META, 0, :], vtok[0:META, 0, :], vec[0:META, 0:D], ALU.add)
            pool.tensor_tensor(vtok[:, 1:3, :], vtok[:, 1:3, :], over(vec[:, 0:D], 1, TT),
                               ALU.add).then_inc(flag("v_ready"), 1)
            for i, (nm, dst) in enumerate((("o2", otok), ("gs", gs), ("gm", gm))):
                for j in range(2 * TT):
                    read_wait(pool, nm, j)
                pool.tensor_tensor(dst, dst, over(vec[:, D * (i + 1):D * (i + 2)], 1, TT),
                                   ALU.add).then_inc(flag("gate_biased"), 1)
            pool.drain()
            pool.dma_start(m_norm, rowvec("m_norm_g_2", 0, D)).then_inc(flag("in_ln1"), 16)
            pool.dma_start(ln1_g, rowvec("ln1_g_2", 0, D)).then_inc(flag("in_ln1"), 16)
            pool.dma_start(ln1_b, rowvec("ln1_b_2", 0, D)).then_inc(flag("in_ln1"), 16)
            pool.wait_ge(flag("glu_read"), 1)
            pool.dma_start(ln2_g, rowvec("ln2_g_2", 0, D)).then_inc(flag("in_ln2"), 16)
            pool.dma_start(ln2_b, rowvec("ln2_b_2", 0, D)).then_inc(flag("in_ln2"), 16)

        @block.tensor
        def _(pe):
            used = [0]

            def begin_turn(*u):
                if turn_no[u] >= 2:
                    pe.wait_ge(turn_read, turn_no[u] - 1)
                return turn_bank(*u)

            def transpose_tile(name, t, src, rows_=P, ready=None):
                for q in range(2):
                    bank = begin_turn(name, t, q)
                    if ready and q == 0:
                        pe.wait_ge(*ready)
                    for j in range(4):
                        k = 4 * q + j
                        last = pe.transpose(bank[:, j * rows_:(j + 1) * rows_],
                                            src[:, k * P:(k + 1) * P], ident[0:rows_, 0:rows_])
                    last.then_inc(turned, 1)

            def next_chunk():
                c = used[0]
                used[0] += 1
                pe.wait_ge(ring_full[c % RING], 16 * (c // RING + 1))
                kt, n = CHUNKS[c][3], CHUNKS[c][5]
                return ring[:, c % RING, 0:kt * n].rearrange("p (k n) -> p k n", k=kt)

            def group(name, i, lhs, rhs, kt, m, n):
                g = GROUP_NO[(name, i)]
                if g >= ACC:
                    pe.wait_ge(bank_free[g % ACC], g // ACC)
                for k in range(kt):
                    last = pe.matmul(psum[0:m, g % ACC, 0:n], lhs(k), rhs(k),
                                     start=(k == 0), stop=(k == kt - 1))
                last.then_inc(bank_full[g % ACC], 1)

            def by_token(name, i, t, w, src, n=512, col=0, kt=KD, base=0, m=P):
                group(name, i, lambda k: src[:, k, base + t * P:base + t * P + m],
                      lambda k: w[:, k, col:col + n], kt, m, n)

            def by_feature(name, i, w, m, lo, hi):
                group(name, i, lambda k: w[:, k, m * P:(m + 1) * P], lambda k: featT[:, k, lo:hi],
                      KD, P, hi - lo)

            def ada(i):
                w = next_chunk()
                group("ada", i, lambda k: crep[:, k, :], lambda k: w[:, k, :], KD, P, 512)

            pe.wait_ge(flag("crep_ready"), 1)
            pe.wait_ge(flag("consts"), 1)
            for i in range(4):
                ada(i)
            for t in range(TT):
                transpose_tile("h1", t, hbuf[:, t, :], ready=(flag("h1_ready"), t + 1))
            turn_read_wait(pe, "h1", TT - 1, 1)
            w = next_chunk()
            for t in range(TT):
                by_token("q1", t, t, w, featT)
            w = next_chunk()
            for t in range(TT):
                by_token("kv1", t, t, w, featT, n=256)
            for nm in ("cb", "cc", "cu"):
                w = next_chunk()
                for m in range(4):
                    by_feature(nm, m, w, m, 0, SEQ)
            ada(4)
            ada(5)
            pe.wait_ge(flag("rope_done"), 1)
            for t in range(TT):
                bank = begin_turn("qT", t, 0)
                for j in range(QPK):
                    last = pe.transpose(bank[:, j * P:(j + 1) * P],
                                        qkr[:, t, j * P:(j + 1) * P], ident[:, :])
                last.then_inc(turned, 1)
            bank = begin_turn("kT", 0, 0)
            for t in range(TT):
                last = pe.transpose(bank[:, t * P:(t + 1) * P], qkr[:, t, AW:QKW], ident[:, :])
            last.then_inc(turned, 1)
            bank = begin_turn("css", 0, 0)
            pe.wait_ge(flag("conv_sq"), 1)
            for m in range(CT):
                last = pe.matmul(bank[:, 0:SEQ], ones[:, :], hp[:, m, 0:SEQ],
                                 start=(m == 0), stop=(m == CT - 1))
            last.then_inc(turned, 1)
            turn_read_wait(pe, "kT", 0, 0)
            unit = 0
            extra = [6, 7, 8, 9, 10, 11]
            for t in range(TT):
                nk = P * (t + 1)
                for s in range(NKV):
                    if unit:
                        pe.wait_ge(flag("O_read"), unit)
                    for j in range(QPK):
                        last = pe.matmul(psum[:, 6 + j // 2, (j % 2) * 256:(j % 2) * 256 + nk],
                                         qT[64 * s:64 * s + 64, t, j, :], kT[64 * s:64 * s + 64, 0:nk],
                                         start=True, stop=True)
                    last.then_inc(flag("S_full"), 1)
                    for _ in range(2 if unit < 2 else 1):
                        ada(extra.pop(0))
                    pe.wait_ge(flag("exp_done"), unit + 1)
                    for b in range(t + 1):
                        bank = begin_turn("P", t, 2 * s + b)
                        for j in range(QPK):
                            last = pe.transpose(bank[:, j * P:(j + 1) * P],
                                                S[:, j, b * P:(b + 1) * P], ident[:, :])
                        last.then_inc(turned, 1)
                    turn_read_wait(pe, "P", t, 2 * s + t)
                    for j in range(QPK):
                        for b in range(t + 1):
                            last = pe.matmul(psum[:, 6, j * HD:(j + 1) * HD], pT[:, b, j, :],
                                             qkv[:, b, QKW + s * HD:QKW + (s + 1) * HD],
                                             start=(b == 0), stop=(b == t))
                    last.then_inc(flag("O_full"), 1)
                    unit += 1
            pe.wait_ge(flag("attn_normed"), 1)
            for t in range(TT):
                bank = begin_turn("m", t, 0)
                for j in range(4):
                    last = pe.transpose(bank[:, j * P:(j + 1) * P], attn[:, t, j * P:(j + 1) * P],
                                        ident[:, :])
                last.then_inc(turned, 1)
            turn_read_wait(pe, "m", TT - 1, 0)
            pe.wait_ge(flag("conv_merged"), 1)
            for n in range(2):
                w = next_chunk()
                for t in range(TT):
                    by_token("out1", TT * n + t, t, w, featT)
            for t in range(TT):
                transpose_tile("h2", t, hbuf[:, t, :], ready=(flag("h2_ready"), t + 1))
            turn_read_wait(pe, "h2", TT - 1, 1)
            pe.wait_ge(flag("in_sk"), 16)

            def score_step(b):
                for a in range(4 * b, 4 * b + 4):
                    read_wait(pe, "wq", a)
                for t in range(TT):
                    bank = begin_turn("sc", t, b)
                    for j in range(4):
                        last = pe.matmul(bank[:, j * KEYS:(j + 1) * KEYS],
                                         qpT[:, 4 * b + j, t * P:(t + 1) * P], skT[:, 4 * b + j, :],
                                         start=True, stop=True)
                    last.then_inc(turned, 1)

            for n in range(4):
                w = next_chunk()
                for m in range(4):
                    by_feature("wq", 4 * n + m, w, m, 0, SEQ)
                    if n and m == 0:
                        score_step(n - 1)
            score_step(3)

            def sum_step(t, pair):
                for par in range(2):
                    for k in range(TOPK):
                        at = 32 * par + TOPK + k
                        s = at % NR
                        pe.wait_ge(row_full[s], pair * (16 * USES) + (t * 4 * USES + at // NR + 1) * 16)
                        pe.wait_ge(flag("diag_full"), pair * 32 + (t * 128 + 16 * par + k + 1))
                        for half in range(2):
                            mm = pe.matmul(psum[:, 6 + half, :], diag[:, k % 8, :],
                                           rows[:, s, 512 * half:512 * (half + 1)],
                                           start=False, stop=False)
                            mm.then_inc((flag("diag_free"), slot_free[s])[half], 1)

            def sum_zero(t, start):
                for half in range(2):
                    mm = pe.matmul(psum[:, 6 + half, :], zeros[:, :],
                                   hbuf[:, t, 512 * half:512 * (half + 1)], start=start, stop=not start)
                return mm

            pe.sem_inc(flag("diag_free"), 7)
            for t in range(TT):
                if t:
                    pe.wait_ge(flag("peer_read"), t)
                sum_zero(t, True)
                with pe.Fori(0, 4) as pair:
                    sum_step(t, pair)
                sum_zero(t, False).then_inc(flag("peer_summed"), 1)
            transpose_tile("meta", 0, xmeta, rows_=META, ready=(flag("meta_ready"), 1))
            for t in range(TT):
                transpose_tile("h0", t, hbuf[:, t, :], ready=(flag("h0_ready"), t + 1))
            turn_read_wait(pe, "h0", TT - 1, 1)
            for nm in ("u", "q2", "k2"):
                w = next_chunk()
                for m in range(4):
                    by_feature(nm, m, w, m, 0, LEN)
            pe.wait_ge(flag("in_if"), 32)
            for c in range(2):
                bank = begin_turn("if", c, 0)
                for k in range(KD):
                    last = pe.matmul(bank[0:MH, 0:LEN], w_if[:, k, MH * c:MH * (c + 1)], featT[:, k, :],
                                     start=(k == 0), stop=(k == KD - 1))
                last.then_inc(turned, 1)

            pe.wait_ge(flag("bd_ready"), 1)
            for c in range(2):
                bank = begin_turn("bd", c, 0)
                for q in range(4):
                    last = pe.transpose(bank[:, q * P:(q + 1) * P], bd[:, c, q * P:(q + 1) * P],
                                        ident[:, :])
                last.then_inc(turned, 1)

            def s5_in(q):
                read_wait(pe, "u", q)
                turn_read_wait(pe, "bd", 1, 0)
                if q:
                    pe.wait_ge(flag("y_read"), q)
                for i in range(4):
                    for c in range(2):
                        n = 8 * q + 2 * i + c
                        if n >= 2:
                            pe.wait_ge(flag("bu_read"), n - 1)
                        pe.matmul(psum[:, 6 + c, 0:LEN], bdT[32 * i:32 * i + 32, c, q, :],
                                  uT[32 * i:32 * i + 32, q, :], start=True,
                                  stop=True).then_inc(flag("bu_full"), 1)

            def s5_out(q):
                pe.wait_ge(flag("state_ready"), q + 1)
                for i in range(4):
                    for c in range(2):
                        last = pe.matmul(psum[32 * i:32 * i + 32, 6, 0:SEQ], cd[:, c, 4 * q + i, :],
                                         s5t[4 + c][:, i, META:LEN], start=(c == 0), stop=(c == 1))
                last.then_inc(flag("y_full"), 1)

            s5_in(0)
            for n in range(2):
                w = next_chunk()
                by_token("v2", 3 * n, 0, w, featT, m=META)
                for t in range(TT):
                    by_token("v2", 3 * n + 1 + t, t, w, featT, base=META)
            for q, nm in enumerate(("o2", "gs", "gm")):
                s5_out(q)
                s5_in(q + 1)
                for n in range(2):
                    w = next_chunk()
                    for t in range(TT):
                        by_token(nm, TT * n + t, t, w, featT, base=META)
            pe.wait_ge(flag("rows_ready"), 1)
            bank = begin_turn("ga", 0, 0)
            pe.transpose(bank[0:META, 0:MH], row_b[:, 0, 0:META], ident[0:MH, 0:MH])
            for t in range(TT):
                lo = META + t * P
                pe.transpose(bank[:, MH * (1 + t):MH * (2 + t)], row_b[:, 0, lo:lo + P],
                             ident[0:MH, 0:MH])
                last = pe.transpose(bank[:, MH * (3 + t):MH * (4 + t)], row_b[:, 2, lo:lo + P],
                                    ident[0:MH, 0:MH])
            last.then_inc(turned, 1)
            s5_out(3)
            pe.wait_ge(flag("y_read"), 4)
            for h in range(MH):
                last = pe.matmul(psum[:, 6 + h // 2, (h % 2) * SEQ:(h % 2 + 1) * SEQ],
                                 ident[0:MH, h:h + 1].broadcast_to([MH, P]), row_b[:, 1, META:LEN],
                                 start=True, stop=True)
            last.then_inc(flag("mbc_full"), 1)
            pe.wait_ge(flag("conv2_done"), 1)
            n = 0
            for b in range(3):
                nr = META if b == 0 else P
                lo = 0 if b == 0 else META + (b - 1) * P
                for hh in range(2):
                    if n < 2:
                        pe.wait_ge(flag("mbc_read"), 1)
                    else:
                        pe.wait_ge(flag("st_read"), n - 1)
                    for h in (2 * hh, 2 * hh + 1):
                        last = pe.matmul(psum[0:nr, 6 + n % 2, (h % 2) * SEQ:(h % 2 + 1) * SEQ],
                                         qkT[:, MH + h, lo:lo + nr], qkT[:, h, META:LEN],
                                         start=True, stop=True)
                    last.then_inc(flag("st_full"), 1)
                    n += 1
            pe.wait_ge(flag("PT_ready"), 1)
            pe.wait_ge(flag("v_ready"), 1)

            def key_tiles(t):
                return [(b, META if b == 0 else P) for b in range(t + 2)]

            bank = begin_turn("den", 0, 0)
            for t in range(TT):
                for h in range(MH):
                    for b, nr in key_tiles(t):
                        last = pe.matmul(bank[:, MH * t + h:MH * t + h + 1],
                                         PT[0:nr, b, h, t * P:(t + 1) * P], ones[0:nr, 0:1],
                                         start=(b == 0), stop=(b == t + 1))
            last.then_inc(turned, 1)
            n = 0
            for t in range(TT):
                for hh in range(2):
                    if n < 2:
                        pe.wait_ge(flag("st_read"), 6)
                    else:
                        pe.wait_ge(flag("num_read"), n - 1)
                    for h in (2 * hh, 2 * hh + 1):
                        for b, nr in key_tiles(t):
                            last = pe.matmul(psum[:, 6 + n % 2, (h % 2) * DV:(h % 2 + 1) * DV],
                                             PT[0:nr, b, h, t * P:(t + 1) * P],
                                             vtok[0:nr, b, h * DV:(h + 1) * DV],
                                             start=(b == 0), stop=(b == t + 1))
                    last.then_inc(flag("num_full"), 1)
                    n += 1
            pe.wait_ge(flag("gy_ready"), 4)
            for z in range(2):
                w = next_chunk()
                for n in range(2):
                    for t in range(TT):
                        by_token("glu", 4 * z + 2 * n + t, t, w, gyT, col=512 * n, kt=4)
            for nm, ready, prod in (("hm", "hm_ready", "mo"), ("mix", "mix_ready", "wo")):
                src = hm if nm == "hm" else gs
                for t in range(TT):
                    transpose_tile(nm, t, src[:, t, :], ready=(flag(ready), 1))
                turn_read_wait(pe, nm, TT - 1, 1)
                for n in range(2):
                    w = next_chunk()
                    for t in range(TT):
                        by_token(prod, TT * n + t, t, w, featT)
            for t in range(TT):
                transpose_tile("hb", t, hbuf[:, t, :], ready=(flag("hb_ready"), t + 1))
            turn_read_wait(pe, "hb", TT - 1, 1)
            for n in range(8):
                w = next_chunk()
                for m in range(4):
                    by_feature("up", 4 * n + m, w, m, 0, SEQ)
            for n in range(8):
                w = next_chunk()
                pe.wait_ge(flag("ff_ready"), n + 1)
                for t in range(TT):
                    for half in range(2):
                        for k in range(4):
                            last = pe.matmul(psum[:, 4 + 2 * t + half, :],
                                             ffT[:, 4 * n + k, t * P:(t + 1) * P],
                                             w[:, k, 512 * half:512 * (half + 1)],
                                             start=(n == 0 and k == 0), stop=(n == 7 and k == 3))
                    if n == 7 and t == 0:
                        last.then_inc(flag("down_first"), 1)
                last.then_inc(flag("down_used"), 1)
        @block.scalar
        def _(act):
            def load(dst, src, name):
                act.dma_start(dst, src).then_inc(flag(name), 16)

            load(pack[:, :], T["pack"], "in_pack")
            load(xres[:, :, :], T["x"].rearrange("(t p) n -> p t n", p=P), "in_x")
            load(modr[:, 0:2 * D], rowvec("ada_b", 0, 2 * D), "in_mod")
            load(pos_i[:, :], T["positions"], "in_pos")
            load(A1, rowvec("norm1_g", 0, D), "in_n1")
            load(qg, rowvec("q_norm_g", 0, HD), "in_vec")
            load(kg, rowvec("k_norm_g", 0, HD), "in_vec")
            load(sinks, rowvec("sinks", 0, NQ), "in_vec")

            act.wait_ge(flag("in_pack"), 16)
            act.activation(c_act, pk("c"), ACT.Silu).then_inc(flag("c_act"), 1)

            def root(dst, src, n, eps, name):
                act.activation(dst, src, ACT.Sqrt, scale=1.0 / n, bias=eps).then_inc(flag(name), 1)

            def row_root(src, t, scratch, n, name):
                act.activation(scratch, src, ACT.Square, accum_out=ss[:, t:t + 1])
                act.drain()
                root(sd[:, t:t + 1], ss[:, t:t + 1], n, eps_c, name)
                act.drain()

            act.wait_ge(flag("in_x"), 16)
            act.wait_ge(flag("consts"), 1)
            for t in range(TT):
                row_root(xres[:, t, :], t, junk_a, D, "n1_sd")
            load(modr[:, 2 * D:], rowvec("ada_b", 2 * D, 6 * D), "in_mod2")
            load(A2, rowvec("norm2_g", 0, D), "in_vec2")
            load(attn_g, rowvec("attn_out_g", 0, AW), "in_vec2")
            load(skT, T["subkeys"], "in_sk")
            load(w_if[:, :, :], T["w_if"], "in_if")
            load(b_if[:, :], T["b_if"], "in_if")
            load(s5_dt[:, :], T["log_dt"], "in_dt")
            act.wait_ge(flag("rope_reduced"), 1)
            act.activation(rope_t[:, 0:2, :, :], rope_t[:, 0:2, :, :], ACT.Sin).then_inc(
                flag("rope_tab"), 1)

            def read_turn(dst, src, *u, func=None, **kw):
                turn_wait(act, *u)
                ins = act.activation(dst, src, func, **kw) if func else act.copy(dst, src)
                ins.then_inc(turn_read, 1)

            def to_features(name, t, lo, width=P):
                for q in range(2):
                    src = turn_bank(name, t, q)[:, 0:4 * width].rearrange("p (j n) -> p j n", j=4)
                    read_turn(featT[:, 4 * q:4 * q + 4, lo:lo + width], src, name, t, q)

            def read_group(dst, name, i, n=512, m=P, func=None, **kw):
                group_wait(act, name, i)
                src = bank_of(name, i)[0:m, 0:n]
                ins = act.activation(dst, src, func, **kw) if func else act.copy(dst, src)
                read_out(ins, name, i)

            for t in range(TT):
                to_features("h1", t, t * P)
            for t in range(TT):
                read_group(qkv[:, t, 0:AW], "q1", t)
            for t in range(TT):
                read_group(qkv[:, t, AW:768], "kv1", t, n=256)
            for m in range(CT):
                read_group(cbT[:, m, :], "cb", m, n=SEQ)
            for m in range(CT):
                read_group(hp[:, m, 2:2 + SEQ], "cc", m, n=SEQ)
            act.wait_ge(flag("qk_ss"), 1)
            root(qrs, qss, HD, eps_c, "qk_sd")
            for t in range(TT):
                src = turn_bank("qT", t, 0).rearrange("p (j n) -> p j n", j=QPK)
                read_turn(qT[:, t, :, :], src, "qT", t, 0)
            read_turn(kT, turn_bank("kT", 0, 0)[:, 0:SEQ], "kT", 0, 0)
            read_turn(css, turn_bank("css", 0, 0)[:, 0:SEQ], "css", 0, 0, func=ACT.Sqrt,
                      scale=1.0 / CW, bias=eps_c)
            unit = 0
            for t in range(TT):
                nk = P * (t + 1)
                for s in range(NKV):
                    act.wait_ge(flag("S_shifted"), unit + 1)
                    act.activation(S[:, :, 0:nk], S[:, :, 0:nk], ACT.Exp)
                    act.activation(esink, esink, ACT.Exp).then_inc(flag("exp_done"), 1)
                    for b in range(t + 1):
                        src = turn_bank("P", t, 2 * s + b).rearrange("p (j n) -> p j n", j=QPK)
                        read_turn(pT[:, b, :, :], src, "P", t, 2 * s + b)
                    unit += 1
            act.wait_ge(flag("attn_done"), 1)
            for t in range(TT):
                row_root(attn[:, t, :], t, junk_a[:, 0:AW], AW, "at_sd")
            for t in range(TT):
                src = turn_bank("m", t, 0).rearrange("p (j n) -> p j n", j=4)
                read_turn(featT[:, 0:4, t * P:(t + 1) * P], src, "m", t, 0)
            for t in range(TT):
                act.wait_ge(flag("x1_ready"), t + 1)
                row_root(xres[:, t, :], t, junk_a, D, "n2_sd")
            for t in range(TT):
                to_features("h2", t, t * P)
            def read_scores(b):
                for t in range(TT):
                    m = 4 * t + b
                    read_turn(sc[:, 512 * m:512 * (m + 1)], turn_bank("sc", t, b), "sc", t, b)

            for a in range(HP):
                read_group(qpT[:, a, :], "wq", a, n=SEQ)
                if a and a % 4 == 0:
                    read_scores(a // 4 - 1)
                if a == 11:
                    act.wait_ge(flag("top_shifted"), 1)
                    act.activation(top, top, ACT.Exp).then_inc(flag("top_exp"), 1)
            read_scores(3)

            def expert_step(t, pair, more):
                h = pair * 2 + t * HEADS
                act.wait_ge(flag("routed"), pair + (4 * t + 1))
                act.copy(stage[:, 0, :], next_idx[:, 0:TOPK]).then_inc(flag("staged"), 1)
                for par in range(2):
                    act.wait_ge(flag("dots_ready"), h + (par + 1))
                    act.activation(gel[:, :], dots[:, :], ACT.Gelu_apprx_tanh).then_inc(
                        flag("gel_ready"), 1)
                    if par == 0:
                        act.copy(stage[:, 1, :], next_idx[:, TOPK:2 * TOPK]).then_inc(flag("staged"), 1)
                    act.wait_ge(flag("wgt_ready"), h + (par + 1))
                    for k in range(TOPK):
                        act.wait_ge(flag("diag_free"), pair * 32 + (t * 128 + 16 * par + k + 1))
                        act.activation(diag[:, k % 8, :], ident[:, :], ACT.Copy,
                                       scale=wgt[:, k:k + 1]).then_inc(flag("diag_full"), 1)
                    if par == 0 and more:
                        act.wait_ge(flag("top_shifted"), pair + (4 * t + 2))
                        act.activation(top, top, ACT.Exp).then_inc(flag("top_exp"), 1)

            def ln_root(t, name, rows_=P, at=None):
                act.wait_ge(flag(name + "_var"), t + 1)
                at = t if at is None else at
                act.activation(sd[0:rows_, t:t + 1], mv[0:rows_, at, 1:2], ACT.Sqrt,
                               bias=ln_eps_c[0:rows_, :]).then_inc(flag(name + "_sd"), 1)

            for t in range(TT):
                with act.Fori(0, 3) as pair:
                    expert_step(t, pair, True)
                expert_step(t, 3, t + 1 < TT)
                if t == 0:
                    ln_root(0, "me", META, TT)
            to_features("meta", 0, 0, META)
            for t in range(TT):
                ln_root(t, "l0")
            for t in range(TT):
                to_features("h0", t, META + t * P)
            act.wait_ge(flag("s5_start"), 1)
            act.wait_ge(flag("in_dt"), 16)
            act.activation(dt_, s5_dt[:, :], ACT.Exp).then_inc(flag("s5_dt_exp"), 1)
            for m in range(4):
                read_group(uT[:, m, :], "u", m, n=LEN, func=ACT.Identity, bias=pk("b_uqk")[:, m:m + 1])
            for j, nm in enumerate(("q2", "k2")):
                for m in range(4):
                    read_group(qk_in[:, 4 * j + m, 3:3 + LEN], nm, m, n=LEN, func=ACT.Identity,
                               bias=pk("b_uqk")[:, 4 * (j + 1) + m:4 * (j + 1) + m + 1])
            act.wait_ge(flag("in_if"), 32)
            act.wait_ge(flag("s5_args"), 1)
            act.activation(mag, lr, ACT.Exp)
            act.activation(cosv, thc, ACT.Sin)
            act.activation(sinv, thk, ACT.Sin).then_inc(flag("s5_tab"), 1)
            act.wait_ge(flag("turn_args"), 1)
            act.activation(turn_a, turn_ang_a, ACT.Sin)
            act.activation(turn_b[0], turn_ang_b[:, 0, :, :], ACT.Sin)
            act.activation(turn_b[1], turn_ang_b[:, 1, :, :], ACT.Sin).then_inc(flag("turn_tab"), 1)
            for c in range(2):
                read_turn(row_a[:, c, :], turn_bank("if", c, 0)[0:MH, 0:LEN], "if", c, 0,
                          func=ACT.Identity, bias=b_if[:, c:c + 1])

            for c in range(2):
                read_turn(bdT[:, c, :, :], turn_bank("bd", c, 0).rearrange("p (q n) -> p q n", q=4),
                          "bd", c, 0)

            def s5_read(q):
                if q:
                    act.wait_ge(flag("state_ready"), q)
                for i in range(4):
                    for c in range(2):
                        act.wait_ge(flag("bu_full"), 8 * q + 2 * i + c + 1)
                        act.copy(s5t[6 + c][:, i, :], psum[:, 6 + c, 0:LEN]).then_inc(flag("bu_read"), 1)

            def gelu_y(q):
                act.wait_ge(flag("y_read"), q + 1)
                act.activation(gyT[:, q, :], gyT[:, q, :], ACT.Gelu_apprx_tanh).then_inc(
                    flag("gy_ready"), 1)

            def read_tokens(name, dst):
                for n in range(2):
                    for t in range(TT):
                        read_group(dst[:, t, 512 * n:512 * (n + 1)], name, TT * n + t)

            s5_read(0)
            for n in range(2):
                for t in range(3):
                    m = META if t == 0 else P
                    read_group(vtok[0:m, t, 512 * n:512 * (n + 1)], "v2", 3 * n + t, m=m)
            s5_read(1)
            read_tokens("o2", otok)
            act.wait_ge(flag("conv2_y"), 1)
            for m in range(8):
                last = act.activation(qkT[:, m, :], qkT[:, m, :], ACT.Silu, bias=pk("qk_b")[:, m:m + 1])
            last.then_inc(flag("conv2_done"), 1)
            turn_read_wait(act, "if", 1, 0)
            act.activation(row_a[:, 2, :], row_a[:, 1, :], ACT.Abs)
            act.drain()
            act.activation(row_a[:, 2, :], row_a[:, 2, :], ACT.Exp, scale=-1.0)
            act.drain()
            act.activation(row_a[:, 2, :], row_a[:, 2, :], ACT.Ln, bias=1.0).then_inc(flag("ln_done"), 1)
            s5_read(2)
            gelu_y(0)
            gelu_y(1)
            read_tokens("gs", gs)
            s5_read(3)
            gelu_y(2)
            read_tokens("gm", gm)
            turn_wait(act, "ga", 0, 0)
            act.copy(gcol[0:META, 0:MH], turn_bank("ga", 0, 0)[0:META, 0:MH])
            act.copy(gcol[:, MH:5 * MH], turn_bank("ga", 0, 0)[:, MH:5 * MH]).then_inc(turn_read, 1)
            act.drain()
            act.activation(enm, gcol[:, 3 * MH:5 * MH], ACT.Exp, scale=-1.0).then_inc(flag("enm"), 1)
            gelu_y(3)
            act.wait_ge(flag("E_args"), 1)
            act.activation(PT[0:META, 0, :, :], PT[0:META, 0, :, :], ACT.Exp)
            act.activation(PT[:, 1, :, :], PT[:, 1, :, :], ACT.Exp)
            act.activation(PT[:, 2, :, P:SEQ], PT[:, 2, :, P:SEQ], ACT.Exp).then_inc(flag("E_exp"), 1)
            for i, dst in enumerate((otok, gs, gm)):
                act.wait_ge(flag("gate_biased"), i + 1)
                act.activation(dst, dst, ACT.Sigmoid).then_inc(flag("gate_sig"), 1)
            read_turn(dens, turn_bank("den", 0, 0)[:, 0:2 * MH], "den", 0, 0)
            for z in range(2):
                for n in range(2):
                    for t in range(TT):
                        dst = (xres, tmp2)[z][:, t, 512 * n:512 * (n + 1)]
                        read_group(dst, "glu", 4 * z + 2 * n + t, func=(None, ACT.Sigmoid)[z])
            act.drain().then_inc(flag("glu_read"), 1)
            act.wait_ge(flag("hv_ready"), 1)
            root(hrs, hvar, DV, ln_eps_c, "hv_sd")
            for t in range(TT):
                to_features("hm", t, t * P)
            for t in range(TT):
                to_features("mix", t, t * P)
            for t in range(TT):
                ln_root(t, "l1")
            for t in range(TT):
                to_features("hb", t, t * P)
            for k in range(FF // P):
                read_group(ffT[:, k, :], "up", k, n=SEQ, func=ACT.Relu, bias=pk("b_up")[:, k:k + 1])
            for t in range(TT):
                ln_root(t, "l2")

        @block.vector
        def _(dve):
            def tt(o, a, b, op):
                return dve.tensor_tensor(o, a, b, op)

            def ts(o, a, s1, s2=None, op0=ALU.mult, op1=None):
                if op1 is None:
                    return dve.tensor_scalar(o, a, s1, None, op0)
                return dve.tensor_scalar(o, a, s1, s2, op0, op1)

            def stt(o, a, s, b, op0=ALU.mult, op1=ALU.add):
                return dve.scalar_tensor_tensor(out=o, in0=a, scalar=s, in1=b, op0=op0, op1=op1)

            def reduced_rest(dst, k_f, quarter=0):
                stt(dst, k_f, -C2, dst)
                dve.drain()
                stt(dst, k_f, -C3, dst)
                dve.drain()
                ts(dst, dst, 0.5 * math.pi * quarter, PI_IN, ALU.add, ALU.min)
                dve.drain()
                return ts(dst, dst, -PI_IN, None, ALU.max)

            def reduce_angle(dst, ang, k_i, k_f, quarter=0):
                ts(k_i, ang, 1.0 / TWO_PI, 0.25 * quarter, ALU.mult, ALU.add)
                dve.drain()
                dve.tensor_copy(k_f, k_i)
                dve.drain()
                stt(dst, k_f, -C1, ang)
                dve.drain()
                return reduced_rest(dst, k_f, quarter)

            def inverse_root(name, t, rows_=P):
                dve.wait_ge(flag(name + "_sd"), t + 1)
                dve.reciprocal(rs[0:rows_, t:t + 1], sd[0:rows_, t:t + 1])
                dve.drain()

            dve.wait_ge(flag("c_act"), 1)
            dve.tensor_copy(crep, over(c_act, 2, P)).then_inc(flag("crep_ready"), 1)
            dve.wait_ge(flag("in_pos"), 16)
            dve.wait_ge(flag("consts"), 1)
            dve.tensor_copy(st[:, 74:76], pos_i[:, :])
            dve.memset(hp[:, :, 0:2], 0.0)
            dve.drain()
            for t in range(TT):
                ts(rope_t[:, 2, t, :], inv_freq[:, :], st[:, 74 + t:75 + t])
            dve.drain()
            k_i = junk[:, 0:64].bitcast(I32).rearrange("p (t n) -> p t n", t=TT)
            reduce_angle(rope_t[:, 1, :, :], rope_t[:, 2, :, :], k_i, rope_t[:, 3, :, :])
            dve.drain()
            reduce_angle(rope_t[:, 0, :, :], rope_t[:, 2, :, :], k_i, rope_t[:, 3, :, :],
                         quarter=1).then_inc(flag("rope_reduced"), 1)

            def add_mod(i):
                group_wait(dve, "ada", i)
                if i == 0:
                    dve.wait_ge(flag("in_mod"), 16)
                if i == 4:
                    dve.wait_ge(flag("in_mod2"), 16)
                sl = modr[:, 512 * i:512 * (i + 1)]
                read_out(tt(sl, sl, bank_of("ada", i), ALU.add), "ada", i)

            for t in range(TT):
                inverse_root("n1", t)
            dve.wait_ge(flag("in_n1"), 16)
            for i in range(4):
                add_mod(i)
                if i >= 2:
                    dve.drain()
                    sl = slice(512 * (i - 2), 512 * (i - 1))
                    stt(A1[:, sl], scale1[:, sl], 1.0, A1[:, sl], ALU.add, ALU.mult)
            dve.drain()

            def modulated(t, gain, shift, name):
                stt(hbuf[:, t, :], xres[:, t, :], rs[:, t:t + 1], gain, ALU.mult, ALU.mult)
                dve.drain()
                tt(hbuf[:, t, :], hbuf[:, t, :], shift, ALU.add).then_inc(flag(name), 1)

            for t in range(TT):
                modulated(t, A1, shift1, "h1_ready")
            dve.wait_ge(flag("in_vec"), 16 * 3)

            for t in range(TT):
                read_wait(dve, "q1", t)
                read_wait(dve, "kv1", t)
            for t in range(TT):
                sq = junk[:, 0:QKW]
                tt(sq, qkv[:, t, 0:QKW], qkv[:, t, 0:QKW], ALU.mult)
                dve.drain()
                dve.tensor_reduce(qss[:, 10 * t:10 * t + 10],
                                  sq.rearrange("p (h d) -> p h d", d=HD), X, ALU.add)
                dve.drain()
            dve.engine_nop().then_inc(flag("qk_ss"), 1)
            dve.wait_ge(flag("qk_sd"), 1)
            dve.reciprocal(qrs, qrs)
            dve.wait_ge(flag("rope_tab"), 1)
            dve.drain()
            for t in range(TT):
                v = qkv[:, t, 0:QKW].rearrange("p (h d) -> p h d", d=HD)
                o = qkr[:, t, :].rearrange("p (h d) -> p h d", d=HD)
                tt(v, v, over(qrs[:, 10 * t:10 * t + 10], 2, HD), ALU.mult)
                dve.drain()
                tt(v[:, 0:NQ, :], v[:, 0:NQ, :], over(qg, 1, NQ), ALU.mult)
                tt(v[:, NQ:10, :], v[:, NQ:10, :], over(kg, 1, NKV), ALU.mult)
                dve.drain()
                x1, x2 = v[:, :, 0:32], v[:, :, 32:64]
                cos, sin = over(rope_t[:, 0, t, :], 1, 10), over(rope_t[:, 1, t, :], 1, 10)
                tt(rp[:, 0, 0:10, :], x1, cos, ALU.mult)
                tt(rp[:, 1, 0:10, :], x2, sin, ALU.mult)
                tt(rp[:, 0, 10:20, :], x2, cos, ALU.mult)
                tt(rp[:, 1, 10:20, :], x1, sin, ALU.mult)
                dve.drain()
                oq = qkr[:, t, 0:AW].rearrange("p (j s d) -> p s j d", s=NKV, d=HD)
                for lo, at, op in ((0, 0, ALU.subtract), (32, 10, ALU.add)):
                    a, b = (rp[:, i, at:at + NQ, :].rearrange("p (s j) d -> p s j d", s=NKV)
                            for i in range(2))
                    tt(oq[:, :, :, lo:lo + 32], a, b, op)
                    tt(o[:, NQ:10, lo:lo + 32], rp[:, 0, at + NQ:at + 10, :],
                       rp[:, 1, at + NQ:at + 10, :], op)
                dve.drain()
            dve.engine_nop().then_inc(flag("rope_done"), 1)

            for m in range(CT):
                read_wait(dve, "cc", m)
                read_wait(dve, "cb", m)
                group_wait(dve, "cu", m)
                sl = hp[:, m, 2:2 + SEQ]
                read_out(tt(sl, sl, bank_of("cu", m)[:, 0:SEQ], ALU.mult), "cu", m)
            dve.drain()
            w = pk("conv_w").rearrange("p (k m) -> p k m", k=3)
            for m in range(CT):
                ts(cy[:, m, :], hp[:, m, 0:SEQ], w[:, 0, m:m + 1])
            for k in (1, 2):
                dve.drain()
                for m in range(CT):
                    stt(cy[:, m, :], hp[:, m, k:k + SEQ], w[:, k, m:m + 1], cy[:, m, :])
            dve.drain()
            tt(cy, cy, cbT, ALU.mult)
            dve.drain()
            tt(hp[:, :, 0:SEQ], cy, cy, ALU.mult).then_inc(flag("conv_sq"), 1)
            add_mod(4)
            add_mod(5)

            unit = 0
            extra = [6, 7, 8, 9, 10, 11]
            for t in range(TT):
                nk = P * (t + 1)
                mk = mask[:, 1 - t:2, :].rearrange("p b k -> p (b k)")
                for s in range(NKV):
                    dve.wait_ge(flag("S_full"), unit + 1)
                    sp4 = psum[:, 6:8, :].rearrange("p b (j k) -> p (b j) k", j=2)[:, :, 0:nk]
                    Sv = S[:, :, 0:nk]
                    stt(Sv, sp4, HD ** -0.5, over(mk, 1, QPK))
                    dve.drain()
                    dve.tensor_reduce(rmax, Sv, X, ALU.max)
                    dve.drain()
                    tt(rmax, rmax, sinks[:, 4 * s:4 * s + 4], ALU.max)
                    dve.drain()
                    tt(esink, sinks[:, 4 * s:4 * s + 4], rmax, ALU.subtract)
                    tt(Sv, Sv, over(rmax, 2, nk), ALU.subtract).then_inc(flag("S_shifted"), 1)
                    for _ in range(2 if unit < 2 else 1):
                        add_mod(extra.pop(0))
                    dve.wait_ge(flag("exp_done"), unit + 1)
                    dve.tensor_reduce(den4, Sv, X, ALU.add)
                    dve.drain()
                    tt(den4, den4, esink, ALU.add)
                    dve.drain()
                    dve.reciprocal(den4, den4)
                    dve.drain()
                    dve.wait_ge(flag("O_full"), unit + 1)
                    tt(attn[:, t, 256 * s:256 * s + 256].rearrange("p (j d) -> p j d", j=QPK),
                       psum[:, 6, 0:256].rearrange("p (j d) -> p j d", j=QPK),
                       over(den4, 2, HD), ALU.mult).then_inc(flag("O_read"), 1)
                    turn_read_wait(dve, "P", t, 2 * s + t)
                    unit += 1
            dve.drain().then_inc(flag("attn_done"), 1)
            turn_read_wait(dve, "css", 0, 0)
            dve.reciprocal(css, css)
            dve.drain()
            for m in range(CT):
                last = stt(featT[:, CT + m, 0:SEQ], cy[:, m, :], pk("conv_g")[:, m:m + 1], css,
                           ALU.mult, ALU.mult)
            last.then_inc(flag("conv_merged"), 1)
            dve.wait_ge(flag("in_vec2"), 32)
            for t in range(TT):
                inverse_root("at", t)
            for t in range(TT):
                last = stt(attn[:, t, :], attn[:, t, :], rs[:, t:t + 1], attn_g, ALU.mult, ALU.mult)
            last.then_inc(flag("attn_normed"), 1)
            stt(A2, scale2, 1.0, A2, ALU.add, ALU.mult)
            for n in range(2):
                for t in range(TT):
                    i = TT * n + t
                    group_wait(dve, "out1", i)
                    part = junk[:, 512 * (i % 2):512 * (i % 2 + 1)]
                    read_out(tt(part, bank_of("out1", i), gate1[:, 512 * n:512 * (n + 1)], ALU.mult),
                             "out1", i)
                    dve.drain()
                    sl = xres[:, t, 512 * n:512 * (n + 1)]
                    tt(sl, sl, part, ALU.add)
                    if n:
                        dve.drain().then_inc(flag("x1_ready"), 1)
            for t in range(TT):
                inverse_root("n2", t)
                modulated(t, A2, shift2, "h2_ready")
            dve.drain()

            def top16(src, v, i_):
                n = range(len(src))
                for lo in (0, 8):
                    for a in n:
                        dve.max(v[a][:, lo:lo + 8], src[a])
                    dve.drain()
                    for a in n:
                        dve.max_index(i_[a][:, lo:lo + 8], v[a][:, lo:lo + 8], src[a])
                    if lo == 0:
                        for a in n:
                            dve.match_replace(src[a], v[a][:, 0:8], src[a], LOWEST)
                    dve.drain()

            def route_values(m):
                dve.tensor_copy(scs.rearrange("p a k -> p (a k)"), sc[:, bass.ds(m * 512, 512)]
                                if not isinstance(m, int) else sc[:, 512 * m:512 * (m + 1)])
                dve.drain()
                top16([scs[:, a, :] for a in range(4)], [vals[:, a, :] for a in range(4)],
                      [ids_u[:, a, :] for a in range(4)])
                v4 = vals.rearrange("p (h s) k -> p h s k", s=2)
                c4 = cand.rearrange("p h (a b) -> p h a b", a=TOPK)
                tt(c4, over(v4[:, :, 0, :], 3, TOPK), over(v4[:, :, 1, :], 2, TOPK), ALU.add)
                dve.tensor_copy(ids_f.rearrange("p h s k -> p (h s) k"), ids_u)
                dve.drain()
                top16([cand[:, h, :] for h in range(2)], [top[:, h, :] for h in range(2)],
                      [pos_u[:, h, :] for h in range(2)])
                dve.tensor_copy(rsm[:, 0:2].unsqueeze(2), top[:, :, 0:1])
                dve.drain()
                tt(top, top, over(rsm[:, 0:2], 2, TOPK), ALU.subtract).then_inc(flag("top_shifted"), 1)

            def route_numbers(m):
                pf = pos_u.rearrange("p h k -> p (h k)")
                ts(ab_u[:, 0, :], pf, 4, None, ALU.logical_shift_right)
                ts(ab_u[:, 1, :], pf, TOPK - 1, None, ALU.bitwise_and)
                dve.drain()
                dve.tensor_copy(ab_f, ab_u)
                dve.drain()
                for s in range(2):
                    oh = onehot.rearrange("p (n a) -> p n a", a=TOPK)
                    tt(oh, over(ab_f[:, s, :], 2, TOPK), over(iota16[:, :], 1, 2 * TOPK), ALU.is_equal)
                    dve.drain()
                    oh4 = onehot.rearrange("p (h j a) -> p h j a", h=2, a=TOPK)
                    tt(oh4, oh4, over(ids_f[:, :, s, :], 2, TOPK), ALU.mult)
                    dve.drain()
                    dve.tensor_reduce(pick[:, s, :], oh, X, ALU.add)
                    dve.drain()
                stt(next_idx[:, :], pick[:, 0, :], float(KEYS), pick[:, 1, :])
                dve.wait_ge(flag("top_exp"), m + 1)
                dve.tensor_reduce(rsm[:, 2:4], top, X, ALU.add)
                dve.drain()
                dve.reciprocal(rsm[:, 2:4], rsm[:, 2:4])
                dve.drain()
                tt(next_gate[:, :].rearrange("p (h k) -> p h k", h=2), top,
                   over(rsm[:, 2:4], 2, TOPK), ALU.mult)
                dve.drain().then_inc(flag("routed"), 1)

            def expert_step(t, pair, next_m=None, first_turn=None):
                for par in range(2):
                    for k in range(TOPK):
                        at = 32 * par + k
                        s = at % NR
                        dve.wait_ge(row_full[s], pair * (16 * USES) + (t * 4 * USES + at // NR + 1) * 16)
                        dve.tensor_tensor_reduce(rows[:, s, :], rows[:, s, :], hbuf[:, t, :], 1.0,
                                                 0.0, ALU.mult, ALU.add,
                                                 dots[:, k:k + 1]).then_inc(slot_free[s], 1)
                    dve.drain().then_inc(flag("dots_ready"), 1)
                    dve.wait_ge(flag("gel_ready"), pair * 2 + (t * HEADS + par + 1))
                    tt(wgt[:, :], next_gate[:, TOPK * par:TOPK * (par + 1)], gel[:, :],
                       ALU.mult).then_inc(flag("wgt_ready"), 1)
                    if next_m is not None and par == 0:
                        dve.wait_ge(turn_read, first_turn)
                        route_values(next_m)
                    if next_m is not None and par == 1:
                        route_numbers(next_m)

            first_sc = turn_no[("sc", 0, 0)]
            all_sc = turn_no[("sc", TT - 1, 3)] + 1
            turn_read_wait(dve, "sc", 0, 0)
            route_values(0)
            route_numbers(0)
            for s in range(NR):
                dve.engine_nop().then_inc(slot_free[s], 1)

            def two(t3):
                return [t3[:, t, :] for t in range(TT)]

            def variance(src, t, name, rows_=P, at=None):
                at = t if at is None else at
                for half in range(2):
                    dve.bn_stats(bn[0:rows_, t, half, :], src[:, 512 * half:512 * (half + 1)])
                dve.drain()
                dve.bn_aggr(mv[0:rows_, at, :], bn[0:rows_, t, :, :]).then_inc(flag(name + "_var"), 1)

            def normalise(dst, src, t, g, b, name, ready=None, rows_=P, at=None):
                at = t if at is None else at
                inverse_root(name, t, rows_)
                ts(dst, src, mv[0:rows_, at, 0:1], rs[0:rows_, t:t + 1], ALU.subtract, ALU.mult)
                dve.drain()
                tt(dst, dst, g, ALU.mult)
                dve.drain()
                last = tt(dst, dst, b, ALU.add)
                if ready:
                    last.then_inc(flag(ready), 1)

            for t in range(TT):
                with dve.Fori(0, 3) as pair:
                    expert_step(t, pair, pair + (4 * t + 1),
                                pair * 2 + (first_sc + 3) if t == 0 else all_sc)
                if t == 0:
                    expert_step(t, 3, 4, all_sc)
                else:
                    expert_step(t, 3)
                if t == 0:
                    dve.wait_ge(flag("in_ln0"), 48)
                    variance(xmeta, 0, "me", META, TT)
                dve.wait_ge(flag("peer_summed"), t + 1)
                for half in range(2):
                    sl = slice(512 * half, 512 * (half + 1))
                    last = tt(peer_out[:, sl], psum[:, 6 + half, :], gate2[:, sl], ALU.mult)
                last.then_inc(flag("peer_read"), 1)
                dve.drain()
                tt(xres[:, t, :], xres[:, t, :], peer_out, ALU.add)
                dve.drain()
                if t == 0:
                    normalise(xmeta, xmeta, 0, ln0_g[0:META, :], ln0_b[0:META, :], "me",
                              "meta_ready", META, TT)
                    variance(xres[:, 0, :], 0, "l0")
            variance(xres[:, 1, :], 1, "l0")
            for t in range(TT):
                normalise(hbuf[:, t, :], xres[:, t, :], t, ln0_g, ln0_b, "l0", "h0_ready")
            dve.memset(qk_in[:, :, 0:3], 0.0)
            dve.drain().then_inc(flag("s5_start"), 1)

            lre, lim = pk("lam_re"), pk("lam_im")
            dve.wait_ge(flag("s5_dt_exp"), 1)
            tt(lr, lre, dt_, ALU.mult)
            tt(th, lim, dt_, ALU.mult)
            dve.drain()
            reduce_angle(thk, th, s5k, ta)
            dve.drain()
            reduce_angle(thc, th, s5k, ta, quarter=1).then_inc(flag("s5_args"), 1)
            tt(n2, lre, lre, ALU.mult)
            tt(tb, lim, lim, ALU.mult)
            dve.drain()
            tt(n2, n2, tb, ALU.add)
            dve.drain()
            dve.reciprocal(n2, n2)
            dve.wait_ge(flag("s5_tab"), 1)
            tt(lbr, mag, cosv, ALU.mult)
            tt(lbi, mag, sinv, ALU.mult)
            dve.tensor_copy(s5_mag[:, :], mag)
            dve.tensor_copy(s5_th[:, :], thk)
            dve.drain()
            ts(lbr, lbr, -1.0, None, ALU.add)
            dve.drain()
            tt(ta, lbr, lre, ALU.mult)
            tt(tb, lbi, lim, ALU.mult)
            tt(ts_, lbi, lre, ALU.mult)
            dve.drain()
            tt(fr, ta, tb, ALU.add)
            dve.drain()
            tt(ta, lbr, lim, ALU.mult)
            dve.drain()
            tt(fi, ts_, ta, ALU.subtract)
            tt(fr, fr, n2, ALU.mult)
            dve.drain()
            tt(fi, fi, n2, ALU.mult)
            dve.memset(bd, 0.0)
            dve.memset(cd, 0.0)
            ts(ta, s5_th[:, :], 16.0)
            dve.drain()
            reduce_angle(tb, ta, s5k, ts_)
            dve.drain()
            for ang, base, steps, n in (
                    (turn_ang_a, tb, iota_t[:, :].rearrange("p (a b) -> p a b", b=16)[:, :, 0], 17),
                    (turn_ang_b, s5_th[:, :], iota_t[:, 0:16], 16)):
                raw = turn_raw[:, :, 0:n]
                ki = turn_k[:, :, 0:n]
                tt(raw, over(base, 2, n), over(steps, 1, SI), ALU.mult)
                dve.drain()
                for c in range(2):
                    reduce_angle(ang[:, c, :, :], raw, ki, turn_kf[:, :, 0:n], quarter=1 - c)
                    dve.drain()
            dve.engine_nop().then_inc(flag("turn_args"), 1)
            dve.drain()
            dve.wait_ge(flag("in_bc"), 16)
            bre, bim, cre, cim = (bc_raw[:, s, :, :] for s in range(4))
            frb, fib = over(fr, 2, S5H), over(fi, 2, S5H)
            tt(bb[:, 0, :, :], bre, frb, ALU.mult)
            tt(bb[:, 1, :, :], bim, fib, ALU.mult)
            tt(bb[:, 2, :, :], bim, frb, ALU.mult)
            tt(bb[:, 3, :, :], bre, fib, ALU.mult)
            dve.drain()
            bd4 = bd.rearrange("p s (i g h) -> p s i g h", i=SI, g=2)
            cd4 = cd.rearrange("p s i (g h) -> p s i g h", g=2)
            for g in range(2):
                r = slice(64 * g, 64 * g + 64)
                tt(bd4[r, 0, :, g, :], bb[r, 0, :, :], bb[r, 1, :, :], ALU.subtract)
                tt(bd4[r, 1, :, g, :], bb[r, 2, :, :], bb[r, 3, :, :], ALU.add)
                dve.tensor_copy(cd4[r, 0, :, g, :], cre[r, :, :])
                ts(cd4[r, 1, :, g, :], cim[r, :, :], -1.0)
            dve.drain().then_inc(flag("bd_ready"), 1)

            def tables(q):
                if q == 0:
                    dve.wait_ge(flag("turn_tab"), 1)
                a, b = s5t[2], s5t[3]
                r = slice(4 * q, 4 * q + 4)

                def prod(o, ca, cb):
                    tt(o.rearrange("p i (a b) -> p i a b", b=16), over(turn_a[:, ca, r, :], 3, 16),
                       over(turn_b[cb][:, r, :], 2, 17), ALU.mult)

                prod(a, 0, 0)
                prod(b, 1, 1)
                dve.drain()
                tt(s5t[0], a, b, ALU.subtract)
                dve.drain()
                prod(a, 1, 0)
                prod(b, 0, 1)
                dve.drain()
                tt(s5t[1], a, b, ALU.add)
                dve.drain()

            def s5_quad(q):
                dve.wait_ge(flag("bu_read"), 8 * q + 8)
                cos, sin = s5t[0], s5t[1]
                a, b = s5t[2], s5t[3]

                def turn(re, im, sign):
                    o1, o2 = (ALU.add, ALU.subtract) if sign < 0 else (ALU.subtract, ALU.add)
                    tt(a, cos, re, ALU.mult)
                    tt(b, sin, im, ALU.mult)
                    dve.drain()
                    tt(s5t[4], a, b, o1)
                    dve.drain()
                    tt(a, cos, im, ALU.mult)
                    tt(b, sin, re, ALU.mult)
                    dve.drain()
                    last = tt(s5t[5], a, b, o2)
                    dve.drain()
                    return last

                turn(s5t[6], s5t[7], -1)
                for i in range(4):
                    r = s5_mag[:, 4 * q + i:4 * q + i + 1].broadcast_to([P, LEN])
                    for c in range(2):
                        dve.tensor_tensor_scan(s5t[6 + c][:, i, :], r, s5t[4 + c][:, i, :], 0.0,
                                               ALU.mult, ALU.add)
                dve.drain()
                turn(s5t[6], s5t[7], 1)
                dve.engine_nop().then_inc(flag("state_ready"), 1)

            def s5_y(q):
                dve.wait_ge(flag("y_full"), q + 1)
                stt(gyT[:, q, :], uT[:, q, META:LEN], pk("s5_d")[:, q:q + 1],
                    psum[:, 6, 0:SEQ]).then_inc(flag("y_read"), 1)

            tables(0)
            s5_quad(0)
            for m in range(4):
                read_wait(dve, "q2", m)
                read_wait(dve, "k2", m)
            w = pk("qk_w").rearrange("p (k m) -> p k m", k=4)
            for m in range(8):
                ts(qkT[:, m, :], qk_in[:, m, 0:LEN], w[:, 0, m:m + 1])
            for k in range(1, 4):
                dve.drain()
                for m in range(8):
                    stt(qkT[:, m, :], qk_in[:, m, k:k + LEN], w[:, k, m:m + 1], qkT[:, m, :])
            dve.drain().then_inc(flag("conv2_y"), 1)
            s5_y(0)
            for q in range(1, 3):
                tables(q)
                s5_quad(q)
                s5_y(q)
            tables(3)
            dve.wait_ge(flag("ln_done"), 1)
            li, f, l1p = (row_a[:, i, :] for i in range(3))
            ra, rM, rN = (row_b[:, i, :] for i in range(3))
            stt(f, f, 0.0, l1p, ALU.min, ALU.subtract)
            dve.drain()
            dve.tensor_tensor_scan(rN, ones[0:MH, 0:1].broadcast_to([MH, LEN]), f, 0.0, ALU.mult, ALU.add)
            dve.drain()
            tt(ra, li, rN, ALU.subtract)
            dve.drain()
            dve.tensor_tensor_scan(rM, ones[0:MH, 0:1].broadcast_to([MH, LEN]), ra, 0.0, ALU.mult, ALU.max)
            dve.drain()
            tt(rN, rN, rM, ALU.add).then_inc(flag("rows_ready"), 1)
            s5_quad(3)
            s5_y(3)

            dve.wait_ge(flag("mbc_full"), 1)
            dve.wait_ge(flag("enm"), 1)
            for b in range(3):
                nr, lo = (META, 0) if b == 0 else (P, (b - 1) * P)
                for h in range(MH):
                    src = psum[0:nr, 6 + h // 2, (h % 2) * SEQ + lo:(h % 2 + 1) * SEQ]
                    last = ts(PT[0:nr, b, h, lo:SEQ], src, -1.0, gcol[0:nr, MH * b + h:MH * b + h + 1],
                              ALU.mult, ALU.add)
            last.then_inc(flag("mbc_read"), 1)
            dve.drain()
            parts = [PT[0:META, 0, :, :], PT[:, 1, :, :], PT[:, 2, :, P:SEQ]]
            for p_ in parts:
                last = ts(p_, p_, 0.0, None, ALU.min)
            last.then_inc(flag("E_args"), 1)
            dve.wait_ge(flag("E_exp"), 1)
            for b in (1, 2):
                sl = PT[:, b, :, (b - 1) * P:b * P]
                tt(sl, sl, over(causal[:, :], 1, MH), ALU.mult)
            dve.drain()
            n = 0
            for b in range(3):
                nr, lo = (META, 0) if b == 0 else (P, (b - 1) * P)
                for hh in range(2):
                    dve.wait_ge(flag("st_full"), n + 1)
                    src = psum[0:nr, 6 + n % 2, :].rearrange("p (h n) -> p h n", h=2)[:, :, lo:SEQ]
                    dst = PT[0:nr, b, 2 * hh:2 * hh + 2, lo:SEQ]
                    stt(dst, src, DK ** -0.5, dst, ALU.mult, ALU.mult).then_inc(flag("st_read"), 1)
                    n += 1
            dve.drain().then_inc(flag("PT_ready"), 1)
            turn_read_wait(dve, "den", 0, 0)
            stt(dens, dens, -1.0, dens, ALU.mult, ALU.max)
            dve.drain()
            tt(dens, dens, enm, ALU.max)
            dve.drain()
            dve.reciprocal(rden, dens)
            dve.drain()
            n = 0
            h4 = hm.rearrange("p t (h e) -> p t h e", h=MH)
            for t in range(TT):
                for hh in range(2):
                    dve.wait_ge(flag("num_full"), n + 1)
                    tt(h4[:, t, 2 * hh:2 * hh + 2, :],
                       psum[:, 6 + n % 2, :].rearrange("p (h e) -> p h e", h=2),
                       over(rden[:, MH * t + 2 * hh:MH * t + 2 * hh + 2], 2, DV),
                       ALU.mult).then_inc(flag("num_read"), 1)
                    n += 1
            dve.drain()
            hf = hm.rearrange("p t (h e) -> p (t h) e", h=MH)
            dve.tensor_reduce(hsum, hf, X, ALU.add)
            dve.drain()
            ts(hsum, hsum, -1.0 / DV)
            dve.drain()
            tt(hf, hf, over(hsum, 2, DV), ALU.add)
            dve.drain()
            sq = PT.rearrange("p b h n -> p (b h n)")[:, 0:2048].rearrange("p (a e) -> p a e", e=DV)
            tt(sq, hf, hf, ALU.mult)
            dve.drain()
            dve.tensor_reduce(hvar, sq, X, ALU.add)
            dve.drain()
            dve.engine_nop().then_inc(flag("hv_ready"), 1)
            dve.wait_ge(flag("hv_sd"), 1)
            dve.reciprocal(hrs, hrs)
            dve.drain()
            tt(hf, hf, over(hrs, 2, DV), ALU.mult)
            dve.drain()
            dve.wait_ge(flag("in_ln1"), 48)
            dve.wait_ge(flag("gate_sig"), 3)
            tt(hm, hm, over(m_norm, 1, TT), ALU.mult)
            dve.drain()
            tt(hm, hm, otok, ALU.mult).then_inc(flag("hm_ready"), 1)
            dve.wait_ge(flag("glu_read"), 1)
            tt(gs, gs, xres[:, :, :], ALU.mult)
            dve.drain()
            tt(gs, gs, tmp2, ALU.mult)
            dve.drain()
            for n in range(2):
                for t in range(TT):
                    i = TT * n + t
                    sl = slice(512 * n, 512 * (n + 1))
                    group_wait(dve, "mo", i)
                    read_out(tt(gm[:, t, sl], gm[:, t, sl], bank_of("mo", i), ALU.mult), "mo", i)
            dve.drain()
            tt(gs, gs, gm, ALU.add).then_inc(flag("mix_ready"), 1)

            def residual(src, t, sl):
                return stt(xres[:, t, sl], hbuf[:, t, sl], ALPHA, src)

            for n in range(2):
                for t in range(TT):
                    i = TT * n + t
                    group_wait(dve, "wo", i)
                    read_out(residual(bank_of("wo", i), t, slice(512 * n, 512 * (n + 1))), "wo", i)
                    if n:
                        dve.drain()
                        variance(xres[:, t, :], t, "l1")
            for t in range(TT):
                normalise(hbuf[:, t, :], xres[:, t, :], t, ln1_g, ln1_b, "l1", "hb_ready")
            for n in range(8):
                read_wait(dve, "up", 4 * n + 3)
                for m in range(3):
                    read_wait(dve, "up", 4 * n + m)
                sl = ffT[:, 4 * n:4 * n + 4, :]
                tt(sl, sl, sl, ALU.mult).then_inc(flag("ff_ready"), 1)
            for t in range(TT):
                dve.wait_ge(*((flag("down_first"), 1) if t == 0 else (flag("down_used"), 8)))
                for half in range(2):
                    residual(psum[:, 4 + 2 * t + half, :], t, slice(512 * half, 512 * (half + 1)))
                dve.drain()
                variance(xres[:, t, :], t, "l2")
            dve.wait_ge(flag("in_ln2"), 32)
            for t in range(TT):
                normalise(fin[:, t, :], xres[:, t, :], t, ln2_g, ln2_b, "l2", "fin_ready")


def kernel(**inputs):
    import concourse.bacc as _bacc
    from concourse.bass_utils import run_bass_kernel_spmd as _run

    A = {n: np.ascontiguousarray(a) for n, a in inputs.items()}

    def cols(v, n):
        return v.reshape(n, P).T

    def state(a):
        return np.moveaxis(a.reshape((SI, P) + a.shape[2:]), 0, 1)

    b_in, w_in2 = A["b_in_2"].reshape(-1), A["w_in_2"][0]
    given = {
        "c": cols(A["c"].reshape(-1), KD),
        "conv_w": np.moveaxis(A["conv_w"][0].reshape(3, CT, P), 2, 0).reshape(P, -1),
        "conv_g": cols(A["conv_out_g"].reshape(-1), CT),
        "b_uqk": cols(b_in[U0:V0], 12),
        "qk_w": np.moveaxis(A["qk_conv_w_2"][0].reshape(4, 8, P), 2, 0).reshape(P, -1),
        "qk_b": cols(A["qk_conv_b_2"].reshape(-1), 8),
        "lam_re": state(A["s5_lambda_re_2"][0]),
        "lam_im": state(A["s5_lambda_im_2"][0]),
        "s5_d": cols(A["s5_d_2"].reshape(-1), 4),
        "b_up": cols(A["b_up_2"].reshape(-1), FF // P),
    }
    c_re, c_im = (np.swapaxes(A[n][0], 1, 2) for n in ("s5_c_re_2", "s5_c_im_2"))
    host = {
        "pack": np.concatenate([given[n] for n, _ in PACK], axis=1),
        "positions": A["positions"].reshape(TT, P).T,
        "x": A["x"].reshape(SEQ, D),
        "subkeys": np.moveaxis(A["peer_subkeys"][0].reshape(HP, KEYS, P), 2, 0),
        "w_if": np.moveaxis(w_in2[:, IF0:IF0 + 2 * MH].reshape(KD, P, 2 * MH), 1, 0),
        "b_if": b_in[IF0:IF0 + 2 * MH].reshape(2, MH).T,
        "log_dt": np.repeat(A["s5_log_dt_2"].reshape(SI, 2).T, S5P, axis=0),
        "s5_bc": np.stack([state(A["s5_b_re_2"][0]), state(A["s5_b_im_2"][0]), state(c_re),
                           state(c_im)], axis=1),
        "meta_tokens_2": A["meta_tokens_2"],
    }
    for n in ("ada_w", "w_in", "w_out", "peer_wq", "peer_u", "peer_v", "w_in_2", "s5_w_glu_2",
              "m_w_out_2", "w_o_2", "w_up_2", "w_down_2"):
        host[n] = A[n][0]
    for n in ("ada_b", "norm1_g", "norm2_g", "q_norm_g", "k_norm_g", "sinks", "attn_out_g", "b_in_2",
              "m_norm_g_2", "ln0_g_2", "ln0_b_2", "ln1_g_2", "ln1_b_2", "ln2_g_2", "ln2_b_2"):
        host[n] = A[n].reshape(-1)

    nc = _bacc.Bacc("TRN2", target_bir_lowering=False, num_devices=1)
    arrays, T = {}, {}
    for n, a in host.items():
        a = np.ascontiguousarray(a)
        arrays[f"in_{n}_dram"] = a
        T[n] = nc.dram_tensor(f"in_{n}_dram", a.shape, mybir.dt.from_np(a.dtype),
                              kind="ExternalInput").ap()
    out = nc.dram_tensor("out_0_dram", (SEQ, D), F32, kind="ExternalOutput").ap()
    build(nc, T, out)
    r = _run(nc, [arrays], core_ids=[0])
    return r.results[0]["out_0_dram"].reshape(1, SEQ, D)
```

```python
from contextlib import ExitStack
import math

import numpy as np

import concourse.bass as bass
from concourse import mybir

ALU = mybir.AluOpType
ACT = mybir.ActivationFunctionType
F32 = mybir.dt.float32
U32 = mybir.dt.uint32
I32 = mybir.dt.int32
X = mybir.AxisListType.X

P = 128
D = 1024
KD = D // P
SEQ = 256
TT = SEQ // P
META = 16
LEN = META + SEQ
HD = 64
NQ, NKV = 8, 2
QPK = NQ // NKV
AW = NQ * HD
QKW = (NQ + NKV) * HD
CW = D - AW
CT = CW // P
THETA = 10000.0
EPS = 1e-6
LN_EPS = 1e-5
NEG = -1e30
HEADS, KEYS, TOPK = 8, 128, 16
HP = 2 * HEADS
S5G, S5H, S5P = 32, 16, 64
SI = S5G * S5P // P
MH, DK, DV = 4, 128, 256
FF = 4 * D
ALPHA = 2.0 ** 0.25
LOWEST = -3.0e38

TWO_PI = 2.0 * math.pi
C1 = 6.28125
C2 = float(np.float32(np.round((TWO_PI - C1) * 2.0 ** 22) / 2.0 ** 22))
C3 = TWO_PI - C1 - C2
PI_IN = 3.1415925

RING = 3
CHUNK = 4096
BY_VECTOR = (2, 5, 8, 11, 14)
SUM_BANK = (0, 6)
USES = 64 // 8
GW = 12
STEPS = 8
NR = 8
ACC = 4

PACK = [("c", KD), ("conv_w", 3 * CT), ("conv_g", CT), ("b_uqk", 12), ("qk_w", 32), ("qk_b", 8),
        ("lam_re", SI), ("lam_im", SI), ("s5_d", 4), ("b_up", FF // P)]
PACK_AT, PACK_W = {}, 0
for _name, _w in PACK:
    PACK_AT[_name] = (PACK_W, PACK_W + _w)
    PACK_W += _w

U0, Q0, K0, V0, O0, IF0, GS0, GM0 = 0, 512, 1024, 1536, 2560, 3584, 3592, 4616


def plan():
    chunks, groups = [], []

    def add(name, w, c, n, k0=0, kt=KD, gs=()):
        chunks.append((name, w, k0, kt, c, n))
        groups.append(list(gs))

    def ada(lo, hi):
        for i in range(lo, hi):
            add("ada", "ada_w", 512 * i, 512, gs=[("ada", i)])

    ada(0, 4)
    add("in1", "w_in", 0, 512, gs=[("q1", t) for t in range(TT)])
    add("in1", "w_in", 512, 256, gs=[("kv1", t) for t in range(TT)])
    for j, nm in enumerate(("cb", "cc", "cu")):
        add("in1", "w_in", 768 + 512 * j, 512, gs=[(nm, m) for m in range(4)])
    ada(4, 12)
    for n in range(2):
        add("out1", "w_out", 512 * n, 512, gs=[("out1", TT * n + t) for t in range(TT)])
    for n in range(4):
        add("wq", "peer_wq", 512 * n, 512, gs=[("wq", 4 * n + m) for m in range(4)])
    by_tile = [(nm + str(t), m) for t in range(TT) for nm in ("u", "q2", "k2") for m in range(4)]
    for nm, c in (("u", U0), ("q2", Q0), ("k2", K0)):
        add("in2", "w_in_2", c, 512, gs=by_tile if nm == "k2" else [])
    for n in range(2):
        add("in2", "w_in_2", V0 + 512 * n, 512, gs=[("v2", 3 * n + t) for t in range(3)])
    for nm, c in (("o2", O0), ("gs", GS0), ("gm", GM0)):
        for n in range(2):
            add("in2", "w_in_2", c + 512 * n, 512, gs=[(nm, TT * n + t) for t in range(TT)])
    for n in range(2):
        add("glu", "s5_w_glu_2", D * n, D, kt=4, gs=[("glu", 4 * n + i) for i in range(4)])
    for n in range(2):
        add("mo", "m_w_out_2", 512 * n, 512, gs=[("mo", TT * n + t) for t in range(TT)])
    for n in range(2):
        add("wo", "w_o_2", 512 * n, 512, gs=[("wo", TT * n + t) for t in range(TT)])
    for n in range(8):
        add("up", "w_up_2", 512 * n, 512, gs=[("up", 4 * n + m) for m in range(4)])
    for n in range(8):
        add("down", "w_down_2", 0, D, k0=4 * n, kt=4, gs=[])
    return chunks, groups


CHUNKS, GROUPS = plan()
LAST_USE = {i: gs[-1] for i, gs in enumerate(GROUPS) if gs}
LAST_WQ = max(i for i, c in enumerate(CHUNKS) if c[0] == "wq")
for _i, _nm in enumerate(("u1", "q21", "k21")):
    LAST_USE[LAST_WQ + 1 + _i] = (_nm, 3)
GROUP_NO = {}
for _gs in GROUPS:
    for _g in _gs:
        GROUP_NO[_g] = len(GROUP_NO)


def build(nc, T, out):
    with ExitStack() as ctx:
        def sb(name, shape, dt=F32):
            return ctx.enter_context(nc.sbuf_tensor(name, shape, dt))

        def sem(name):
            return ctx.enter_context(nc.semaphore(name))

        def over(ap, axis, n):
            ap = ap.unsqueeze(axis)
            shape = list(ap.shape)
            shape[axis] = n
            return ap.broadcast_to(shape)

        ring = sb("weight_ring", [P, RING, CHUNK])
        xres = sb("xres", [P, TT, D])
        featT = sb("featT", [P, KD, LEN])
        hbuf = sb("hbuf", [P, TT, D])
        modr = sb("modr", [P, 6 * D])
        wk = sb("work", [P, 8704])
        G = sb("gathered", [P, GW * D])
        vec = sb("vectors", [P, 4 * D])
        pack = sb("pack", [P, PACK_W])
        ident = sb("ident", [P, P])
        ones = sb("ones", [P, P])
        mask = sb("mask", [P, 2, P])
        causal = sb("causal", [P, P])
        iota_t = sb("iota_t", [P, LEN])
        iota16 = sb("iota16", [P, TOPK])
        zeros = sb("zeros", [P, P])
        rope_t = sb("rope_t", [P, 4, TT, HD // 2])
        inv_freq = sb("inv_freq", [P, HD // 2])
        uT = sb("uT", [P, 4, LEN])
        next_idx = sb("next_idx", [P, 2 * TOPK], U32)
        next_gate = sb("next_gate", [P, 2 * TOPK])
        bn = sb("bn", [P, TT, 2, 6])
        mv = sb("mean_var", [P, TT + 1, 2])
        stage = sb("stage", [P, 2, TOPK], U32)
        dots = sb("dots", [P, TOPK])
        gel = sb("gel", [P, TOPK])
        wgt = sb("wgt", [P, TOPK])
        st = sb("stats", [P, 96])
        pos_i = sb("pos_i", [P, TT], I32)
        w_if = sb("w_if", [P, KD, 2 * MH])
        b_if = sb("b_if", [MH, 2])
        s5_dt = sb("s5_log_dt", [P, SI])
        s5_mag = sb("s5_mag", [P, SI])
        s5_th = sb("s5_theta", [P, SI])
        col2 = sb("mlstm_cols", [P, 52])
        psum = ctx.enter_context(nc.psum_tensor("psum", [P, 8, 512], F32))

        def pk(name):
            a, b = PACK_AT[name]
            return pack[:, a:b]

        crep = G[:, 0:1024].rearrange("p (k m) -> p k m", k=KD)
        qkv = G[:, 1024:2560].rearrange("p (t n) -> p t n", t=TT)
        qkr = G[:, 2560:3840].rearrange("p (t n) -> p t n", t=TT)
        S = G[:, 3840:4864].rearrange("p (j k) -> p j k", j=QPK)
        pT = G[:, 4864:5888].rearrange("p (b j q) -> p b j q", b=2, j=QPK)
        qT = G[:, 5888:6912].rearrange("p (t j q) -> p t j q", t=TT, j=QPK)
        kT = G[:, 6912:7168]
        attn = G[:, 7168:8192].rearrange("p (t n) -> p t n", t=TT)
        cbT = G[:, 8192:9216].rearrange("p (m n) -> p m n", m=CT)
        hp = G[:, 9216:10248].rearrange("p (m n) -> p m n", m=CT)
        cy = G[:, 10248:11272].rearrange("p (m n) -> p m n", m=CT)
        junk = wk[:, 0:1280]
        junk_a = wk[:, 1280:2304]
        rp = wk[:, 2304:3584].rearrange("p (n a b) -> p n a b", n=2, b=HD // 2)
        A1, A2, attn_g = vec[:, 0:D], vec[:, D:2 * D], vec[:, 2 * D:2 * D + AW]
        qg, kg = vec[:, 2560:2624], vec[:, 2624:2688]
        sinks = vec[:, 2688:2696]
        shift1, scale1, gate1, shift2, scale2, gate2 = (modr[:, D * i:D * (i + 1)] for i in range(6))
        qpT = wk[:, 0:4096].rearrange("p (a t) -> p a t", a=HP)
        skT = wk[:, 4096:6144].rearrange("p (a k) -> p a k", a=HP)
        rt = wk[:, 6144:8704]
        scs = rt[:, 0:512].rearrange("p (a k) -> p a k", a=4)
        cand = rt[:, 512:1024].rearrange("p (h n) -> p h n", h=2)
        onehot = rt[:, 1024:1536]
        vals = rt[:, 1536:1600].rearrange("p (a k) -> p a k", a=4)
        ids_u = rt[:, 1600:1664].bitcast(U32).rearrange("p (a k) -> p a k", a=4)
        ids_f = rt[:, 1664:1728].rearrange("p (h s k) -> p h s k", s=2, k=TOPK)
        top = rt[:, 1728:1760].rearrange("p (h k) -> p h k", h=2)
        pos_u = rt[:, 1760:1792].bitcast(U32).rearrange("p (h k) -> p h k", h=2)
        ab_u = rt[:, 1792:1856].bitcast(U32).rearrange("p (s n) -> p s n", s=2)
        ab_f = rt[:, 1856:1920].rearrange("p (s n) -> p s n", s=2)
        pick = rt[:, 1920:1984].rearrange("p (s n) -> p s n", s=2)
        rsm = rt[:, 1984:1988]
        sc = G[:, NR * D:NR * D + STEPS * 512]
        rows = G[:, 0:NR * D].rearrange("p (s n) -> p s n", s=NR)
        diag = modr[:, 0:D].rearrange("p (s n) -> p s n", s=8)
        peer_out = modr[:, D:2 * D]
        ln0_g, ln0_b = wk[:, 2048:3072], wk[:, 3072:4096]
        xmeta = wk[0:META, 4096:5120]
        bc_raw = wk[:, 5120:6144].rearrange("p (s i h) -> p s i h", s=4, i=SI)
        bb = wk[:, 6144:7168].rearrange("p (s i h) -> p s i h", s=4, i=SI)
        bd = wk[:, 7168:8192].rearrange("p (s n) -> p s n", s=2)
        s5c = wk[:, 8192:8448].rearrange("p (s i) -> p s i", s=16)
        s5k = wk[:, 8448:8464].bitcast(I32)
        turn_b = [mask[:, :, :].rearrange("p b (i n) -> p (b i) n", n=16),
                  rope_t[:, :, :, :].rearrange("p a t (i n) -> p (a t i) n", n=16)]
        turn_ang_a = wk[:, 0:544].rearrange("p (s i n) -> p s i n", s=2, i=SI)
        turn_ang_b = wk[:, 544:1056].rearrange("p (s i n) -> p s i n", s=2, i=SI)
        turn_k = wk[:, 1056:1328].bitcast(I32).rearrange("p (i n) -> p i n", i=SI)
        turn_kf = wk[:, 1328:1600].rearrange("p (i n) -> p i n", i=SI)
        turn_raw = wk[:, 1600:1872].rearrange("p (i n) -> p i n", i=SI)
        turn_a = modr[:, 4248:4792].rearrange("p (s i n) -> p s i n", s=2, i=SI)
        bdT = modr[:, 0:1024].rearrange("p (s q n) -> p s q n", s=2, q=4)
        cd = modr[:, 1024:2048].rearrange("p (s i n) -> p s i n", s=2, i=SI)
        qk_in = modr[:, 2048:4248].rearrange("p (m n) -> p m n", m=8)
        gyT = modr[:, 2048:3072].rearrange("p (m n) -> p m n", m=4)
        row_a = modr[0:MH, 5120:5936].rearrange("p (s n) -> p s n", s=3)
        vtok = G[:, 0:3072].rearrange("p (t n) -> p t n", t=3)
        otok = G[:, 3072:5120].rearrange("p (t n) -> p t n", t=TT)
        gs = G[:, 5120:7168].rearrange("p (t n) -> p t n", t=TT)
        gm = G[:, 7168:9216].rearrange("p (t n) -> p t n", t=TT)
        qkT = G[:, 9216:11392].rearrange("p (m n) -> p m n", m=8)
        row_b = G[0:MH, 11392:12208].rearrange("p (s n) -> p s n", s=3)
        QW = 4 * LEN
        s5t = [wk[:, QW * i:QW * (i + 1)].rearrange("p (i n) -> p i n", i=4) for i in range(8)]
        PT = wk[:, 0:3072].rearrange("p (b h n) -> p b h n", b=3, h=MH)
        hm = wk[:, 3072:5120].rearrange("p (t n) -> p t n", t=TT)
        tmp2 = wk[:, 5120:7168].rearrange("p (t n) -> p t n", t=TT)
        ffT = wk[:, 0:8192].rearrange("p (k n) -> p k n", k=FF // P)
        m_norm, ln1_g, ln1_b = vec[:, 0:D], vec[:, D:2 * D], vec[:, 2 * D:3 * D]
        ln2_g, ln2_b = modr[:, 0:D], modr[:, D:2 * D]
        fin = G[:, 0:2048].rearrange("p (t n) -> p t n", t=TT)

        ring_full = [sem(f"ring_full{i}") for i in range(RING)]
        bank_full = [sem(f"bank_full{i}") for i in range(ACC)]
        bank_free = [sem(f"bank_free{i}") for i in range(ACC)]
        turned = sem("turned")
        turn_read = sem("turn_read")
        row_full = [sem(f"row_full{i}") for i in range(NR)]
        slot_free = [sem(f"slot_free{i}") for i in range(NR)]
        S_ = {}

        def flag(name):
            if name not in S_:
                S_[name] = sem(name)
            return S_[name]

        def group_wait(eng, name, i):
            g = GROUP_NO[(name, i)]
            eng.wait_ge(bank_full[g % ACC], g // ACC + 1)

        def bank_of(name, i):
            return psum[:, GROUP_NO[(name, i)] % ACC, :]

        def read_out(ins, name, i):
            ins.then_inc(bank_free[GROUP_NO[(name, i)] % ACC], 1)

        block = ctx.enter_context(nc.Block())
        ss, sd, rs = (st[:, 2 * i:2 * i + 2] for i in range(3))
        qss, qrs = st[:, 12:32], st[:, 32:52]
        rmax, esink, den4 = st[:, 52:56], st[:, 56:60], st[:, 60:64]
        c_act = st[:, 64:72]
        eps_c, ln_eps_c = st[:, 72:73], st[:, 73:74]
        gcol = col2[:, 0:20]
        enm, dens, rden = col2[:, 20:28], col2[:, 28:36], col2[:, 36:44]
        hrs = col2[:, 44:52]
        hbn = wk[:, 7168:7216].rearrange("p (a s) -> p a s", s=6)
        hmv = wk[:, 7216:7232].rearrange("p (a s) -> p a s", s=2)
        css = wk[:, 3584:3840]
        lr, th, thk, thc, mag, cosv, sinv, lbr, lbi, fr, fi, n2, ta, tb, ts_ = (
            s5c[:, i, :] for i in range(15))

        turns = []
        turns += [("h1", t, q) for t in range(TT) for q in range(2)]
        turns += [("qT", t, 0) for t in range(TT)] + [("kT", 0, 0), ("css", 0, 0)]
        for t in range(TT):
            for s in range(NKV):
                turns += [("P", t, 2 * s + b) for b in range(t + 1)]
        turns += [("m", t, 0) for t in range(TT)]
        turns += [("h2", t, q) for t in range(TT) for q in range(2)]
        turns += [("sc", t, b) for b in range(STEPS // TT) for t in range(TT)]
        turns += [("meta", 0, q) for q in range(2)]
        turns += [("h0", t, q) for t in range(TT) for q in range(2)]
        turns += [("if", c, 0) for c in range(2)] + [("bd", c, 0) for c in range(2)]
        turns += [("ga", 0, 0), ("den", 0, 0)]
        for nm in ("hm", "mix", "hb"):
            turns += [(nm, t, q) for t in range(TT) for q in range(2)]
        turn_no = {u: n for n, u in enumerate(turns)}

        def turn_bank(*u):
            return psum[:, 4 + turn_no[u] % 2, :]

        def turn_wait(eng, *u):
            eng.wait_ge(turned, turn_no[u] + 1)

        def turn_read_wait(eng, *u):
            eng.wait_ge(turn_read, turn_no[u] + 1)

        def read_wait(eng, name, i):
            g = GROUP_NO[(name, i)]
            eng.wait_ge(bank_free[g % ACC], g // ACC + 1)

        def tensor_rows(last):
            return [k for k in range(TOPK) if not (last and k in BY_VECTOR)]

        def tile_range(t):
            return (0 if t == 0 else META + P), META + (t + 1) * P

        def rowvec(name, lo, hi):
            return T[name][lo:hi].partition_broadcast(P)

        @block.sync
        def _(sp):
            for c, (_, w, k0, kt, col, n) in enumerate(CHUNKS):
                if c >= RING:
                    if c - RING in LAST_USE:
                        group_wait(sp, *LAST_USE[c - RING])
                    else:
                        sp.wait_ge(flag("down_used"), c - RING - (len(CHUNKS) - 8) + 1)
                dst = ring[:, c % RING, 0:kt * n].rearrange("p (k n) -> p k n", k=kt)
                src = T[w].rearrange("(k p) n -> p k n", p=P)[:, k0:k0 + kt, col:col + n]
                sp.dma_start(dst, src).then_inc(ring_full[c % RING], 16)
                if c == LAST_WQ + RING:
                    turn_read_wait(sp, "sc", TT - 1, 3)
                    for dst, name in ((ln0_g, "ln0_g_2"), (ln0_b, "ln0_b_2")):
                        sp.dma_start(dst, rowvec(name, 0, D)).then_inc(flag("in_ln0"), 16)
                    sp.dma_start(xmeta, T["meta_tokens_2"]).then_inc(flag("in_ln0"), 16)
                    sp.dma_start(bc_raw, T["s5_bc"]).then_inc(flag("in_bc"), 16)
                    for i, lo in enumerate((V0, O0, GS0, GM0)):
                        sp.dma_start(vec[:, D * i:D * (i + 1)], rowvec("b_in_2", lo, lo + D)).then_inc(
                            flag("in_bias2"), 16)
            for t in range(TT):
                sp.wait_ge(flag("fin_ready"), t + 1)
                sp.dma_start(out[t * P:(t + 1) * P, :], fin[:, t, :]).then_inc(flag("stored"), 16)
            sp.wait_ge(flag("stored"), 16 * TT)

        @block.gpsimd
        def _(pool):
            pool.memset(ident[:, :], 0.0)
            pool.memset(ones[:, :], 1.0)
            pool.memset(zeros[:, :], 0.0)
            pool.memset(mask[:, :, :], 0.0)
            pool.memset(causal[:, :], 1.0)
            pool.iota(iota_t[:, :], [[1, LEN]], base=0, channel_multiplier=0,
                      allow_small_or_imprecise_dtypes=True)
            pool.iota(iota16[:, :], [[1, TOPK]], base=0, channel_multiplier=0,
                      allow_small_or_imprecise_dtypes=True)
            for j in range(HD // 2):
                pool.memset(inv_freq[:, j:j + 1], float(np.float32(THETA) ** np.float32(-2.0 * j / HD)))
            pool.drain()
            pool.affine_select(out=ident[:, :], in_=ident[:, :], compare_op=ALU.not_equal, fill=1.0,
                               base=0, pattern=[[-1, P]], channel_multiplier=1)
            pool.affine_select(out=mask[:, 0, :], in_=mask[:, 0, :], compare_op=ALU.is_gt, fill=NEG,
                               base=0, pattern=[[1, P]], channel_multiplier=-1)
            pool.affine_select(out=mask[:, 1, :], in_=mask[:, 1, :], compare_op=ALU.is_ge, fill=NEG,
                               base=0, pattern=[[-1, P]], channel_multiplier=1)
            pool.affine_select(out=causal[:, :], in_=causal[:, :], compare_op=ALU.is_ge, fill=0.0,
                               base=0, pattern=[[1, P]], channel_multiplier=-1)
            pool.memset(eps_c, EPS)
            pool.memset(ln_eps_c, LN_EPS)
            pool.drain().then_inc(flag("consts"), 1)

            def gather_step(t, pair):
                for par in range(2):
                    for part, tab in enumerate(("peer_u", "peer_v")):
                        for k in range(TOPK):
                            at = 32 * par + TOPK * part + k
                            s = at % NR
                            if part == 0 and k == 0:
                                pool.wait_ge(flag("staged"), pair * 2 + (t * HEADS + par + 1))
                            pool.wait_ge(slot_free[s], pair * USES + (t * 4 * USES + at // NR + 1))
                            pool.sem_inc(flag("gather_cleared"), 1)
                            pool.indirect_dma_start(
                                rows[:, s, :], None, T[tab],
                                bass.IndirectOffsetOnAxis(ap=stage[:, par, k:k + 1], axis=0),
                            ).then_inc(row_full[s], 16)

            for t in range(TT):
                with pool.Fori(0, 4) as pair:
                    gather_step(t, pair)

            for t in range(3):
                for n in range(2):
                    read_wait(pool, "v2", 3 * n + t)
            pool.wait_ge(flag("in_bias2"), 64)
            pool.tensor_tensor(vtok[0:META, 0, :], vtok[0:META, 0, :], vec[0:META, 0:D], ALU.add)
            pool.tensor_tensor(vtok[:, 1:3, :], vtok[:, 1:3, :], over(vec[:, 0:D], 1, TT),
                               ALU.add).then_inc(flag("v_ready"), 1)
            for i, (nm, dst) in enumerate((("o2", otok), ("gs", gs), ("gm", gm))):
                for j in range(2 * TT):
                    read_wait(pool, nm, j)
                pool.tensor_tensor(dst, dst, over(vec[:, D * (i + 1):D * (i + 2)], 1, TT),
                                   ALU.add).then_inc(flag("gate_biased"), 1)
            pool.drain()
            pool.dma_start(m_norm, rowvec("m_norm_g_2", 0, D)).then_inc(flag("in_ln1"), 16)
            pool.dma_start(ln1_g, rowvec("ln1_g_2", 0, D)).then_inc(flag("in_ln1"), 16)
            pool.dma_start(ln1_b, rowvec("ln1_b_2", 0, D)).then_inc(flag("in_ln1"), 16)
            pool.wait_ge(flag("glu_read"), 1)
            pool.dma_start(ln2_g, rowvec("ln2_g_2", 0, D)).then_inc(flag("in_ln2"), 16)
            pool.dma_start(ln2_b, rowvec("ln2_b_2", 0, D)).then_inc(flag("in_ln2"), 16)

        @block.tensor
        def _(pe):
            used = [0]

            def begin_turn(*u):
                if turn_no[u] >= 2:
                    pe.wait_ge(turn_read, turn_no[u] - 1)
                return turn_bank(*u)

            def transpose_tile(name, t, src, rows_=P, ready=None):
                for q in range(2):
                    bank = begin_turn(name, t, q)
                    if ready and q == 0:
                        pe.wait_ge(*ready)
                    for j in range(4):
                        k = 4 * q + j
                        last = pe.transpose(bank[:, j * rows_:(j + 1) * rows_],
                                            src[:, k * P:(k + 1) * P], ident[0:rows_, 0:rows_])
                    last.then_inc(turned, 1)

            def next_chunk():
                c = used[0]
                used[0] += 1
                pe.wait_ge(ring_full[c % RING], 16 * (c // RING + 1))
                kt, n = CHUNKS[c][3], CHUNKS[c][5]
                return ring[:, c % RING, 0:kt * n].rearrange("p (k n) -> p k n", k=kt)

            def group(name, i, lhs, rhs, kt, m, n):
                g = GROUP_NO[(name, i)]
                if g >= ACC:
                    pe.wait_ge(bank_free[g % ACC], g // ACC)
                for k in range(kt):
                    last = pe.matmul(psum[0:m, g % ACC, 0:n], lhs(k), rhs(k),
                                     start=(k == 0), stop=(k == kt - 1))
                last.then_inc(bank_full[g % ACC], 1)

            def by_token(name, i, t, w, src, n=512, col=0, kt=KD, base=0, m=P):
                group(name, i, lambda k: src[:, k, base + t * P:base + t * P + m],
                      lambda k: w[:, k, col:col + n], kt, m, n)

            def by_feature(name, i, w, m, lo, hi):
                group(name, i, lambda k: w[:, k, m * P:(m + 1) * P], lambda k: featT[:, k, lo:hi],
                      KD, P, hi - lo)

            def ada(i):
                w = next_chunk()
                group("ada", i, lambda k: crep[:, k, :], lambda k: w[:, k, :], KD, P, 512)

            pe.wait_ge(flag("crep_ready"), 1)
            pe.wait_ge(flag("consts"), 1)
            for i in range(4):
                ada(i)

            def tile_by_tile(name, src, ready, products, turn=None, before=None):
                w = {}
                units = 1 if turn else 2

                def tile(t):
                    if turn:
                        turn(t)
                    else:
                        transpose_tile(name, t, src[:, t, :], ready=(flag(ready), t + 1))

                for t in range(TT):
                    if t == 0:
                        tile(0)
                        if before:
                            pe.wait_ge(flag(before), 1)
                    turn_read_wait(pe, name, t, units - 1)
                    for j, (nm, index, n) in enumerate(products):
                        if t == 0:
                            w[j] = next_chunk()
                        by_token(nm, index(t), t, w[j], featT, n=n)
                        if t == 0 and j == 0:
                            tile(1)

            def two_chunks(nm):
                return [(nm, lambda t: t, 512), (nm, lambda t: TT + t, 512)]

            def first_chunk(name, ready, nm):
                w = next_chunk()
                transpose_tile(name, 0, hbuf[:, 0, :], ready=(flag(ready), 1))
                turn_read_wait(pe, name, 0, 1)
                for t in range(TT):
                    lo, hi = t * P, (t + 1) * P
                    for m in range(4):
                        g = GROUP_NO[(nm, m)]
                        if t == 0:
                            pe.wait_ge(bank_free[g % ACC], g // ACC)
                        for k in range(KD):
                            last = pe.matmul(psum[:, g % ACC, lo:hi], w[:, k, m * P:(m + 1) * P],
                                             featT[:, k, lo:hi], start=(k == 0), stop=(k == KD - 1))
                        if t == 0 and m == 2:
                            transpose_tile(name, 1, hbuf[:, 1, :], ready=(flag(ready), 2))
                        if t:
                            last.then_inc(bank_full[g % ACC], 1)
                    if t == 0:
                        turn_read_wait(pe, name, 1, 1)

            tile_by_tile("h1", hbuf, "h1_ready", [("q1", lambda t: t, 512), ("kv1", lambda t: t, 256)])
            for nm in ("cb", "cc", "cu"):
                w = next_chunk()
                for m in range(4):
                    by_feature(nm, m, w, m, 0, SEQ)
            ada(4)
            ada(5)
            pe.wait_ge(flag("rope_done"), 1)
            for t in range(TT):
                bank = begin_turn("qT", t, 0)
                for j in range(QPK):
                    last = pe.transpose(bank[:, j * P:(j + 1) * P],
                                        qkr[:, t, j * P:(j + 1) * P], ident[:, :])
                last.then_inc(turned, 1)
            bank = begin_turn("kT", 0, 0)
            for t in range(TT):
                last = pe.transpose(bank[:, t * P:(t + 1) * P], qkr[:, t, AW:QKW], ident[:, :])
            last.then_inc(turned, 1)
            bank = begin_turn("css", 0, 0)
            pe.wait_ge(flag("conv_sq"), 1)
            for m in range(CT):
                last = pe.matmul(bank[:, 0:SEQ], ones[:, :], hp[:, m, 0:SEQ],
                                 start=(m == 0), stop=(m == CT - 1))
            last.then_inc(turned, 1)
            turn_read_wait(pe, "kT", 0, 0)
            unit = 0
            extra = [6, 7, 8, 9, 10, 11]
            for t in range(TT):
                nk = P * (t + 1)
                for s in range(NKV):
                    if unit:
                        pe.wait_ge(flag("O_read"), unit)
                    for j in range(QPK):
                        last = pe.matmul(psum[:, 6 + j // 2, (j % 2) * 256:(j % 2) * 256 + nk],
                                         qT[64 * s:64 * s + 64, t, j, :], kT[64 * s:64 * s + 64, 0:nk],
                                         start=True, stop=True)
                    last.then_inc(flag("S_full"), 1)
                    for _ in range(2 if unit < 2 else 1):
                        ada(extra.pop(0))
                    pe.wait_ge(flag("exp_done"), unit + 1)
                    for b in range(t + 1):
                        bank = begin_turn("P", t, 2 * s + b)
                        for j in range(QPK):
                            last = pe.transpose(bank[:, j * P:(j + 1) * P],
                                                S[:, j, b * P:(b + 1) * P], ident[:, :])
                        last.then_inc(turned, 1)
                    turn_read_wait(pe, "P", t, 2 * s + t)
                    for j in range(QPK):
                        for b in range(t + 1):
                            last = pe.matmul(psum[:, 6, j * HD:(j + 1) * HD], pT[:, b, j, :],
                                             qkv[:, b, QKW + s * HD:QKW + (s + 1) * HD],
                                             start=(b == 0), stop=(b == t))
                    last.then_inc(flag("O_full"), 1)
                    unit += 1
            def turn_attention(t):
                bank = begin_turn("m", t, 0)
                pe.wait_ge(flag("attn_normed"), t + 1)
                for j in range(4):
                    last = pe.transpose(bank[:, j * P:(j + 1) * P], attn[:, t, j * P:(j + 1) * P],
                                        ident[:, :])
                last.then_inc(turned, 1)

            tile_by_tile("m", None, None, two_chunks("out1"), turn=turn_attention,
                         before="conv_merged")

            def score_step(b):
                for a in range(4 * b, 4 * b + 4):
                    read_wait(pe, "wq", a)
                for t in range(TT):
                    bank = begin_turn("sc", t, b)
                    for j in range(4):
                        last = pe.matmul(bank[:, j * KEYS:(j + 1) * KEYS],
                                         qpT[:, 4 * b + j, t * P:(t + 1) * P], skT[:, 4 * b + j, :],
                                         start=True, stop=True)
                    last.then_inc(turned, 1)

            first_chunk("h2", "h2_ready", "wq")
            pe.wait_ge(flag("in_sk"), 16)
            score_step(0)
            for n in range(1, 4):
                w = next_chunk()
                for m in range(4):
                    by_feature("wq", 4 * n + m, w, m, 0, SEQ)
                    if n > 1 and m == 0:
                        score_step(n - 1)
            score_step(3)

            def sum_step(t, pair, last=False):
                for par in range(2):
                    for j, k in enumerate(tensor_rows(last and par == 1)):
                        at = 32 * par + TOPK + k
                        s = at % NR
                        pe.wait_ge(row_full[s], pair * (16 * USES) + (t * 4 * USES + at // NR + 1) * 16)
                        pe.wait_ge(flag("diag_full"), pair * 32 + (t * 128 + 16 * par + j + 1))
                        for half in range(2):
                            mm = pe.matmul(psum[:, SUM_BANK[t] + half, :], diag[:, j % 8, :],
                                           rows[:, s, 512 * half:512 * (half + 1)],
                                           start=False, stop=False)
                            mm.then_inc((flag("diag_free"), slot_free[s])[half], 1)

            def sum_zero(t, start):
                for half in range(2):
                    mm = pe.matmul(psum[:, SUM_BANK[t] + half, :], zeros[:, :],
                                   hbuf[:, t, 512 * half:512 * (half + 1)], start=start, stop=not start)
                return mm

            in2_chunks = {}

            def tile_columns(nm, t):
                if t == 0:
                    in2_chunks[nm] = next_chunk()
                lo, hi = tile_range(t)
                for m in range(4):
                    by_feature(nm + str(t), m, in2_chunks[nm], m, lo, hi)

            pe.sem_inc(flag("diag_free"), 7)
            for t in range(TT):
                sum_zero(t, True)
                if t == 0:
                    with pe.Fori(0, 4) as pair:
                        sum_step(t, pair)
                else:
                    sum_step(t, 0)
                    transpose_tile("meta", 0, xmeta, rows_=META, ready=(flag("meta_ready"), 1))
                    transpose_tile("h0", 0, hbuf[:, 0, :], ready=(flag("h0_ready"), 1))
                    turn_read_wait(pe, "h0", 0, 1)
                    tile_columns("u", 0)
                    sum_step(t, 1)
                    tile_columns("q2", 0)
                    sum_step(t, 2)
                    sum_step(t, 3, last=True)
                sum_zero(t, False).then_inc(flag("peer_summed"), 1)
            tile_columns("k2", 0)
            transpose_tile("h0", 1, hbuf[:, 1, :], ready=(flag("h0_ready"), 2))
            turn_read_wait(pe, "h0", 1, 1)
            for nm in ("u", "q2", "k2"):
                tile_columns(nm, 1)
            pe.wait_ge(flag("in_if"), 32)
            for c in range(2):
                bank = begin_turn("if", c, 0)
                for k in range(KD):
                    last = pe.matmul(bank[0:MH, 0:LEN], w_if[:, k, MH * c:MH * (c + 1)], featT[:, k, :],
                                     start=(k == 0), stop=(k == KD - 1))
                last.then_inc(turned, 1)

            pe.wait_ge(flag("bd_ready"), 1)
            for c in range(2):
                bank = begin_turn("bd", c, 0)
                for q in range(4):
                    last = pe.transpose(bank[:, q * P:(q + 1) * P], bd[:, c, q * P:(q + 1) * P],
                                        ident[:, :])
                last.then_inc(turned, 1)

            def s5_in(q):
                read_wait(pe, "u1", q)
                turn_read_wait(pe, "bd", 1, 0)
                if q:
                    pe.wait_ge(flag("y_read"), q)
                for i in range(4):
                    for c in range(2):
                        n = 8 * q + 2 * i + c
                        if n >= 2:
                            pe.wait_ge(flag("bu_read"), n - 1)
                        pe.matmul(psum[:, 6 + c, 0:LEN], bdT[32 * i:32 * i + 32, c, q, :],
                                  uT[32 * i:32 * i + 32, q, :], start=True,
                                  stop=True).then_inc(flag("bu_full"), 1)

            def s5_out(q):
                pe.wait_ge(flag("state_ready"), q + 1)
                for i in range(4):
                    for c in range(2):
                        last = pe.matmul(psum[32 * i:32 * i + 32, 6, 0:SEQ], cd[:, c, 4 * q + i, :],
                                         s5t[4 + c][:, i, META:LEN], start=(c == 0), stop=(c == 1))
                last.then_inc(flag("y_full"), 1)

            s5_in(0)
            for n in range(2):
                w = next_chunk()
                by_token("v2", 3 * n, 0, w, featT, m=META)
                for t in range(TT):
                    by_token("v2", 3 * n + 1 + t, t, w, featT, base=META)
            for q, nm in enumerate(("o2", "gs", "gm")):
                s5_out(q)
                s5_in(q + 1)
                for n in range(2):
                    w = next_chunk()
                    for t in range(TT):
                        by_token(nm, TT * n + t, t, w, featT, base=META)
            pe.wait_ge(flag("rows_ready"), 1)
            bank = begin_turn("ga", 0, 0)
            pe.transpose(bank[0:META, 0:MH], row_b[:, 0, 0:META], ident[0:MH, 0:MH])
            for t in range(TT):
                lo = META + t * P
                pe.transpose(bank[:, MH * (1 + t):MH * (2 + t)], row_b[:, 0, lo:lo + P],
                             ident[0:MH, 0:MH])
                last = pe.transpose(bank[:, MH * (3 + t):MH * (4 + t)], row_b[:, 2, lo:lo + P],
                                    ident[0:MH, 0:MH])
            last.then_inc(turned, 1)
            s5_out(3)
            pe.wait_ge(flag("y_read"), 4)
            for h in range(MH):
                last = pe.matmul(psum[:, 6 + h // 2, (h % 2) * SEQ:(h % 2 + 1) * SEQ],
                                 ident[0:MH, h:h + 1].broadcast_to([MH, P]), row_b[:, 1, META:LEN],
                                 start=True, stop=True)
            last.then_inc(flag("mbc_full"), 1)

            def glu(z, n, w):
                for t in range(TT):
                    by_token("glu", 4 * z + 2 * n + t, t, w, gyT, col=512 * n, kt=4)

            pe.wait_ge(flag("gy_ready"), 4)
            w = next_chunk()
            glu(0, 0, w)
            pe.wait_ge(flag("conv2_done"), 1)
            n = 0
            for b in range(3):
                nr = META if b == 0 else P
                lo = 0 if b == 0 else META + (b - 1) * P
                for hh in range(2):
                    if n < 2:
                        pe.wait_ge(flag("mbc_read"), 1)
                    else:
                        pe.wait_ge(flag("st_read"), n - 1)
                    for h in (2 * hh, 2 * hh + 1):
                        last = pe.matmul(psum[0:nr, 6 + n % 2, (h % 2) * SEQ:(h % 2 + 1) * SEQ],
                                         qkT[:, MH + h, lo:lo + nr], qkT[:, h, META:LEN],
                                         start=True, stop=True)
                    last.then_inc(flag("st_full"), 1)
                    n += 1
            glu(0, 1, w)
            pe.wait_ge(flag("PT_ready"), 1)
            pe.wait_ge(flag("v_ready"), 1)

            def key_tiles(t):
                return [(b, META if b == 0 else P) for b in range(t + 2)]

            bank = begin_turn("den", 0, 0)
            for t in range(TT):
                for h in range(MH):
                    for b, nr in key_tiles(t):
                        last = pe.matmul(bank[:, MH * t + h:MH * t + h + 1],
                                         PT[0:nr, b, h, t * P:(t + 1) * P], ones[0:nr, 0:1],
                                         start=(b == 0), stop=(b == t + 1))
            last.then_inc(turned, 1)
            n = 0
            for t in range(TT):
                for hh in range(2):
                    if n < 2:
                        pe.wait_ge(flag("st_read"), 6)
                    else:
                        pe.wait_ge(flag("num_read"), n - 1)
                    for h in (2 * hh, 2 * hh + 1):
                        for b, nr in key_tiles(t):
                            last = pe.matmul(psum[:, 6 + n % 2, (h % 2) * DV:(h % 2 + 1) * DV],
                                             PT[0:nr, b, h, t * P:(t + 1) * P],
                                             vtok[0:nr, b, h * DV:(h + 1) * DV],
                                             start=(b == 0), stop=(b == t + 1))
                    last.then_inc(flag("num_full"), 1)
                    n += 1
            w = next_chunk()
            glu(1, 0, w)
            glu(1, 1, w)
            tile_by_tile("hm", hm, "hm_ready", two_chunks("mo"))
            tile_by_tile("mix", gs, "mix_ready", two_chunks("wo"))
            first_chunk("hb", "hb_ready", "up")
            for n in range(1, 8):
                w = next_chunk()
                for m in range(4):
                    by_feature("up", 4 * n + m, w, m, 0, SEQ)
            for n in range(8):
                w = next_chunk()
                pe.wait_ge(flag("ff_ready"), n + 1)
                for t in range(TT):
                    for half in range(2):
                        for k in range(4):
                            last = pe.matmul(psum[:, 4 + 2 * t + half, :],
                                             ffT[:, 4 * n + k, t * P:(t + 1) * P],
                                             w[:, k, 512 * half:512 * (half + 1)],
                                             start=(n == 0 and k == 0), stop=(n == 7 and k == 3))
                    if n == 7 and t == 0:
                        last.then_inc(flag("down_first"), 1)
                last.then_inc(flag("down_used"), 1)
        @block.scalar
        def _(act):
            def load(dst, src, name):
                act.dma_start(dst, src).then_inc(flag(name), 16)

            load(pack[:, :], T["pack"], "in_pack")
            load(xres[:, :, :], T["x"].rearrange("(t p) n -> p t n", p=P), "in_x")
            load(modr[:, 0:2 * D], rowvec("ada_b", 0, 2 * D), "in_mod")
            load(pos_i[:, :], T["positions"], "in_pos")
            load(A1, rowvec("norm1_g", 0, D), "in_n1")
            load(qg, rowvec("q_norm_g", 0, HD), "in_vec")
            load(kg, rowvec("k_norm_g", 0, HD), "in_vec")
            load(sinks, rowvec("sinks", 0, NQ), "in_vec")

            act.wait_ge(flag("in_pack"), 16)
            act.activation(c_act, pk("c"), ACT.Silu).then_inc(flag("c_act"), 1)

            def root(dst, src, n, eps, name):
                act.activation(dst, src, ACT.Sqrt, scale=1.0 / n, bias=eps).then_inc(flag(name), 1)

            def row_root(src, t, scratch, n, name):
                act.activation(scratch, src, ACT.Square, accum_out=ss[:, t:t + 1])
                act.drain()
                root(sd[:, t:t + 1], ss[:, t:t + 1], n, eps_c, name)
                act.drain()

            act.wait_ge(flag("in_x"), 16)
            act.wait_ge(flag("consts"), 1)
            for t in range(TT):
                row_root(xres[:, t, :], t, junk_a, D, "n1_sd")
            act.wait_ge(flag("rope_reduced"), 1)
            act.activation(rope_t[:, 0:2, :, :], rope_t[:, 0:2, :, :], ACT.Sin).then_inc(
                flag("rope_tab"), 1)

            def read_turn(dst, src, *u, func=None, **kw):
                turn_wait(act, *u)
                ins = act.activation(dst, src, func, **kw) if func else act.copy(dst, src)
                ins.then_inc(turn_read, 1)

            def to_features(name, t, lo, width=P):
                for q in range(2):
                    src = turn_bank(name, t, q)[:, 0:4 * width].rearrange("p (j n) -> p j n", j=4)
                    read_turn(featT[:, 4 * q:4 * q + 4, lo:lo + width], src, name, t, q)

            def read_group(dst, name, i, n=512, m=P, func=None, **kw):
                group_wait(act, name, i)
                src = bank_of(name, i)[0:m, 0:n]
                ins = act.activation(dst, src, func, **kw) if func else act.copy(dst, src)
                read_out(ins, name, i)

            for t in range(TT):
                to_features("h1", t, t * P)
            load(modr[:, 2 * D:], rowvec("ada_b", 2 * D, 6 * D), "in_mod2")
            load(A2, rowvec("norm2_g", 0, D), "in_vec2")
            load(attn_g, rowvec("attn_out_g", 0, AW), "in_vec2")
            load(skT, T["subkeys"], "in_sk")
            load(w_if[:, :, :], T["w_if"], "in_if")
            load(b_if[:, :], T["b_if"], "in_if")
            load(s5_dt[:, :], T["log_dt"], "in_dt")
            for t in range(TT):
                read_group(qkv[:, t, 0:AW], "q1", t)
            for t in range(TT):
                read_group(qkv[:, t, AW:768], "kv1", t, n=256)
            for m in range(CT):
                read_group(cbT[:, m, :], "cb", m, n=SEQ)
            for m in range(CT):
                read_group(hp[:, m, 2:2 + SEQ], "cc", m, n=SEQ)
            act.wait_ge(flag("qk_ss"), 1)
            root(qrs, qss, HD, eps_c, "qk_sd")
            for t in range(TT):
                src = turn_bank("qT", t, 0).rearrange("p (j n) -> p j n", j=QPK)
                read_turn(qT[:, t, :, :], src, "qT", t, 0)
            read_turn(kT, turn_bank("kT", 0, 0)[:, 0:SEQ], "kT", 0, 0)
            read_turn(css, turn_bank("css", 0, 0)[:, 0:SEQ], "css", 0, 0, func=ACT.Sqrt,
                      scale=1.0 / CW, bias=eps_c)

            def read_attention(t):
                src = turn_bank("m", t, 0).rearrange("p (j n) -> p j n", j=4)
                read_turn(featT[:, 0:4, t * P:(t + 1) * P], src, "m", t, 0)

            unit = 0
            for t in range(TT):
                nk = P * (t + 1)
                for s in range(NKV):
                    act.wait_ge(flag("S_shifted"), unit + 1)
                    act.activation(S[:, :, 0:nk], S[:, :, 0:nk], ACT.Exp)
                    act.activation(esink, esink, ACT.Exp).then_inc(flag("exp_done"), 1)
                    for b in range(t + 1):
                        src = turn_bank("P", t, 2 * s + b).rearrange("p (j n) -> p j n", j=QPK)
                        read_turn(pT[:, b, :, :], src, "P", t, 2 * s + b)
                    unit += 1
                if t:
                    read_attention(0)
                act.wait_ge(flag("attn_done"), t + 1)
                row_root(attn[:, t, :], t, junk_a[:, 0:AW], AW, "at_sd")
            read_attention(1)
            for t in range(TT):
                act.wait_ge(flag("x1_ready"), t + 1)
                row_root(xres[:, t, :], t, junk_a, D, "n2_sd")
                to_features("h2", t, t * P)

            def read_scores(b):
                for t in range(TT):
                    m = 4 * t + b
                    read_turn(sc[:, 512 * m:512 * (m + 1)], turn_bank("sc", t, b), "sc", t, b)

            def stage_first(m):
                act.wait_ge(flag("routed"), m + 1)
                act.copy(stage[:, 0, :], next_idx[:, 0:TOPK]).then_inc(flag("staged"), 1)

            for a in range(HP):
                read_group(qpT[:, a, :], "wq", a, n=SEQ)
                if a == 3:
                    read_scores(0)
                if a >= 8 and a % 4 == 0:
                    read_scores(a // 4 - 1)
                if a == 6:
                    act.wait_ge(flag("top_shifted"), 1)
                    act.activation(top, top, ACT.Exp).then_inc(flag("top_exp"), 1)
                if a == 8:
                    stage_first(0)
            read_scores(3)

            def turn_tables():
                act.wait_ge(flag("turn_args"), 1)
                act.activation(turn_a, turn_ang_a, ACT.Sin)
                act.activation(turn_b[0], turn_ang_b[:, 0, :, :], ACT.Sin)
                act.activation(turn_b[1], turn_ang_b[:, 1, :, :], ACT.Sin).then_inc(flag("turn_tab"), 1)

            def expert_step(t, pair, more, between=None):
                h = pair * 2 + t * HEADS
                for par in range(2):
                    act.wait_ge(flag("dots_ready"), h + (par + 1))
                    act.activation(gel[:, :], dots[:, :], ACT.Gelu_apprx_tanh).then_inc(
                        flag("gel_ready"), 1)
                    if par == 0:
                        act.copy(stage[:, 1, :], next_idx[:, TOPK:2 * TOPK]).then_inc(flag("staged"), 1)
                    act.wait_ge(flag("wgt_ready"), h + (par + 1))
                    for j, k in enumerate(tensor_rows(par == 1 and not more)):
                        act.wait_ge(flag("diag_free"), pair * 32 + (t * 128 + 16 * par + j + 1))
                        act.activation(diag[:, j % 8, :], ident[:, :], ACT.Copy,
                                       scale=wgt[:, k:k + 1]).then_inc(flag("diag_full"), 1)
                    if par == 0 and more:
                        act.wait_ge(flag("top_shifted"), pair + (4 * t + 2))
                        act.activation(top, top, ACT.Exp).then_inc(flag("top_exp"), 1)
                    if par == 0 and between:
                        between()
                    if par == 1 and more:
                        stage_first(pair + (4 * t + 1))

            def ln_root(t, name, rows_=P, at=None):
                act.wait_ge(flag(name + "_var"), t + 1)
                at = t if at is None else at
                act.activation(sd[0:rows_, t:t + 1], mv[0:rows_, at, 1:2], ACT.Sqrt,
                               bias=ln_eps_c[0:rows_, :]).then_inc(flag(name + "_sd"), 1)

            def read_columns(nm, t, m):
                lo, hi = tile_range(t)
                if nm == "u":
                    dst = uT[:, m, lo:hi]
                else:
                    dst = qk_in[:, (0 if nm == "q2" else 4) + m, 3 + lo:3 + hi]
                at = 4 * ("u", "q2", "k2").index(nm) + m
                group_wait(act, nm + str(t), m)
                read_out(act.activation(dst, bank_of(nm + str(t), m)[:, 0:hi - lo], ACT.Identity,
                                        bias=pk("b_uqk")[:, at:at + 1]), nm + str(t), m)

            with act.Fori(0, 3) as pair:
                expert_step(0, pair, True)
            expert_step(0, 3, True)
            expert_step(1, 0, True)
            ln_root(0, "me", META, TT)
            ln_root(0, "l0")
            to_features("meta", 0, 0, META)
            to_features("h0", 0, META)
            for m in range(4):
                read_columns("u", 0, m)
            expert_step(1, 1, True)
            for m in range(4):
                read_columns("q2", 0, m)
            act.wait_ge(flag("in_dt"), 16)
            act.activation(s5_dt[:, :], s5_dt[:, :], ACT.Exp).then_inc(flag("s5_dt_exp"), 1)
            expert_step(1, 2, True)
            act.wait_ge(flag("s5_args"), 1)
            act.activation(mag, lr, ACT.Exp)
            act.activation(cosv, thc, ACT.Sin)
            act.activation(sinv, thk, ACT.Sin).then_inc(flag("s5_tab"), 1)
            expert_step(1, 3, False, turn_tables)
            ln_root(1, "l0")
            for m in range(4):
                read_columns("k2", 0, m)
            to_features("h0", 1, META + P)
            for m in range(4):
                read_columns("u", 1, m)
            for nm in ("q2", "k2"):
                for m in range(4):
                    read_columns(nm, 1, m)
            act.wait_ge(flag("in_if"), 32)
            for c in range(2):
                read_turn(row_a[:, c, :], turn_bank("if", c, 0)[0:MH, 0:LEN], "if", c, 0,
                          func=ACT.Identity, bias=b_if[:, c:c + 1])

            for c in range(2):
                read_turn(bdT[:, c, :, :], turn_bank("bd", c, 0).rearrange("p (q n) -> p q n", q=4),
                          "bd", c, 0)

            def s5_read(q):
                if q:
                    act.wait_ge(flag("state_ready"), q)
                for i in range(4):
                    for c in range(2):
                        act.wait_ge(flag("bu_full"), 8 * q + 2 * i + c + 1)
                        act.copy(s5t[6 + c][:, i, :], psum[:, 6 + c, 0:LEN]).then_inc(flag("bu_read"), 1)

            def gelu_y(q):
                act.wait_ge(flag("y_read"), q + 1)
                act.activation(gyT[:, q, :], gyT[:, q, :], ACT.Gelu_apprx_tanh).then_inc(
                    flag("gy_ready"), 1)

            def read_tokens(name, dst):
                for n in range(2):
                    for t in range(TT):
                        read_group(dst[:, t, 512 * n:512 * (n + 1)], name, TT * n + t)

            s5_read(0)
            for n in range(2):
                for t in range(3):
                    m = META if t == 0 else P
                    read_group(vtok[0:m, t, 512 * n:512 * (n + 1)], "v2", 3 * n + t, m=m)
            s5_read(1)
            act.wait_ge(flag("conv2_y"), 1)
            for m in range(8):
                last = act.activation(qkT[:, m, :], qkT[:, m, :], ACT.Silu, bias=pk("qk_b")[:, m:m + 1])
            last.then_inc(flag("conv2_done"), 1)
            turn_read_wait(act, "if", 1, 0)
            act.activation(row_a[:, 2, :], row_a[:, 1, :], ACT.Abs)
            act.drain()
            act.activation(row_a[:, 2, :], row_a[:, 2, :], ACT.Exp, scale=-1.0)
            act.drain()
            act.activation(row_a[:, 2, :], row_a[:, 2, :], ACT.Ln, bias=1.0).then_inc(flag("ln_done"), 1)
            read_tokens("o2", otok)
            s5_read(2)
            gelu_y(0)
            gelu_y(1)
            read_tokens("gs", gs)
            s5_read(3)
            gelu_y(2)
            read_tokens("gm", gm)
            turn_wait(act, "ga", 0, 0)
            act.copy(gcol[0:META, 0:MH], turn_bank("ga", 0, 0)[0:META, 0:MH])
            act.copy(gcol[:, MH:5 * MH], turn_bank("ga", 0, 0)[:, MH:5 * MH]).then_inc(turn_read, 1)
            act.drain()
            act.activation(enm, gcol[:, 3 * MH:5 * MH], ACT.Exp, scale=-1.0).then_inc(flag("enm"), 1)
            gelu_y(3)
            act.wait_ge(flag("E_args"), 1)
            act.activation(PT[0:META, 0, :, :], PT[0:META, 0, :, :], ACT.Exp)
            act.activation(PT[:, 1, :, :], PT[:, 1, :, :], ACT.Exp)
            act.activation(PT[:, 2, :, P:SEQ], PT[:, 2, :, P:SEQ], ACT.Exp).then_inc(flag("E_exp"), 1)
            for i, dst in enumerate((otok, gs, gm)):
                act.wait_ge(flag("gate_biased"), i + 1)
                act.activation(dst, dst, ACT.Sigmoid).then_inc(flag("gate_sig"), 1)
            def read_glu(z):
                for n in range(2):
                    for t in range(TT):
                        dst = (xres, tmp2)[z][:, t, 512 * n:512 * (n + 1)]
                        read_group(dst, "glu", 4 * z + 2 * n + t, func=(None, ACT.Sigmoid)[z])

            read_glu(0)
            read_turn(dens, turn_bank("den", 0, 0)[:, 0:2 * MH], "den", 0, 0)
            for t in range(TT):
                act.wait_ge(flag("hv_var"), t + 1)
                act.activation(hrs[:, MH * t:MH * (t + 1)], hmv[:, MH * t:MH * (t + 1), 1], ACT.Sqrt,
                               bias=ln_eps_c).then_inc(flag("hv_sd"), 1)
            read_glu(1)
            act.drain().then_inc(flag("glu_read"), 1)
            for t in range(TT):
                to_features("hm", t, t * P)
            for t in range(TT):
                to_features("mix", t, t * P)
            for t in range(TT):
                ln_root(t, "l1")
                to_features("hb", t, t * P)
            for k in range(FF // P):
                read_group(ffT[:, k, :], "up", k, n=SEQ, func=ACT.Relu, bias=pk("b_up")[:, k:k + 1])
            for t in range(TT):
                ln_root(t, "l2")

        @block.vector
        def _(dve):
            def tt(o, a, b, op):
                return dve.tensor_tensor(o, a, b, op)

            def ts(o, a, s1, s2=None, op0=ALU.mult, op1=None):
                if op1 is None:
                    return dve.tensor_scalar(o, a, s1, None, op0)
                return dve.tensor_scalar(o, a, s1, s2, op0, op1)

            def stt(o, a, s, b, op0=ALU.mult, op1=ALU.add):
                return dve.scalar_tensor_tensor(out=o, in0=a, scalar=s, in1=b, op0=op0, op1=op1)

            def reduced_rest(dst, k_f, quarter=0):
                stt(dst, k_f, -C2, dst)
                dve.drain()
                stt(dst, k_f, -C3, dst)
                dve.drain()
                ts(dst, dst, 0.5 * math.pi * quarter, PI_IN, ALU.add, ALU.min)
                dve.drain()
                return ts(dst, dst, -PI_IN, None, ALU.max)

            def reduce_angle(dst, ang, k_i, k_f, quarter=0):
                ts(k_i, ang, 1.0 / TWO_PI, 0.25 * quarter, ALU.mult, ALU.add)
                dve.drain()
                dve.tensor_copy(k_f, k_i)
                dve.drain()
                stt(dst, k_f, -C1, ang)
                dve.drain()
                return reduced_rest(dst, k_f, quarter)

            def inverse_root(name, t, rows_=P):
                dve.wait_ge(flag(name + "_sd"), t + 1)
                dve.reciprocal(rs[0:rows_, t:t + 1], sd[0:rows_, t:t + 1])
                dve.drain()

            dve.wait_ge(flag("c_act"), 1)
            dve.tensor_copy(crep, over(c_act, 2, P)).then_inc(flag("crep_ready"), 1)
            dve.wait_ge(flag("in_pos"), 16)
            dve.wait_ge(flag("consts"), 1)
            dve.tensor_copy(st[:, 74:76], pos_i[:, :])
            dve.memset(hp[:, :, 0:2], 0.0)
            dve.drain()
            for t in range(TT):
                ts(rope_t[:, 2, t, :], inv_freq[:, :], st[:, 74 + t:75 + t])
            dve.drain()
            k_i = junk[:, 0:64].bitcast(I32).rearrange("p (t n) -> p t n", t=TT)
            reduce_angle(rope_t[:, 1, :, :], rope_t[:, 2, :, :], k_i, rope_t[:, 3, :, :])
            dve.drain()
            reduce_angle(rope_t[:, 0, :, :], rope_t[:, 2, :, :], k_i, rope_t[:, 3, :, :],
                         quarter=1).then_inc(flag("rope_reduced"), 1)

            def add_mod(i):
                group_wait(dve, "ada", i)
                if i == 0:
                    dve.wait_ge(flag("in_mod"), 16)
                if i == 4:
                    dve.wait_ge(flag("in_mod2"), 16)
                sl = modr[:, 512 * i:512 * (i + 1)]
                read_out(tt(sl, sl, bank_of("ada", i), ALU.add), "ada", i)

            for t in range(TT):
                inverse_root("n1", t)
            dve.wait_ge(flag("in_n1"), 16)
            for i in range(4):
                add_mod(i)
                if i >= 2:
                    dve.drain()
                    sl = slice(512 * (i - 2), 512 * (i - 1))
                    stt(A1[:, sl], scale1[:, sl], 1.0, A1[:, sl], ALU.add, ALU.mult)
            dve.drain()

            def modulated(t, gain, shift, name):
                stt(hbuf[:, t, :], xres[:, t, :], rs[:, t:t + 1], gain, ALU.mult, ALU.mult)
                dve.drain()
                tt(hbuf[:, t, :], hbuf[:, t, :], shift, ALU.add).then_inc(flag(name), 1)

            for t in range(TT):
                modulated(t, A1, shift1, "h1_ready")
            dve.wait_ge(flag("in_vec"), 16 * 3)

            for t in range(TT):
                read_wait(dve, "q1", t)
                read_wait(dve, "kv1", t)
            for t in range(TT):
                sq = junk[:, 0:QKW]
                tt(sq, qkv[:, t, 0:QKW], qkv[:, t, 0:QKW], ALU.mult)
                dve.drain()
                dve.tensor_reduce(qss[:, 10 * t:10 * t + 10],
                                  sq.rearrange("p (h d) -> p h d", d=HD), X, ALU.add)
                dve.drain()
            dve.engine_nop().then_inc(flag("qk_ss"), 1)
            dve.wait_ge(flag("qk_sd"), 1)
            dve.reciprocal(qrs, qrs)
            dve.wait_ge(flag("rope_tab"), 1)
            dve.drain()
            for t in range(TT):
                v = qkv[:, t, 0:QKW].rearrange("p (h d) -> p h d", d=HD)
                o = qkr[:, t, :].rearrange("p (h d) -> p h d", d=HD)
                tt(v, v, over(qrs[:, 10 * t:10 * t + 10], 2, HD), ALU.mult)
                dve.drain()
                tt(v[:, 0:NQ, :], v[:, 0:NQ, :], over(qg, 1, NQ), ALU.mult)
                tt(v[:, NQ:10, :], v[:, NQ:10, :], over(kg, 1, NKV), ALU.mult)
                dve.drain()
                x1, x2 = v[:, :, 0:32], v[:, :, 32:64]
                cos, sin = over(rope_t[:, 0, t, :], 1, 10), over(rope_t[:, 1, t, :], 1, 10)
                tt(rp[:, 0, 0:10, :], x1, cos, ALU.mult)
                tt(rp[:, 1, 0:10, :], x2, sin, ALU.mult)
                tt(rp[:, 0, 10:20, :], x2, cos, ALU.mult)
                tt(rp[:, 1, 10:20, :], x1, sin, ALU.mult)
                dve.drain()
                oq = qkr[:, t, 0:AW].rearrange("p (j s d) -> p s j d", s=NKV, d=HD)
                for lo, at, op in ((0, 0, ALU.subtract), (32, 10, ALU.add)):
                    a, b = (rp[:, i, at:at + NQ, :].rearrange("p (s j) d -> p s j d", s=NKV)
                            for i in range(2))
                    tt(oq[:, :, :, lo:lo + 32], a, b, op)
                    tt(o[:, NQ:10, lo:lo + 32], rp[:, 0, at + NQ:at + 10, :],
                       rp[:, 1, at + NQ:at + 10, :], op)
                dve.drain()
            dve.engine_nop().then_inc(flag("rope_done"), 1)

            for m in range(CT):
                read_wait(dve, "cc", m)
                read_wait(dve, "cb", m)
                group_wait(dve, "cu", m)
                sl = hp[:, m, 2:2 + SEQ]
                read_out(tt(sl, sl, bank_of("cu", m)[:, 0:SEQ], ALU.mult), "cu", m)
            dve.drain()
            w = pk("conv_w").rearrange("p (k m) -> p k m", k=3)
            for m in range(CT):
                ts(cy[:, m, :], hp[:, m, 0:SEQ], w[:, 0, m:m + 1])
            for k in (1, 2):
                dve.drain()
                for m in range(CT):
                    stt(cy[:, m, :], hp[:, m, k:k + SEQ], w[:, k, m:m + 1], cy[:, m, :])
            dve.drain()
            tt(cy, cy, cbT, ALU.mult)
            dve.drain()
            tt(hp[:, :, 0:SEQ], cy, cy, ALU.mult).then_inc(flag("conv_sq"), 1)
            add_mod(4)
            add_mod(5)

            def merge_convolution():
                turn_read_wait(dve, "css", 0, 0)
                dve.reciprocal(css, css)
                dve.drain()
                for m in range(CT):
                    last = stt(featT[:, CT + m, 0:SEQ], cy[:, m, :], pk("conv_g")[:, m:m + 1], css,
                               ALU.mult, ALU.mult)
                last.then_inc(flag("conv_merged"), 1)

            def attention_norm(t):
                inverse_root("at", t)
                if t == 0:
                    dve.wait_ge(flag("in_vec2"), 32)
                stt(attn[:, t, :], attn[:, t, :], rs[:, t:t + 1], attn_g, ALU.mult,
                    ALU.mult).then_inc(flag("attn_normed"), 1)

            unit = 0
            extra = [6, 7, 8, 9, 10, 11]
            for t in range(TT):
                nk = P * (t + 1)
                mk = mask[:, 1 - t:2, :].rearrange("p b k -> p (b k)")
                for s in range(NKV):
                    dve.wait_ge(flag("S_full"), unit + 1)
                    sp4 = psum[:, 6:8, :].rearrange("p b (j k) -> p (b j) k", j=2)[:, :, 0:nk]
                    Sv = S[:, :, 0:nk]
                    stt(Sv, sp4, HD ** -0.5, over(mk, 1, QPK))
                    dve.drain()
                    dve.tensor_reduce(rmax, Sv, X, ALU.max)
                    dve.drain()
                    tt(rmax, rmax, sinks[:, 4 * s:4 * s + 4], ALU.max)
                    dve.drain()
                    tt(esink, sinks[:, 4 * s:4 * s + 4], rmax, ALU.subtract)
                    tt(Sv, Sv, over(rmax, 2, nk), ALU.subtract).then_inc(flag("S_shifted"), 1)
                    if unit == 2:
                        merge_convolution()
                        attention_norm(0)
                    for _ in range(2 if unit < 2 else 1):
                        add_mod(extra.pop(0))
                    dve.wait_ge(flag("exp_done"), unit + 1)
                    dve.tensor_reduce(den4, Sv, X, ALU.add)
                    dve.drain()
                    tt(den4, den4, esink, ALU.add)
                    dve.drain()
                    dve.reciprocal(den4, den4)
                    dve.drain()
                    dve.wait_ge(flag("O_full"), unit + 1)
                    tt(attn[:, t, 256 * s:256 * s + 256].rearrange("p (j d) -> p j d", j=QPK),
                       psum[:, 6, 0:256].rearrange("p (j d) -> p j d", j=QPK),
                       over(den4, 2, HD), ALU.mult).then_inc(flag("O_read"), 1)
                    turn_read_wait(dve, "P", t, 2 * s + t)
                    unit += 1
                dve.drain().then_inc(flag("attn_done"), 1)
            attention_norm(1)
            stt(A2, scale2, 1.0, A2, ALU.add, ALU.mult)
            for t in range(TT):
                for n in range(2):
                    i = TT * n + t
                    group_wait(dve, "out1", i)
                    part = junk[:, 512 * (i % 2):512 * (i % 2 + 1)]
                    read_out(tt(part, bank_of("out1", i), gate1[:, 512 * n:512 * (n + 1)], ALU.mult),
                             "out1", i)
                    dve.drain()
                    sl = xres[:, t, 512 * n:512 * (n + 1)]
                    tt(sl, sl, part, ALU.add)
                    dve.drain()
                dve.engine_nop().then_inc(flag("x1_ready"), 1)
                inverse_root("n2", t)
                modulated(t, A2, shift2, "h2_ready")
            dve.drain()

            def top16(src, v, i_):
                n = range(len(src))
                for lo in (0, 8):
                    for a in n:
                        dve.max(v[a][:, lo:lo + 8], src[a])
                    dve.drain()
                    for a in n:
                        dve.max_index(i_[a][:, lo:lo + 8], v[a][:, lo:lo + 8], src[a])
                    if lo == 0:
                        for a in n:
                            dve.match_replace(src[a], v[a][:, 0:8], src[a], LOWEST)
                    dve.drain()

            def route_values(m):
                dve.tensor_copy(scs.rearrange("p a k -> p (a k)"), sc[:, bass.ds(m * 512, 512)]
                                if not isinstance(m, int) else sc[:, 512 * m:512 * (m + 1)])
                dve.drain()
                top16([scs[:, a, :] for a in range(4)], [vals[:, a, :] for a in range(4)],
                      [ids_u[:, a, :] for a in range(4)])
                v4 = vals.rearrange("p (h s) k -> p h s k", s=2)
                c4 = cand.rearrange("p h (a b) -> p h a b", a=TOPK)
                tt(c4, over(v4[:, :, 0, :], 3, TOPK), over(v4[:, :, 1, :], 2, TOPK), ALU.add)
                dve.tensor_copy(ids_f.rearrange("p h s k -> p (h s) k"), ids_u)
                dve.drain()
                top16([cand[:, h, :] for h in range(2)], [top[:, h, :] for h in range(2)],
                      [pos_u[:, h, :] for h in range(2)])
                dve.tensor_copy(rsm[:, 0:2].unsqueeze(2), top[:, :, 0:1])
                dve.drain()
                tt(top, top, over(rsm[:, 0:2], 2, TOPK), ALU.subtract).then_inc(flag("top_shifted"), 1)

            def route_numbers(m):
                pf = pos_u.rearrange("p h k -> p (h k)")
                ts(ab_u[:, 0, :], pf, 4, None, ALU.logical_shift_right)
                ts(ab_u[:, 1, :], pf, TOPK - 1, None, ALU.bitwise_and)
                dve.drain()
                dve.tensor_copy(ab_f, ab_u)
                dve.drain()
                for s in range(2):
                    oh = onehot.rearrange("p (n a) -> p n a", a=TOPK)
                    tt(oh, over(ab_f[:, s, :], 2, TOPK), over(iota16[:, :], 1, 2 * TOPK), ALU.is_equal)
                    dve.drain()
                    oh4 = onehot.rearrange("p (h j a) -> p h j a", h=2, a=TOPK)
                    tt(oh4, oh4, over(ids_f[:, :, s, :], 2, TOPK), ALU.mult)
                    dve.drain()
                    dve.tensor_reduce(pick[:, s, :], oh, X, ALU.add)
                    dve.drain()
                stt(next_idx[:, :], pick[:, 0, :], float(KEYS), pick[:, 1, :])
                dve.wait_ge(flag("top_exp"), m + 1)
                dve.tensor_reduce(rsm[:, 2:4], top, X, ALU.add)
                dve.drain()
                dve.reciprocal(rsm[:, 2:4], rsm[:, 2:4])
                dve.drain()
                tt(next_gate[:, :].rearrange("p (h k) -> p h k", h=2), top,
                   over(rsm[:, 2:4], 2, TOPK), ALU.mult)
                dve.drain().then_inc(flag("routed"), 1)

            def expert_step(t, pair, next_m=None, first_turn=None, between=None):
                for par in range(2):
                    for k in range(TOPK):
                        at = 32 * par + k
                        s = at % NR
                        dve.wait_ge(row_full[s], pair * (16 * USES) + (t * 4 * USES + at // NR + 1) * 16)
                        dve.tensor_tensor_reduce(rows[:, s, :], rows[:, s, :], hbuf[:, t, :], 1.0,
                                                 0.0, ALU.mult, ALU.add,
                                                 dots[:, k:k + 1]).then_inc(slot_free[s], 1)
                    dve.drain().then_inc(flag("dots_ready"), 1)
                    dve.wait_ge(flag("gel_ready"), pair * 2 + (t * HEADS + par + 1))
                    tt(wgt[:, :], next_gate[:, TOPK * par:TOPK * (par + 1)], gel[:, :],
                       ALU.mult).then_inc(flag("wgt_ready"), 1)
                    if next_m is not None and par == 0:
                        dve.wait_ge(turn_read, first_turn)
                        route_values(next_m)
                    if between and par == 0:
                        between()
                    if next_m is not None and par == 1:
                        route_numbers(next_m)

            first_sc = turn_no[("sc", 0, 0)]
            all_sc = turn_no[("sc", TT - 1, 3)] + 1
            turn_read_wait(dve, "sc", 0, 0)
            route_values(0)
            route_numbers(0)
            for s in range(NR):
                dve.engine_nop().then_inc(slot_free[s], 1)

            def variance(src, t, name, rows_=P, at=None):
                at = t if at is None else at
                if src is not None:
                    for half in range(2):
                        dve.bn_stats(bn[0:rows_, t, half, :], src[:, 512 * half:512 * (half + 1)])
                dve.drain()
                dve.bn_aggr(mv[0:rows_, at, :], bn[0:rows_, t, :, :]).then_inc(flag(name + "_var"), 1)

            def normalise(dst, src, t, g, b, name, ready=None, rows_=P, at=None):
                at = t if at is None else at
                dve.drain()
                stt(dst, src, mv[0:rows_, at, 0:1], g, ALU.subtract, ALU.mult)
                inverse_root(name, t, rows_)
                last = stt(dst, dst, rs[0:rows_, t:t + 1], b)
                if ready:
                    last.then_inc(flag(ready), 1)

            def second_input(t):
                dve.wait_ge(flag("peer_summed"), t + 1)
                for half in range(2):
                    sl = slice(512 * half, 512 * (half + 1))
                    tt(peer_out[:, sl], psum[:, SUM_BANK[t] + half, :], gate2[:, sl], ALU.mult)
                dve.drain()
                tt(xres[:, t, :], xres[:, t, :], peer_out, ALU.add)
                dve.drain()
                variance(xres[:, t, :], t, "l0")
                normalise(hbuf[:, t, :], xres[:, t, :], t, ln0_g, ln0_b, "l0", "h0_ready")

            lre, lim = pk("lam_re"), pk("lam_im")

            def s5_arguments():
                dve.wait_ge(flag("s5_dt_exp"), 1)
                tt(lr, lre, s5_dt[:, :], ALU.mult)
                tt(th, lim, s5_dt[:, :], ALU.mult)
                dve.drain()
                reduce_angle(thk, th, s5k, ta)
                dve.drain()
                reduce_angle(thc, th, s5k, ta, quarter=1).then_inc(flag("s5_args"), 1)
                tt(n2, lre, lre, ALU.mult)
                tt(tb, lim, lim, ALU.mult)
                dve.drain()
                tt(n2, n2, tb, ALU.add)
                dve.drain()
                dve.reciprocal(n2, n2)

            def s5_inputs():
                dve.wait_ge(flag("s5_tab"), 1)
                tt(lbr, mag, cosv, ALU.mult)
                tt(lbi, mag, sinv, ALU.mult)
                dve.tensor_copy(s5_mag[:, :], mag)
                dve.tensor_copy(s5_th[:, :], thk)
                dve.drain()
                ts(lbr, lbr, -1.0, None, ALU.add)
                dve.drain()
                tt(ta, lbr, lre, ALU.mult)
                tt(tb, lbi, lim, ALU.mult)
                tt(ts_, lbi, lre, ALU.mult)
                dve.drain()
                tt(fr, ta, tb, ALU.add)
                dve.drain()
                tt(ta, lbr, lim, ALU.mult)
                dve.drain()
                tt(fi, ts_, ta, ALU.subtract)
                tt(fr, fr, n2, ALU.mult)
                dve.drain()
                tt(fi, fi, n2, ALU.mult)
                dve.memset(bd, 0.0)
                ts(ta, s5_th[:, :], 16.0)
                dve.drain()
                reduce_angle(tb, ta, s5k, ts_)
                dve.drain()
                for ang, base, steps, n in (
                        (turn_ang_a, tb, iota_t[:, 0:17], 17),
                        (turn_ang_b, s5_th[:, :], iota_t[:, 0:16], 16)):
                    raw = turn_raw[:, :, 0:n]
                    ki = turn_k[:, :, 0:n]
                    tt(raw, over(base, 2, n), over(steps, 1, SI), ALU.mult)
                    dve.drain()
                    for c in range(2):
                        reduce_angle(ang[:, c, :, :], raw, ki, turn_kf[:, :, 0:n], quarter=1 - c)
                        dve.drain()
                dve.engine_nop().then_inc(flag("turn_args"), 1)
                dve.drain()
                dve.wait_ge(flag("in_bc"), 16)
                bre, bim = (bc_raw[:, s, :, :] for s in range(2))
                frb, fib = over(fr, 2, S5H), over(fi, 2, S5H)
                tt(bb[:, 0, :, :], bre, frb, ALU.mult)
                tt(bb[:, 1, :, :], bim, fib, ALU.mult)
                tt(bb[:, 2, :, :], bim, frb, ALU.mult)
                tt(bb[:, 3, :, :], bre, fib, ALU.mult)
                dve.drain()
                bd4 = bd.rearrange("p s (i g h) -> p s i g h", i=SI, g=2)
                for g in range(2):
                    r = slice(64 * g, 64 * g + 64)
                    tt(bd4[r, 0, :, g, :], bb[r, 0, :, :], bb[r, 1, :, :], ALU.subtract)
                    tt(bd4[r, 1, :, g, :], bb[r, 2, :, :], bb[r, 3, :, :], ALU.add)
                dve.drain().then_inc(flag("bd_ready"), 1)

            with dve.Fori(0, 3) as pair:
                expert_step(0, pair, pair + 1, pair * 2 + (first_sc + 3))
            expert_step(0, 3, 4, all_sc)
            expert_step(1, 0, 5, all_sc)
            dve.wait_ge(flag("in_ln0"), 48)
            variance(xmeta, 0, "me", META, TT)
            normalise(xmeta, xmeta, 0, ln0_g[0:META, :], ln0_b[0:META, :], "me", "meta_ready", META,
                      TT)
            second_input(0)
            with dve.Fori(1, 3) as pair:
                expert_step(1, pair, pair + 5, all_sc)
            s5_arguments()
            expert_step(1, 3, between=s5_inputs)
            dve.drain()
            for i, k in enumerate(BY_VECTOR):
                at = 32 + TOPK + k
                s = at % NR
                dve.wait_ge(row_full[s], (7 * USES + at // NR + 1) * 16)
                if i == 0:
                    last = ts(peer_out, rows[:, s, :], wgt[:, k:k + 1])
                else:
                    last = stt(peer_out, rows[:, s, :], wgt[:, k:k + 1], peer_out)
                if k < TOPK - NR:
                    last.then_inc(slot_free[s], 1)
                dve.drain()
            tt(peer_out, peer_out, gate2, ALU.mult)
            dve.drain()
            tt(xres[:, 1, :], xres[:, 1, :], peer_out, ALU.add)
            dve.drain()
            second_input(1)
            dve.memset(qk_in[:, :, 0:3], 0.0)
            dve.memset(cd, 0.0)
            dve.drain()
            cre, cim = (bc_raw[:, s, :, :] for s in (2, 3))
            cd4 = cd.rearrange("p s i (g h) -> p s i g h", g=2)
            for g in range(2):
                r = slice(64 * g, 64 * g + 64)
                dve.tensor_copy(cd4[r, 0, :, g, :], cre[r, :, :])
                ts(cd4[r, 1, :, g, :], cim[r, :, :], -1.0)
            dve.drain()


            def tables(q):
                if q == 0:
                    dve.wait_ge(flag("turn_tab"), 1)
                a, b = s5t[2], s5t[3]
                r = slice(4 * q, 4 * q + 4)

                def prod(o, ca, cb):
                    tt(o.rearrange("p i (a b) -> p i a b", b=16), over(turn_a[:, ca, r, :], 3, 16),
                       over(turn_b[cb][:, r, :], 2, 17), ALU.mult)

                prod(a, 0, 0)
                prod(b, 1, 1)
                dve.drain()
                tt(s5t[0], a, b, ALU.subtract)
                dve.drain()
                prod(a, 1, 0)
                prod(b, 0, 1)
                dve.drain()
                tt(s5t[1], a, b, ALU.add)
                dve.drain()

            def s5_quad(q):
                dve.wait_ge(flag("bu_read"), 8 * q + 8)
                cos, sin = s5t[0], s5t[1]
                a, b = s5t[2], s5t[3]

                def turn(re, im, sign):
                    o1, o2 = (ALU.add, ALU.subtract) if sign < 0 else (ALU.subtract, ALU.add)
                    tt(a, cos, re, ALU.mult)
                    tt(b, sin, im, ALU.mult)
                    dve.drain()
                    tt(s5t[4], a, b, o1)
                    dve.drain()
                    tt(a, cos, im, ALU.mult)
                    tt(b, sin, re, ALU.mult)
                    dve.drain()
                    last = tt(s5t[5], a, b, o2)
                    dve.drain()
                    return last

                turn(s5t[6], s5t[7], -1)
                for i in range(4):
                    r = s5_mag[:, 4 * q + i:4 * q + i + 1].broadcast_to([P, LEN])
                    for c in range(2):
                        dve.tensor_tensor_scan(s5t[6 + c][:, i, :], r, s5t[4 + c][:, i, :], 0.0,
                                               ALU.mult, ALU.add)
                dve.drain()
                turn(s5t[6], s5t[7], 1)
                dve.engine_nop().then_inc(flag("state_ready"), 1)

            def s5_y(q):
                dve.wait_ge(flag("y_full"), q + 1)
                stt(gyT[:, q, :], uT[:, q, META:LEN], pk("s5_d")[:, q:q + 1],
                    psum[:, 6, 0:SEQ]).then_inc(flag("y_read"), 1)

            tables(0)
            s5_quad(0)
            for m in range(4):
                read_wait(dve, "q21", m)
                read_wait(dve, "k21", m)
            w = pk("qk_w").rearrange("p (k m) -> p k m", k=4)
            for m in range(8):
                ts(qkT[:, m, :], qk_in[:, m, 0:LEN], w[:, 0, m:m + 1])
            for k in range(1, 4):
                dve.drain()
                for m in range(8):
                    stt(qkT[:, m, :], qk_in[:, m, k:k + LEN], w[:, k, m:m + 1], qkT[:, m, :])
            dve.drain().then_inc(flag("conv2_y"), 1)
            s5_y(0)
            for q in range(1, 3):
                tables(q)
                s5_quad(q)
                s5_y(q)
            tables(3)
            dve.wait_ge(flag("ln_done"), 1)
            li, f, l1p = (row_a[:, i, :] for i in range(3))
            ra, rM, rN = (row_b[:, i, :] for i in range(3))
            stt(f, f, 0.0, l1p, ALU.min, ALU.subtract)
            dve.drain()
            dve.tensor_tensor_scan(rN, ones[0:MH, 0:1].broadcast_to([MH, LEN]), f, 0.0, ALU.mult, ALU.add)
            dve.drain()
            tt(ra, li, rN, ALU.subtract)
            dve.drain()
            dve.tensor_tensor_scan(rM, ones[0:MH, 0:1].broadcast_to([MH, LEN]), ra, 0.0, ALU.mult, ALU.max)
            dve.drain()
            tt(rN, rN, rM, ALU.add).then_inc(flag("rows_ready"), 1)
            s5_quad(3)
            s5_y(3)

            dve.wait_ge(flag("mbc_full"), 1)
            dve.wait_ge(flag("enm"), 1)
            for b in range(3):
                nr, lo = (META, 0) if b == 0 else (P, (b - 1) * P)
                for h in range(MH):
                    src = psum[0:nr, 6 + h // 2, (h % 2) * SEQ + lo:(h % 2 + 1) * SEQ]
                    last = ts(PT[0:nr, b, h, lo:SEQ], src, -1.0, gcol[0:nr, MH * b + h:MH * b + h + 1],
                              ALU.mult, ALU.add)
            last.then_inc(flag("mbc_read"), 1)
            dve.drain()
            parts = [PT[0:META, 0, :, :], PT[:, 1, :, :], PT[:, 2, :, P:SEQ]]
            for p_ in parts:
                last = ts(p_, p_, 0.0, None, ALU.min)
            last.then_inc(flag("E_args"), 1)
            dve.wait_ge(flag("E_exp"), 1)
            for b in (1, 2):
                sl = PT[:, b, :, (b - 1) * P:b * P]
                tt(sl, sl, over(causal[:, :], 1, MH), ALU.mult)
            dve.drain()
            n = 0
            for b in range(3):
                nr, lo = (META, 0) if b == 0 else (P, (b - 1) * P)
                for hh in range(2):
                    dve.wait_ge(flag("st_full"), n + 1)
                    src = psum[0:nr, 6 + n % 2, :].rearrange("p (h n) -> p h n", h=2)[:, :, lo:SEQ]
                    dst = PT[0:nr, b, 2 * hh:2 * hh + 2, lo:SEQ]
                    stt(dst, src, DK ** -0.5, dst, ALU.mult, ALU.mult).then_inc(flag("st_read"), 1)
                    n += 1
            dve.drain().then_inc(flag("PT_ready"), 1)
            dve.wait_ge(flag("in_ln1"), 48)
            dve.wait_ge(flag("gate_sig"), 1)
            tt(otok, otok, over(m_norm, 1, TT), ALU.mult)
            turn_read_wait(dve, "den", 0, 0)
            stt(dens, dens, -1.0, dens, ALU.mult, ALU.max)
            dve.drain()
            tt(dens, dens, enm, ALU.max)
            dve.drain()
            dve.reciprocal(rden, dens)
            dve.drain()
            n = 0
            h4 = hm.rearrange("p t (h e) -> p t h e", h=MH)
            for t in range(TT):
                for hh in range(2):
                    dve.wait_ge(flag("num_full"), n + 1)
                    tt(h4[:, t, 2 * hh:2 * hh + 2, :],
                       psum[:, 6 + n % 2, :].rearrange("p (h e) -> p h e", h=2),
                       over(rden[:, MH * t + 2 * hh:MH * t + 2 * hh + 2], 2, DV),
                       ALU.mult).then_inc(flag("num_read"), 1)
                    dve.drain()
                    for h in (2 * hh, 2 * hh + 1):
                        dve.bn_stats(hbn[:, MH * t + h, :], h4[:, t, h, :])
                    n += 1
                dve.drain()
                for h in range(MH):
                    dve.bn_aggr(hmv[:, MH * t + h, :], hbn[:, MH * t + h:MH * t + h + 1, :])
                dve.drain().then_inc(flag("hv_var"), 1)
            for t in range(TT):
                dve.wait_ge(flag("hv_sd"), t + 1)
                dve.reciprocal(hrs[:, MH * t:MH * (t + 1)], hrs[:, MH * t:MH * (t + 1)])
                dve.drain()
                for h in range(MH):
                    i = MH * t + h
                    ts(h4[:, t, h, :], h4[:, t, h, :], hmv[:, i, 0:1], hrs[:, i:i + 1], ALU.subtract,
                       ALU.mult)
                dve.drain()
                tt(hm[:, t, :], hm[:, t, :], otok[:, t, :], ALU.mult).then_inc(flag("hm_ready"), 1)
            dve.wait_ge(flag("gate_sig"), 3)
            dve.wait_ge(flag("glu_read"), 1)
            for t in range(TT):
                tt(gs[:, t, :], gs[:, t, :], xres[:, t, :], ALU.mult)
            dve.drain()
            for t in range(TT):
                tt(gs[:, t, :], gs[:, t, :], tmp2[:, t, :], ALU.mult)
            for t in range(TT):
                for n in range(2):
                    i = TT * n + t
                    sl = slice(512 * n, 512 * (n + 1))
                    group_wait(dve, "mo", i)
                    read_out(tt(gm[:, t, sl], gm[:, t, sl], bank_of("mo", i), ALU.mult), "mo", i)
                    dve.drain()
                    tt(gs[:, t, sl], gs[:, t, sl], gm[:, t, sl], ALU.add)
                dve.drain().then_inc(flag("mix_ready"), 1)

            def residual(src, t, half):
                sl = slice(512 * half, 512 * (half + 1))
                last = stt(xres[:, t, sl], hbuf[:, t, sl], ALPHA, src)
                dve.drain()
                dve.bn_stats(bn[:, t, half, :], xres[:, t, sl])
                return last

            for t in range(TT):
                for n in range(2):
                    i = TT * n + t
                    group_wait(dve, "wo", i)
                    read_out(residual(bank_of("wo", i), t, n), "wo", i)
                variance(None, t, "l1")
                normalise(hbuf[:, t, :], xres[:, t, :], t, ln1_g, ln1_b, "l1", "hb_ready")
            for n in range(8):
                read_wait(dve, "up", 4 * n + 3)
                for m in range(3):
                    read_wait(dve, "up", 4 * n + m)
                sl = ffT[:, 4 * n:4 * n + 4, :]
                tt(sl, sl, sl, ALU.mult).then_inc(flag("ff_ready"), 1)
            dve.wait_ge(flag("in_ln2"), 32)
            for t in range(TT):
                dve.wait_ge(*((flag("down_first"), 1) if t == 0 else (flag("down_used"), 8)))
                for half in range(2):
                    residual(psum[:, 4 + 2 * t + half, :], t, half)
                variance(None, t, "l2")
                normalise(fin[:, t, :], xres[:, t, :], t, ln2_g, ln2_b, "l2", "fin_ready")


def kernel(**inputs):
    import concourse.bacc as _bacc
    from concourse.bass_utils import run_bass_kernel_spmd as _run

    A = {n: np.ascontiguousarray(a) for n, a in inputs.items()}

    def cols(v, n):
        return v.reshape(n, P).T

    def state(a):
        return np.moveaxis(a.reshape((SI, P) + a.shape[2:]), 0, 1)

    b_in, w_in2 = A["b_in_2"].reshape(-1), A["w_in_2"][0]
    given = {
        "c": cols(A["c"].reshape(-1), KD),
        "conv_w": np.moveaxis(A["conv_w"][0].reshape(3, CT, P), 2, 0).reshape(P, -1),
        "conv_g": cols(A["conv_out_g"].reshape(-1), CT),
        "b_uqk": cols(b_in[U0:V0], 12),
        "qk_w": np.moveaxis(A["qk_conv_w_2"][0].reshape(4, 8, P), 2, 0).reshape(P, -1),
        "qk_b": cols(A["qk_conv_b_2"].reshape(-1), 8),
        "lam_re": state(A["s5_lambda_re_2"][0]),
        "lam_im": state(A["s5_lambda_im_2"][0]),
        "s5_d": cols(A["s5_d_2"].reshape(-1), 4),
        "b_up": cols(A["b_up_2"].reshape(-1), FF // P),
    }
    c_re, c_im = (np.swapaxes(A[n][0], 1, 2) for n in ("s5_c_re_2", "s5_c_im_2"))
    host = {
        "pack": np.concatenate([given[n] for n, _ in PACK], axis=1),
        "positions": A["positions"].reshape(TT, P).T,
        "x": A["x"].reshape(SEQ, D),
        "subkeys": np.moveaxis(A["peer_subkeys"][0].reshape(HP, KEYS, P), 2, 0),
        "w_if": np.moveaxis(w_in2[:, IF0:IF0 + 2 * MH].reshape(KD, P, 2 * MH), 1, 0),
        "b_if": b_in[IF0:IF0 + 2 * MH].reshape(2, MH).T,
        "log_dt": np.repeat(A["s5_log_dt_2"].reshape(SI, 2).T, S5P, axis=0),
        "s5_bc": np.stack([state(A["s5_b_re_2"][0]), state(A["s5_b_im_2"][0]), state(c_re),
                           state(c_im)], axis=1),
        "meta_tokens_2": A["meta_tokens_2"],
    }
    for n in ("ada_w", "w_in", "w_out", "peer_wq", "peer_u", "peer_v", "w_in_2", "s5_w_glu_2",
              "m_w_out_2", "w_o_2", "w_up_2", "w_down_2"):
        host[n] = A[n][0]
    for n in ("ada_b", "norm1_g", "norm2_g", "q_norm_g", "k_norm_g", "sinks", "attn_out_g", "b_in_2",
              "m_norm_g_2", "ln0_g_2", "ln0_b_2", "ln1_g_2", "ln1_b_2", "ln2_g_2", "ln2_b_2"):
        host[n] = A[n].reshape(-1)

    nc = _bacc.Bacc("TRN2", target_bir_lowering=False, num_devices=1)
    arrays, T = {}, {}
    for n, a in host.items():
        a = np.ascontiguousarray(a)
        arrays[f"in_{n}_dram"] = a
        T[n] = nc.dram_tensor(f"in_{n}_dram", a.shape, mybir.dt.from_np(a.dtype),
                              kind="ExternalInput").ap()
    out = nc.dram_tensor("out_0_dram", (SEQ, D), F32, kind="ExternalOutput").ap()
    build(nc, T, out)
    r = _run(nc, [arrays], core_ids=[0])
    return r.results[0]["out_0_dram"].reshape(1, SEQ, D)
```
